# Optimizing a Trainium2 kernel written in Bass

```python
import jax, jax.numpy as jnp
from jax import lax
import numpy as np

D_MODEL = 1024
BATCH = 1
SEQ = 512
DEPTH = 4

N_MIXERS = 3
N_A = (DEPTH + 2) // 3
N_B = (DEPTH + 1) // 3
N_C = DEPTH // 3
D_RNN = 1280
A_HEADS = 16
A_HEAD_DIM = D_RNN // A_HEADS
A_CONV = 4
LRU_C = 8.0
D_SGU = D_MODEL
SGU_CHUNK = 128
SGU_GROUPS = 8
SGU_GROUP_DIM = D_SGU // SGU_GROUPS
D_CONV = D_MODEL
C_CONV = 3
D_FF = 4 * D_MODEL
EPS = 1e-6


def _rmsnorm(x, g):
    x32 = x.astype(jnp.float32)
    y = x32 * lax.rsqrt(jnp.mean(x32 * x32, axis=-1, keepdims=True) + EPS)
    return y.astype(x.dtype) * g

def _causal_dwconv(x, w):
    k = w.shape[0]
    return lax.conv_general_dilated(
        x, w[:, None, :].astype(x.dtype), window_strides=(1,),
        padding=[(k - 1, 0)], dimension_numbers=("NWC", "WIO", "NWC"),
        feature_group_count=x.shape[-1])

def _lru_combine(left, right):
    a_l, b_l = left
    a_r, b_r = right
    return a_l * a_r, a_r * b_l + b_r

def _rglru_mixer(h, w_in, conv_w, conv_b, gate_a_w, gate_a_b, gate_x_w, gate_x_b, lam, w_out):
    b, s, _ = h.shape
    gate, xr = jnp.split(h @ w_in, 2, axis=-1)
    gate = jax.nn.gelu(gate)
    xr = _causal_dwconv(xr, conv_w) + conv_b
    xh = xr.reshape(b, s, A_HEADS, A_HEAD_DIM)
    r = jax.nn.sigmoid(jnp.einsum("bshi,hij->bshj", xh, gate_a_w).reshape(b, s, D_RNN) + gate_a_b)
    ig = jax.nn.sigmoid(jnp.einsum("bshi,hij->bshj", xh, gate_x_w).reshape(b, s, D_RNN) + gate_x_b)
    log_a = -LRU_C * r.astype(jnp.float32) * jax.nn.softplus(-lam.astype(jnp.float32))
    a = jnp.exp(log_a)
    u = jnp.sqrt(-jnp.expm1(2.0 * log_a)) * (ig * xr).astype(jnp.float32)
    _, hs = lax.associative_scan(_lru_combine, (a, u), axis=1)
    return (hs.astype(h.dtype) * gate) @ w_out

def _sgu_mixer(h, w_in, norm_g, w_s, s_bias, w_out):
    b, s, _ = h.shape
    z = jax.nn.gelu(h @ w_in)
    u, v = jnp.split(z, 2, axis=-1)
    v = _rmsnorm(v, norm_g)
    n_chunks = s // SGU_CHUNK
    v = v.reshape(b, n_chunks, SGU_CHUNK, SGU_GROUPS, SGU_GROUP_DIM)
    causal = jnp.tril(jnp.ones((SGU_CHUNK, SGU_CHUNK), dtype=bool))
    w_causal = jnp.where(causal[None], w_s, jnp.zeros((), w_s.dtype))
    mixed = jnp.einsum("gts,bnsgc->bntgc", w_causal, v) + s_bias.T[None, None, :, :, None]
    y = u * mixed.reshape(b, s, D_SGU)
    return y @ w_out

def _shortconv_mixer(h, w_in, conv_w, w_out):
    gb, gc, xv = jnp.split(h @ w_in, 3, axis=-1)
    y = gb * _causal_dwconv(gc * xv, conv_w)
    return y @ w_out

def _sqrelu_mlp(h, w1, w2):
    return jnp.square(jax.nn.relu(h @ w1)) @ w2

def first_inputs(seed: int = 0) -> dict:
    key = jax.random.key(seed)
    ks = jax.random.split(key, 24)
    f32 = jnp.float32

    def w(k, shape, fan_in):
        return jax.random.normal(k, shape, f32) * (fan_in ** -0.5)

    def gain(k, shape):
        return 1.0 + 0.1 * jax.random.normal(k, shape, f32)

    def bias(k, shape, scale=0.1):
        return scale * jax.random.normal(k, shape, f32)

    a_c = jax.random.uniform(ks[11], (N_A, D_RNN), f32, minval=0.9, maxval=0.999)
    a0 = a_c ** (1.0 / LRU_C)
    a_lambda = jnp.log(a0) - jnp.log1p(-a0)

    return {
        "x": jax.random.normal(ks[0], (BATCH, SEQ, D_MODEL), f32),
        "norm_mix_g": gain(ks[1], (DEPTH, D_MODEL)),
        "norm_mlp_g": gain(ks[2], (DEPTH, D_MODEL)),
        "final_norm_g": gain(ks[3], (D_MODEL,)),
        "a_w_in": w(ks[4], (N_A, D_MODEL, 2 * D_RNN), D_MODEL),
        "a_conv_w": w(ks[5], (N_A, A_CONV, D_RNN), A_CONV),
        "a_conv_b": bias(ks[6], (N_A, D_RNN)),
        "a_gate_a_w": w(ks[7], (N_A, A_HEADS, A_HEAD_DIM, A_HEAD_DIM), A_HEAD_DIM),
        "a_gate_a_b": bias(ks[8], (N_A, D_RNN)),
        "a_gate_x_w": w(ks[9], (N_A, A_HEADS, A_HEAD_DIM, A_HEAD_DIM), A_HEAD_DIM),
        "a_gate_x_b": bias(ks[10], (N_A, D_RNN)),
        "a_lambda": a_lambda,
        "a_w_out": w(ks[12], (N_A, D_RNN, D_MODEL), D_RNN),
        "b_w_in": w(ks[13], (N_B, D_MODEL, 2 * D_SGU), D_MODEL),
        "b_norm_g": gain(ks[14], (N_B, D_SGU)),
        "b_w_s": w(ks[15], (N_B, SGU_GROUPS, SGU_CHUNK, SGU_CHUNK), SGU_CHUNK),
        "b_s_bias": gain(ks[16], (N_B, SGU_GROUPS, SGU_CHUNK)),
        "b_w_out": w(ks[17], (N_B, D_SGU, D_MODEL), D_SGU),
        "c_w_in": w(ks[18], (N_C, D_MODEL, 3 * D_CONV), D_MODEL),
        "c_conv_w": w(ks[19], (N_C, C_CONV, D_CONV), C_CONV),
        "c_w_out": w(ks[20], (N_C, D_CONV, D_MODEL), D_CONV),
        "mlp_w1": w(ks[21], (DEPTH, D_MODEL, D_FF), D_MODEL),
        "mlp_w2": w(ks[22], (DEPTH, D_FF, D_MODEL), D_FF),
    }

def first_block(x, norm_mix_g, norm_mlp_g, final_norm_g,
              a_w_in, a_conv_w, a_conv_b, a_gate_a_w, a_gate_a_b, a_gate_x_w, a_gate_x_b, a_lambda, a_w_out,
              b_w_in, b_norm_g, b_w_s, b_s_bias, b_w_out,
              c_w_in, c_conv_w, c_w_out,
              mlp_w1, mlp_w2):
    for i in range(DEPTH):
        kind, j = i % N_MIXERS, i // N_MIXERS
        h = _rmsnorm(x, norm_mix_g[i])
        if kind == 0:
            mix = _rglru_mixer(h, a_w_in[j], a_conv_w[j], a_conv_b[j], a_gate_a_w[j], a_gate_a_b[j],
                               a_gate_x_w[j], a_gate_x_b[j], a_lambda[j], a_w_out[j])
        elif kind == 1:
            mix = _sgu_mixer(h, b_w_in[j], b_norm_g[j], b_w_s[j], b_s_bias[j], b_w_out[j])
        else:
            mix = _shortconv_mixer(h, c_w_in[j], c_conv_w[j], c_w_out[j])
        x = x + mix
        x = x + _sqrelu_mlp(_rmsnorm(x, norm_mlp_g[i]), mlp_w1[i], mlp_w2[i])
    return _rmsnorm(x, final_norm_g)


DEPTH_2 = 1

HEAD_DIM = 64
RWKV_HEADS = 16
RWKV_DIM = RWKV_HEADS * HEAD_DIM
DECAY_LORA = 64
AAA_LORA = 64
GATE_LORA = 160
GN_EPS = HEAD_DIM * 1e-5
RWKV_IN = 3 * RWKV_DIM + DECAY_LORA + AAA_LORA + GATE_LORA
DIL_GROUPS = ((128, 1), (512, 4), (2048, 16))
HEADS_PER_GROUP = 4
ATTN_HEADS = 3 * HEADS_PER_GROUP
ATTN_DIM = ATTN_HEADS * HEAD_DIM
ATTN_OUT_DIM = HEADS_PER_GROUP * HEAD_DIM
IN_SPLITS = (RWKV_DIM, RWKV_DIM, RWKV_DIM, DECAY_LORA, AAA_LORA, GATE_LORA,
             ATTN_DIM, ATTN_DIM, ATTN_DIM, D_MODEL, D_MODEL)
N_IN = RWKV_IN + 3 * ATTN_DIM + 2 * D_MODEL
MEM_LEN = 256
XATTN_HEADS = 4
XATTN_HEAD_DIM = D_MODEL // XATTN_HEADS
FFN_DIM = 4 * D_MODEL
NORM_EPS = 1e-6


def rmsnorm(x, g):
    xf = x.astype(jnp.float32)
    y = xf * lax.rsqrt(jnp.mean(xf * xf, axis=-1, keepdims=True) + NORM_EPS) * g.astype(jnp.float32)
    return y.astype(x.dtype)

def alibi_slopes(n_heads):
    return jnp.exp2(-8.0 * (jnp.arange(n_heads, dtype=jnp.float32) + 1.0) / n_heads)

def rwkv7_scan(r, w, k, v, a_, b_):
    B, S, H, N = r.shape

    def step(state, inp):
        r_t, w_t, k_t, v_t, a_t, b_t = inp
        sa = jnp.einsum('bhij,bhj->bhi', state, a_t)
        state = state * w_t[:, :, None, :] + sa[..., None] * b_t[:, :, None, :] + v_t[..., None] * k_t[:, :, None, :]
        return state, jnp.einsum('bhij,bhj->bhi', state, r_t)

    xs = tuple(jnp.moveaxis(t, 1, 0) for t in (r, w, k, v, a_, b_))
    _, ys = lax.scan(step, jnp.zeros((B, H, N, N), jnp.float32), xs)
    return jnp.moveaxis(ys, 0, 1)

def rwkv7_mix(p_r, p_k, p_v, p_wd, p_ad, p_gd, w0, w2, a0, a2, g2, k_k, k_a, r_k, gn_w, gn_b):
    B, S, _ = p_r.shape
    heads = lambda t: t.reshape(B, S, RWKV_HEADS, HEAD_DIM)
    w_log = -jax.nn.softplus(-(w0 + jnp.tanh(p_wd) @ w2)) - 0.5
    decay = jnp.exp(-jnp.exp(w_log))
    a = jax.nn.sigmoid(a0 + p_ad @ a2)
    g = jax.nn.sigmoid(p_gd) @ g2
    kk = heads(p_k * k_k)
    kk = kk / jnp.maximum(jnp.sqrt(jnp.sum(kk * kk, axis=-1, keepdims=True)), 1e-12)
    k = p_k * (1.0 + (a - 1.0) * k_a)
    r, k, v, decay, a = heads(p_r), heads(k), heads(p_v), heads(decay), heads(a)
    y = rwkv7_scan(r, decay, k, v, -kk, kk * a)
    mean = jnp.mean(y, axis=-1, keepdims=True)
    var = jnp.mean(jnp.square(y - mean), axis=-1, keepdims=True)
    yn = ((y - mean) * lax.rsqrt(var + GN_EPS)).reshape(B, S, RWKV_DIM) * gn_w + gn_b
    bonus = (jnp.sum(r * k * r_k, axis=-1, keepdims=True) * v).reshape(B, S, RWKV_DIM)
    return (yn + bonus) * g

def dilated_attention(q, k, v, window, dilation, slopes):
    B, S, H, Dh = q.shape
    blk = window // dilation
    span = blk * dilation
    Sp = -(-S // span) * span
    nb = Sp // span
    padw = ((0, 0), (0, Sp - S), (0, 0), (0, 0))

    def blocks(t):
        return jnp.pad(t, padw).astype(jnp.float32).reshape(B, nb, blk, dilation, H, Dh)

    def with_prev(t):
        prev = jnp.pad(t, ((0, 0), (1, 0), (0, 0), (0, 0), (0, 0), (0, 0)))[:, :-1]
        return jnp.concatenate([prev, t], axis=2)

    qb = blocks(q) * (Dh ** -0.5)
    kc, vc = with_prev(blocks(k)), with_prev(blocks(v))
    s = jnp.einsum('bnqrhc,bnkrhc->bnrhqk', qb, kc)
    qi = jnp.arange(blk)[:, None]
    ki = jnp.arange(2 * blk)[None, :]
    steps = qi + blk - ki
    in_band = (steps >= 0) & (steps <= blk)
    exists = (jnp.arange(nb)[:, None, None] > 0) | (ki >= blk)[None]
    valid = in_band[None] & exists
    bias = -slopes[:, None, None] * (steps * dilation).astype(jnp.float32)[None]
    s = jnp.where(valid[None, :, None, None], s + bias[None, None, None], -jnp.inf)
    lse = jax.nn.logsumexp(s, axis=-1)
    p = jnp.exp(s - lse[..., None])
    o = jnp.einsum('bnrhqk,bnkrhc->bnqrhc', p, vc).reshape(B, Sp, H, Dh)[:, :S]
    lse = jnp.transpose(lse, (0, 1, 4, 2, 3)).reshape(B, Sp, H)[:, :S]
    return o, lse

def dilated_mixture(q, k, v):
    B, S = q.shape[:2]
    slopes = alibi_slopes(ATTN_HEADS)
    outs, lses = [], []
    for gi, (window, dilation) in enumerate(DIL_GROUPS):
        hs = slice(gi * HEADS_PER_GROUP, (gi + 1) * HEADS_PER_GROUP)
        o, l = dilated_attention(q[:, :, hs], k[:, :, hs], v[:, :, hs], window, dilation, slopes[hs])
        outs.append(o)
        lses.append(l)
    wts = jax.nn.softmax(jnp.stack(lses, axis=0), axis=0)
    y = jnp.sum(wts[..., None] * jnp.stack(outs, axis=0), axis=0)
    return y.reshape(B, S, ATTN_OUT_DIM)

def memory_cross_attention(xn, memn, wq, w_kv, wo):
    B, S, _ = xn.shape
    q = (xn @ wq).astype(jnp.float32).reshape(B, S, XATTN_HEADS, XATTN_HEAD_DIM)
    kv = (memn @ w_kv).astype(jnp.float32).reshape(B, MEM_LEN, 2, XATTN_HEADS, XATTN_HEAD_DIM)
    s = jnp.einsum('bshc,bmhc->bhsm', q, kv[:, :, 0]) * (XATTN_HEAD_DIM ** -0.5)
    p = jax.nn.softmax(s, axis=-1)
    o = jnp.einsum('bhsm,bmhc->bshc', p, kv[:, :, 1]).reshape(B, S, D_MODEL)
    return (o @ wo.astype(jnp.float32)).astype(xn.dtype)

def second_inputs(seed: int = 0) -> dict:
    key = jax.random.key(seed)
    ks = jax.random.split(key, 32)
    f32 = jnp.float32
    nrm = lambda k, shape, scale: jax.random.normal(k, shape, f32) * scale
    L = DEPTH_2
    return {
        'x': jax.random.normal(ks[0], (BATCH, SEQ, D_MODEL), f32),
        'mem': jax.random.normal(ks[1], (BATCH, MEM_LEN, D_MODEL), f32),
        'norm_mix_g': 1.0 + nrm(ks[2], (L, D_MODEL), 0.02),
        'w_in': nrm(ks[3], (L, D_MODEL, N_IN), D_MODEL ** -0.5),
        'shift_mu': jax.random.uniform(ks[4], (L, RWKV_IN), f32),
        'w0': jax.random.uniform(ks[5], (L, RWKV_DIM), f32, -5.0, 1.0),
        'w2': nrm(ks[6], (L, DECAY_LORA, RWKV_DIM), 0.1),
        'a0': nrm(ks[7], (L, RWKV_DIM), 0.1),
        'a2': nrm(ks[8], (L, AAA_LORA, RWKV_DIM), 0.1),
        'g2': nrm(ks[9], (L, GATE_LORA, RWKV_DIM), GATE_LORA ** -0.5),
        'k_k': 0.85 + nrm(ks[10], (L, RWKV_DIM), 0.05),
        'k_a': 1.0 + nrm(ks[11], (L, RWKV_DIM), 0.05),
        'r_k': nrm(ks[12], (L, RWKV_HEADS, HEAD_DIM), 0.1),
        'gn_w': 1.0 + nrm(ks[13], (L, RWKV_DIM), 0.02),
        'gn_b': nrm(ks[14], (L, RWKV_DIM), 0.02),
        'p_rwkv': nrm(ks[15], (L, RWKV_DIM, D_MODEL), RWKV_DIM ** -0.5),
        'p_attn': nrm(ks[16], (L, ATTN_OUT_DIM, D_MODEL), ATTN_OUT_DIM ** -0.5),
        'w_out': nrm(ks[17], (L, D_MODEL, D_MODEL), D_MODEL ** -0.5),
        'norm_x_g': 1.0 + nrm(ks[18], (L, D_MODEL), 0.02),
        'norm_mem_g': 1.0 + nrm(ks[19], (L, D_MODEL), 0.02),
        'xa_wq': nrm(ks[20], (L, D_MODEL, D_MODEL), D_MODEL ** -0.5),
        'xa_wkv': nrm(ks[21], (L, D_MODEL, 2 * D_MODEL), D_MODEL ** -0.5),
        'xa_wo': nrm(ks[22], (L, D_MODEL, D_MODEL), D_MODEL ** -0.5),
        'norm_ffn_g': 1.0 + nrm(ks[23], (L, D_MODEL), 0.02),
        'ffn_w1': nrm(ks[24], (L, D_MODEL, FFN_DIM), D_MODEL ** -0.5),
        'ffn_w2': nrm(ks[25], (L, FFN_DIM, D_MODEL), FFN_DIM ** -0.5),
        'norm_final_g': 1.0 + nrm(ks[26], (D_MODEL,), 0.02),
    }

def second_block(x, mem, norm_mix_g, w_in, shift_mu, w0, w2, a0, a2, g2, k_k, k_a, r_k, gn_w, gn_b,
              p_rwkv, p_attn, w_out, norm_x_g, norm_mem_g, xa_wq, xa_wkv, xa_wo,
              norm_ffn_g, ffn_w1, ffn_w2, norm_final_g):
    f32 = jnp.float32
    B, S, _ = x.shape
    bounds = list(np.cumsum(IN_SPLITS)[:-1])
    h = x
    for l in range(DEPTH_2):
        n = rmsnorm(h, norm_mix_g[l])
        proj = (n @ w_in[l]).astype(f32)
        rw = proj[..., :RWKV_IN]
        rw_prev = jnp.pad(rw, ((0, 0), (1, 0), (0, 0)))[:, :-1]
        proj = jnp.concatenate([rw + shift_mu[l].astype(f32) * (rw_prev - rw), proj[..., RWKV_IN:]], axis=-1)
        (p_r, p_k, p_v, p_wd, p_ad, p_gd, q, k, v, gate_r, gate_a) = jnp.split(proj, bounds, axis=-1)
        y_rwkv = rwkv7_mix(p_r, p_k, p_v, p_wd, p_ad, p_gd,
                           w0[l].astype(f32), w2[l].astype(f32), a0[l].astype(f32), a2[l].astype(f32),
                           g2[l].astype(f32), k_k[l].astype(f32), k_a[l].astype(f32), r_k[l].astype(f32),
                           gn_w[l].astype(f32), gn_b[l].astype(f32))
        hd = lambda t: t.reshape(B, S, ATTN_HEADS, HEAD_DIM)
        y_attn = dilated_mixture(hd(q), hd(k), hd(v))
        merged = (jax.nn.sigmoid(gate_r) * (y_rwkv @ p_rwkv[l].astype(f32))
                  + jax.nn.sigmoid(gate_a) * (y_attn @ p_attn[l].astype(f32)))
        h = h + (merged @ w_out[l].astype(f32)).astype(h.dtype)
        h = h + memory_cross_attention(rmsnorm(h, norm_x_g[l]), rmsnorm(mem, norm_mem_g[l]),
                                       xa_wq[l], xa_wkv[l], xa_wo[l])
        u = rmsnorm(h, norm_ffn_g[l]) @ ffn_w1[l]
        h = h + (jnp.square(jax.nn.relu(u)) @ ffn_w2[l]).astype(h.dtype)
    return rmsnorm(h, norm_final_g)


def setup_inputs(seed=0):
    out = dict(first_inputs(seed))
    for name, value in second_inputs(seed + 1).items():
        if name != "x":
            out[name + "_2"] = value
    return out


def reference(
    x, norm_mix_g, norm_mlp_g, final_norm_g, a_w_in, a_conv_w, a_conv_b, a_gate_a_w, a_gate_a_b,
    a_gate_x_w, a_gate_x_b, a_lambda, a_w_out, b_w_in, b_norm_g, b_w_s, b_s_bias, b_w_out,
    c_w_in, c_conv_w, c_w_out, mlp_w1, mlp_w2, mem_2, norm_mix_g_2, w_in_2, shift_mu_2, w0_2,
    w2_2, a0_2, a2_2, g2_2, k_k_2, k_a_2, r_k_2, gn_w_2, gn_b_2, p_rwkv_2, p_attn_2, w_out_2,
    norm_x_g_2, norm_mem_g_2, xa_wq_2, xa_wkv_2, xa_wo_2, norm_ffn_g_2, ffn_w1_2, ffn_w2_2,
    norm_final_g_2,
):
    x = first_block(
        x, norm_mix_g, norm_mlp_g, final_norm_g, a_w_in, a_conv_w, a_conv_b, a_gate_a_w,
        a_gate_a_b, a_gate_x_w, a_gate_x_b, a_lambda, a_w_out, b_w_in, b_norm_g, b_w_s,
        b_s_bias, b_w_out, c_w_in, c_conv_w, c_w_out, mlp_w1, mlp_w2,
    )
    return second_block(
        x, mem_2, norm_mix_g_2, w_in_2, shift_mu_2, w0_2, w2_2, a0_2, a2_2, g2_2, k_k_2, k_a_2,
        r_k_2, gn_w_2, gn_b_2, p_rwkv_2, p_attn_2, w_out_2, norm_x_g_2, norm_mem_g_2, xa_wq_2,
        xa_wkv_2, xa_wo_2, norm_ffn_g_2, ffn_w1_2, ffn_w2_2, norm_final_g_2,
    )


_drawn_inputs = setup_inputs


def setup_inputs(seed=0):
    import zlib

    import numpy as np

    out = dict(_drawn_inputs(seed))
    spreads = {}
    factors = {'a_gate_a_b': 3.317,
     'norm_mix_g_2': 4.253,
     'a0_2': 4.094,
     'gn_w_2': 8.0,
     'gn_b_2': 8.0,
     'norm_x_g_2': 8.0,
     'norm_mem_g_2': 8.0,
     'norm_ffn_g_2': 11.236,
     'norm_final_g_2': 7.452}
    for name, (base, spread) in spreads.items():
        noise = np.random.default_rng([zlib.crc32(name.encode()), seed]).standard_normal(out[name].shape)
        drawn = base * np.exp(spread * noise) if base else spread * noise
        out[name] = __import__('jax').numpy.asarray(drawn.astype(out[name].dtype))
    for name, factor in factors.items():
        out[name] = (out[name] * factor).astype(out[name].dtype)
    return out
```

```python
import math
from contextlib import ExitStack

import concourse.bass as bass
from concourse import mybir

ALU = mybir.AluOpType
ACT = mybir.ActivationFunctionType
AX = mybir.AxisListType
F32 = mybir.dt.float32
F32R = mybir.dt.float32r

P = 128
T = 512
D = 1024
ND = D // P
FF = 4 * D
DRNN = 1280
NR = DRNN // P
HDA = 80
EPS = 1e-6
LOG_DECAY = math.exp(-0.5)
GN_EPS = 64 * 1e-5
CH = 64
NC = T // CH
NH2 = 8
MEM = 256
NEG = 1e30
KIB = 1024


class Stage:

    def __init__(self, name, w, groups, upg, kb, col, row0=0, rhs="x", kind="plain", period=None, swap=False,
                 n=T, only1=False, hook=False):
        self.name, self.w, self.groups, self.upg, self.kb, self.col, self.row0 = name, w, groups, upg, kb, col, row0
        self.rhs, self.kind, self.period, self.swap, self.n, self.only1, self.hook = rhs, kind, period, swap, n, only1, hook


class At:

    def __init__(self, st, i, c, half):
        self.j, self.st, self.c, self.i, self.half_i = i + c, st, c, i, half

    def unit(self, s):
        return self.i * self.st.upg + (self.st.u0 + self.c * self.st.upg + s)

    def slot(self, s):
        return (self.st.u0 + self.c * self.st.upg + s) % 2

    def turn(self, s):
        return self.half_i * self.st.upg + (self.st.u0 + self.c * self.st.upg + s) // 2

    def group(self):
        return self.i + (self.st.g0 + self.c)

    def pair(self):
        return (self.st.g0 + self.c) % 2


def run_groups(eng, st, body):
    c = 0
    if st.hook:
        body(At(st, 0, 0, 0), True)
        c = 1
    per = st.period or 2
    n = (st.groups - c) // per if st.loop else 0
    if n >= 2:
        with eng.Fori(0, n) as i:
            for s in range(per):
                body(At(st, i * per, c + s, i * (per // 2)), False)
        c += n * per
    while c < st.groups:
        body(At(st, 0, c, 0), False)
        c += 1


def build(nc, a, out):
    ctx = ExitStack()
    base = nc.sbuf_base
    PERS = (base + 63) // 32 * 32
    used = [PERS]

    def pers(name, shape, dt=F32):
        n = 4
        for s in shape[1:]:
            n *= s
        off = used[0]
        used[0] += (n + 31) // 32 * 32
        return nc.alloc_sbuf_tensor_at(name, shape, dt, offset=off)

    def sem(name):
        return ctx.enter_context(nc.semaphore(name))

    raw = pers("raw", [P, 2, 8, 256])
    wh = pers("wh", [P, 2, 8, 256], F32R)
    wl = pers("wl", [P, 2, 8, 256], F32R)
    x = pers("x", [P, ND, T])
    XH_AT = used[0]
    xh = pers("xh", [P, ND, T], F32R)
    xl = pers("xl", [P, ND, T], F32R)
    ident = pers("ident", [P, P])
    ones = pers("ones", [P, P])
    headones = pers("headones", [P, P])
    rs = pers("rs", [P, T])
    acc = pers("acc", [P, T])
    tmp = pers("tmp", [P, 2, T + 8])
    hf = pers("hf", [P, 2, T])
    sq = hf
    sd = hf
    prm = [pers(f"prm{i}", [P, P]) for i in range(4)]
    small = pers("small", [P, 64])
    c8 = pers("c8", [P, 2, 2 * NR])
    ARENA = used[0]
    LIMIT = nc.sbuf_top

    def at(name, kib, shape, dt=F32, base_at=None):
        n = 4
        for s in shape[1:]:
            n *= s
        off = (ARENA if base_at is None else base_at) + int(kib * KIB)
        assert base_at is not None or off + n <= LIMIT, (name, off + n, LIMIT)
        return nc.alloc_sbuf_tensor_at(name, shape, dt, offset=off)

    hh = at("hh", 0, [P, 16, T], F32R)
    hl = at("hl", 32, [P, 16, T], F32R)
    yh = at("yh", 40, [P, NR, T], F32R)
    yl = at("yl", 60, [P, NR, T], F32R)
    xtok = at("xtok", 0, [P, 4, D])
    rows = at("rows", 16, [P, 4, P])
    ga = at("ga", 0, [P, NR, T])
    xc = at("xc", 20, [P, NR, T])
    ra = at("ra", 40, [P, NR, T])
    ig = at("ig", 60, [P, NR, T])
    gw = at("gw", 80, [P, 2, 13, P])
    th = at("th", 0, [P, NR, T], base_at=XH_AT)
    xpad = at("xpad", 60, [P, 2, T + 8])
    vv = at("vv", 0, [P, ND, T])
    uu = at("uu", 16, [P, ND, T])
    wsT = at("wsT", 32, [P, 8, P])
    wsr = at("wsr", 36, [P, 8, P])
    vtok = at("vtok", 80, [P, 2, 4, P])
    sbrow = at("sbrow", 84, [1, 8 * P])
    gcs = at("gcs", 0, [P, 2, T])
    pc = at("pc", 4, [P, 2, T + 8])
    cv = at("cv", 9, [P, 2, T])

    qT = at("qT", 0, [P, 6, T])
    kT = at("kT", 12, [P, 6, T])
    vt = at("vt", 24, [P, 4, 768])
    dist = at("dist", 36, [P, 3, T])
    sc = at("sc", 42, [P, 2, 1280])
    pt = at("pt", 52, [P, 10, P])
    I32 = mybir.dt.int32
    disti = at("disti", 60, [P, T], I32)
    distm = at("distm", 62, [P, T], I32)
    distf = at("distf", 64, [P, T])
    d0 = at("d0", 66, [P, T])
    den = at("den", 59.5, [P, 4])
    rscol = at("rscol", 59, [P, 8])
    stat = at("stat", 59.25, [P, 4])
    ya = at("ya", 80, [P, 2, T])
    gsp = at("gsp", 47, [P, 2, T])
    AR = at("AR", 0, [P, NC, NH2, 2, CH])
    BT = at("BT", 32, [P, NC, NH2, CH])
    KT = at("KT", 48, [P, NC, NH2, CH])
    VT = at("VT", 64, [P, NH2, T])
    gd = at("gd", 84, [P, 2, T])
    w2a2 = at("w2a2", 88, [P, D])
    wda = at("wda", 92, [P, T])
    PCt = at("PC", 94, [P, NC, NH2])
    XT_AT = XH_AT - 16 * KIB
    rt = at("rt", 0, [P, 8, T], base_at=XT_AT)
    names = ["Vt", "Bt", "Kt", "TM", "X", "Z", "Yt", "W0", "U", "ST"]
    ck = {n_: at("c" + n_, 2 * i_, [P, NH2, CH], base_at=XH_AT) for i_, n_ in enumerate(names)}
    TLB = at("TLB", 20, [P, NH2, 2, CH], base_at=XH_AT)
    TLK = at("TLK", 24, [P, NH2, 2, CH], base_at=XH_AT)
    mk = at("mk", 28, [P, 8, CH], base_at=XH_AT)
    i64 = at("i64", 30.25, [P, CH], base_at=XH_AT)
    srci = at("srci", 30.5, [P, CH], mybir.dt.int32, base_at=XH_AT)
    tgti = at("tgti", 30.75, [P, CH], mybir.dt.int32, base_at=XH_AT)
    inta = at("inta", 31, [P, CH], mybir.dt.int32, base_at=XH_AT)
    intb = at("intb", 31.25, [P, CH], mybir.dt.int32, base_at=XH_AT)
    srcf = at("srcf", 31.5, [P, CH], base_at=XH_AT)
    tgtf = at("tgtf", 31.75, [P, CH], base_at=XH_AT)
    gl = at("gl", 0, [P, 16, T], base_at=XH_AT)
    mg = at("mg", 0, [P, ND, T])
    g2s = at("g2s", 0, [P, 2, D])
    gns = at("gns", 8, [P, 3, T])
    bon = at("bon", 14, [P, 2, T])
    qx = at("qx", 0, [P, ND, T])
    kx = at("kx", 16, [P, ND, MEM])
    vx = at("vx", 24, [P, 2, D])
    mh = at("mh", 32, [P, ND, MEM], F32R)
    ml = at("ml", 76, [P, ND, MEM], F32R)
    mtok = at("mtok", 40, [P, 2, D])
    msq = at("msq", 56, [P, 8])
    sx = at("sx", 84, [P, 4, MEM])
    ptx = at("ptx", 88, [P, 2, T])
    stx = at("stx", 92, [P, 16])
    mjunk = at("mjunk", 84, [P, D])
    fo = at("fo", 16, [P, ND, T])

    ps = [ctx.enter_context(nc.psum_tensor(f"ps{i}", [P, T], F32)) for i in range(8)]

    x_spill = nc.dram_tensor("x_spill", [P, ND, T], F32).ap()
    gate_spill = nc.dram_tensor("gate_spill", [16, P, T], F32).ap()
    bonus_spill = nc.dram_tensor("bonus_spill", [ND, P, T], F32).ap()

    landed = [sem("weights_landed_0"), sem("weights_landed_1")]
    upper = sem("weights_upper")
    lower = sem("weights_lower")
    units = sem("units_multiplied")
    evac = sem("tiles_evacuated")
    acted = sem("tiles_acted")
    pooled = sem("pool_done")
    squared = sem("squares_ready")
    split = sem("operands_split")
    ssum = sem("square_sums")
    rooted = sem("roots_ready")
    chain = sem("vector_chain")
    S = {}

    def s(name):
        if name not in S:
            S[name] = sem(name)
        return S[name]

    stages = {}
    order = []
    count = dict(u=0, g=0, a=0, q=0, t=0, n=0)

    def stage(name, *args, **kw):
        st = Stage(name, *args, **kw)
        st.u0, st.g0, st.a0, st.q0, st.t0, st.n0 = (count[k] for k in "ugaqtn")
        st.norm = (count["q"], count["n"] - 1)
        back = {"x": ND, "h": 16, "y": 5 * st.upg if st.upg == 2 else ND + 2 * (name == "merge"), "m": None}[st.rhs]
        st.need0 = count["t"] - back if (st.hook or st.rhs in "hy") and back else None
        st.s0 = 8 * count["n"]
        st.nosplit = name in ("l3_mlp_down1", "ffn_down1")
        st.loop = st.kind in ("relu", "resid", "fin", "gelu", "sigm", "scale", "gelusq")
        tiles = 2 * st.groups
        if st.nosplit:
            st.kind = "last"
        count["u"] += st.groups * st.upg
        count["g"] += st.groups
        count["a"] += {"relu": tiles, "fin": tiles, "gelu": tiles, "gelusq": tiles, "sigm": tiles, "spill": tiles, "y": tiles}.get(st.kind, 0) + kw.get("extra_a", 0)
        count["q"] += {"relu": tiles, "fin": tiles + 1, "last": tiles + 1, "gelusq": tiles + 1}.get(st.kind, 0)
        count["t"] += {"relu": tiles, "fin": tiles}.get(st.kind, 0)
        count["n"] += {"fin": 1, "last": 1, "gelusq": 1}.get(st.kind, 0)
        if st.nosplit:
            st.kind = "fin"
        stages[name] = st
        order.append(st)
        return st

    def tiles_split(name, n):
        stages[name] = (count["t"], count["a"])
        count["t"] += n
        count["a"] += n

    lin = lambda c0: (lambda j: j * 256 + c0)

    def norm_from_pool(name):
        stages[name] = (count["q"], count["n"], count["a"], count["t"])
        count["q"] += ND + 1
        count["n"] += 1
        count["a"] += ND
        count["t"] += ND

    norm_from_pool("init")
    G_MIX, G_MLP, G_FIN, G_B, G_MIX2, G_X, G_MEM, G_FFN, G_FIN2 = 0, 32, 64, 72, 80, 88, 96, 104, 112
    gain = lambda c: (0, c)

    def mlp(name, w1, w2, g):
        for h in range(2):
            stage(f"{name}_up{h}", w1, 8, 1, 8, lin(h * 2048), kind="relu", hook=h == 0)
            stage(f"{name}_down{h}", w2, 4, 2, 8, lin(0), row0=h * 16, rhs="h", kind="fin" if h else "resid")
            stages[f"{name}_down{h}"].gain = g

    for l in range(4):
        kind, j = l % 3, l // 3
        if kind == 0:
            w = a["a_w_in"][j]
            stage(f"l{l}_branch", w, 5, 1, 8, lin(DRNN), kind="conv4", hook=True)
            stage(f"l{l}_gate", w, 5, 1, 8, lin(0), kind="gelu")
            tiles_split(f"l{l}_mix", NR)
            stage(f"l{l}_out", a["a_w_out"][j], 4, 2, 5, lin(0), rhs="y", kind="fin")
        elif kind == 1:
            stage(f"l{l}_v", a["b_w_in"][0], 4, 1, 8, lin(D), kind="gelusq", hook=True)
            stage(f"l{l}_u", a["b_w_in"][0], 4, 1, 8, lin(0), kind="gelu")
            tiles_split(f"l{l}_mix", ND)
            stage(f"l{l}_out", a["b_w_out"][0], 4, 1, 8, lin(0), rhs="y", kind="fin")
        else:
            stage(f"l{l}_in", a["c_w_in"][0], 12, 1, 8, lambda j: [1, 2, 0][j % 3] * D + j // 3 * 256, kind="conv3", hook=True)
            tiles_split(f"l{l}_mix", ND)
            stage(f"l{l}_out", a["c_w_out"][0], 4, 1, 8, lin(0), rhs="y", kind="fin")
        stages[f"l{l}_out"].gain = G_MLP + 8 * l
        mlp(f"l{l}_mlp", a["mlp_w1"][l], a["mlp_w2"][l], G_MIX + 8 * (l + 1) if l < 3 else None)
        if l == 3:
            stages["l3_mlp_down1"].gain = G_FIN
    norm_from_pool("mid")
    w2nd = a["w_in_2"][0]
    Q0 = 3 * D + 288
    stage("q", w2nd, 3, 1, 8, lin(Q0), kind="scale", hook=True)
    stage("k", w2nd, 3, 1, 8, lin(Q0 + 768), kind="scale")
    stage("v", w2nd, 3, 1, 8, lin(Q0 + 1536), kind="tok", swap=True)
    stage("gates", w2nd, 8, 1, 8, lin(Q0 + 2304), kind="spill")
    stage("lora", w2nd, 2, 1, 8, lambda j: [3 * D, 3 * D + 32][j], kind="lora")
    stage("rkv", w2nd, 12, 1, 8, lambda j: j % 3 * D + j // 3 * 256, kind="rkv")
    tiles_split("ysplit", ND + 2)
    stage("merge", None, 8, 1, None, lin(0), rhs="y", kind="merge")
    tiles_split("msplit", ND)
    stage("out2", a["w_out_2"][0], 4, 1, 8, lin(0), rhs="y", kind="fin").gain = G_X
    stage("wq", a["xa_wq_2"][0], 4, 1, 8, lin(0), kind="scale", hook=True)
    stage("memk", a["xa_wkv_2"][0], 4, 1, 8, lin(0), rhs="m", kind="memk", n=MEM)
    stage("memv", a["xa_wkv_2"][0], 4, 1, 8, lin(D), rhs="m", kind="memv", swap=True)
    tiles_split("xsplit", ND)
    stage("xo", a["xa_wo_2"][0], 4, 1, 8, lin(0), rhs="y", kind="fin").gain = G_FFN
    mlp("ffn", a["ffn_w1_2"][0], a["ffn_w2_2"][0], G_FIN2)
    U_TOTAL = count["u"]
    final_norm, G_OUT = (count["q"], count["n"] - 1), G_FIN2
    order[-1].loop = False

    def weights(st, j, su):
        if st.kind == "merge":
            return (a["p_rwkv_2"][0], 0, 8, j // 2 * 256) if j % 2 == 0 else (a["p_attn_2"][0], 0, 2, j // 2 * 256)
        return st.w, st.row0 + su * st.kb, st.kb, st.col(j)

    srcs = {"x": (xh, xl), "h": (hh, hl), "y": (yh, yl), "m": (mh, ml)}


    def sp_stage(sp, st):
        def body(p, first):
            for su in range(st.upg):
                w, r, kb, c = weights(st, p.j, su)
                src = w.rearrange("(k p) n -> p k n", p=P)[:, r:r + kb, bass.ds(c, 256)]
                sp.wait_ge(lower, p.unit(su) + 1)
                sp.dma_start(raw[:, p.slot(su), 0:kb], src).then_inc(landed[p.slot(su)], 16)
        run_groups(sp, st, body)

    def act_split(act, p, su):
        act.wait_ge(landed[p.slot(su)], p.turn(su) * 16 + 16)
        act.wait_ge(units, p.unit(su) + 1)
        nc.scalar.activation(wh[:, p.slot(su)], raw[:, p.slot(su)], ACT.Copy).then_inc(upper, 1)

    def dve_split(dve, p, su):
        dve.wait_ge(upper, p.unit(su) + 1)
        nc.vector.tensor_tensor(wl[:, p.slot(su)], raw[:, p.slot(su)], wh[:, p.slot(su)],
                                ALU.subtract).then_inc(lower, 1)

    def split_next(fn, eng, p, st):
        for su in range(st.upg):
            if st is order[-1] and p.c == st.groups - 1 and su == st.upg - 1:
                return
            fn(eng, p, su + 1)

    def pe_stage(pe, st):
        ops = srcs[st.rhs]
        need = (lambda k: st.need0 + k + 1) if st.need0 is not None else None

        def body(p, first):
            banks = [ps[2 * p.pair()], ps[2 * p.pair() + 1]]
            pe.wait_ge(evac, p.group() * 2 + 2)
            for su in range(st.upg):
                slot = p.slot(su)
                kb = st.kb if st.kind != "merge" else (8, 2)[p.c % 2]
                pe.wait_ge(lower, p.unit(su) + 3)
                k0 = su * kb
                terms = ((wh, 0), (wh, 1), (wl, 0))
                if st.swap:
                    nt = 4 if st.rhs == "x" else 2
                    for tt in range(nt):
                        bank = banks[tt // (nt // 2)]
                        o = bank[:, tt % (nt // 2) * 256:tt % (nt // 2) * 256 + 256]
                        for k in range(kb):
                            if need and tt == 0 and p.c == 0:
                                pe.wait_ge(split, need(k))
                            for n_, (wt, oi) in enumerate(terms):
                                last = nc.tensor.matmul(o, ops[oi][:, k, tt * P:tt * P + P], wt[:, slot, k],
                                                        start=k == 0 and n_ == 0, stop=k == kb - 1 and n_ == 2)
                    last.then_inc(units, 1)
                    continue
                mts = (1,) if st.kind == "lora" and p.c == 1 else (0, 1)
                for k in range(kb):
                    kk = k0 + k
                    if st.kind == "merge" and p.c % 2:
                        kk = ND + k
                    if need and (p.c < 1 or st.kind == "merge"):
                        pe.wait_ge(split, need(kk))
                    for mt in mts:
                        for n_, (wt, oi) in enumerate(terms):
                            last = nc.tensor.matmul(banks[mt][:, 0:st.n], wt[:, slot, k, mt * P:mt * P + P],
                                                    ops[oi][:, kk, 0:st.n],
                                                    start=k == 0 and su == 0 and n_ == 0,
                                                    stop=k == kb - 1 and su == st.upg - 1 and n_ == 2)
                last.then_inc(units, 1)
            if first:
                pe_norm(pe, st.norm)
            if st.kind == "rkv" and p.c % 3 == 2:
                pe_pair(pe, p.c // 3 * 2)
                pe_pair(pe, p.c // 3 * 2 + 1)
        run_groups(pe, st, body)

    def pe_norm(pe, n):
        pe.wait_ge(pooled, n[0])
        nc.tensor.matmul(ps[4][:], ones[:], acc[:], start=True, stop=True).then_inc(ssum, 1)

    def act_norm(act, n):
        act.wait_ge(ssum, n[1] + 1)
        nc.scalar.activation(sd[:, 0], ps[4][:], ACT.Sqrt, scale=1.0 / D, bias=small[:, 0:1]).then_inc(rooted, 1)

    def dve_norm(dve, n):
        dve.wait_ge(rooted, n[1] + 1)
        link(nc.vector.reciprocal(rs[:], sd[:, 0]))

    links = [0]

    def link(ins):
        links[0] += 1
        ins.then_inc(chain, 1)
        nc.vector.wait_ge(chain, links[0])

    def col(k, c):
        return prm[k][:, c:c + 1]

    def gaincol(st, t):
        return prm[0][:, bass.ds(t + st.gain, 1)]

    def act_stage(act, st, dest=None, fn=None, custom=None):
        def body(p, first):
            split_next(act_split, act, p, st)
            if first:
                act_norm(act, st.norm)
            if custom:
                custom(p)
            for mt in range(2):
                t = p.j * 2 + mt
                if custom or st.kind in ("scale", "resid", "conv4", "tok", "memk", "memv"):
                    continue
                act.wait_ge(evac, p.group() * 2 + 5 + mt)
                if st.kind in ("fin", "gelusq"):
                    act.wait_ge(pooled, p.i * 2 + (st.q0 + 2 * p.c + mt))
                act.wait_ge(evac, 1)
                if st.kind == "relu":
                    nc.scalar.activation(hh[:, bass.ds(t, 1)], tmp[:, mt:mt + 1, 0:T], ACT.Square).then_inc(acted, 1)
                elif st.kind == "fin":
                    if not st.nosplit:
                        nc.scalar.activation(xh[:, bass.ds(t, 1)], x[:, bass.ds(t, 1)], ACT.Copy,
                                             scale=gaincol(st, t)).then_inc(acted, 1)
                    nc.scalar.activation(sq[:, mt:mt + 1], x[:, bass.ds(t, 1)], ACT.Square).then_inc(squared, 1)
                elif st.kind == "gelusq":
                    nc.scalar.activation(dest[:, bass.ds(t, 1)], tmp[:, mt:mt + 1, 0:T], fn).then_inc(acted, 1)
                    act.wait_ge(acted, p.i * 2 + (st.a0 + 2 * p.c + mt + 3))
                    nc.scalar.activation(sq[:, mt:mt + 1], dest[:, bass.ds(t, 1)], ACT.Square).then_inc(squared, 1)
                elif st.kind in ("gelu", "sigm"):
                    nc.scalar.activation(dest[:, bass.ds(t, 1)], tmp[:, mt:mt + 1, 0:T], fn).then_inc(acted, 1)
        run_groups(act, st, body)

    def pool_stage(pool, st):
        if st.kind not in ("relu", "fin", "gelusq"):
            return
        if st.kind in ("fin", "gelusq"):
            pool_norm_start(pool, st.n0)

        def body(p, first):
            for mt in range(2):
                if st.kind == "relu":
                    pool.wait_ge(evac, p.group() * 2 + 5 + mt)
                    nc.gpsimd.tensor_tensor(hf[:, mt], tmp[:, mt, 0:T], tmp[:, mt, 0:T], ALU.mult).then_inc(pooled, 1)
                else:
                    pool.wait_ge(squared, p.i * 2 + (st.s0 + 2 * p.c + mt + 1))
                    pool.wait_ge(pooled, p.i * 2 + (st.q0 + 2 * p.c + mt + 1))
                    nc.gpsimd.tensor_tensor(acc[:], acc[:], sq[:, mt], ALU.add).then_inc(pooled, 1)
        run_groups(pool, st, body)

    def pool_norm_start(pool, n):
        if n:
            pool.wait_ge(ssum, n)
        nc.gpsimd.memset(acc[:], 0.0).then_inc(pooled, 1)

    def dve_stage(dve, st, dest=None, custom=None):
        def body(p, first):
            split_next(dve_split, dve, p, st)
            if first:
                dve_norm(dve, st.norm)
            dve.wait_ge(units, p.unit(st.upg - 1) + 3)
            b = 2 * p.pair()
            t0 = p.j * 2
            if custom:
                custom(p, b)
            elif st.kind == "relu":
                for mt in range(2):
                    nc.vector.scalar_tensor_tensor(out=tmp[:, mt, 0:T], in0=ps[b + mt][:], scalar=0.0, in1=rs[:],
                                                   op0=ALU.max, op1=ALU.mult).then_inc(evac, 1)
                for mt in range(2):
                    dve.wait_ge(acted, p.i * 2 + (st.a0 + 2 * p.c + mt + 3))
                    dve.wait_ge(pooled, p.i * 2 + (st.q0 + 2 * p.c + mt + 1))
                    t = t0 + mt
                    nc.vector.tensor_tensor(hl[:, bass.ds(t, 1)], hf[:, mt:mt + 1], hh[:, bass.ds(t, 1)],
                                            ALU.subtract).then_inc(split, 1)
            elif st.kind in ("resid", "fin"):
                for mt in range(2):
                    xt = x[:, bass.ds(t0 + mt, 1)]
                    nc.vector.tensor_tensor(xt, xt, ps[b + mt][:].rearrange("p (a n) -> p a n", a=1),
                                            ALU.add).then_inc(evac, 1)
                if st.kind == "fin" and not st.nosplit:
                    for mt in range(2):
                        t = t0 + mt
                        dve.wait_ge(acted, p.i * 2 + (st.a0 + 2 * p.c + mt + 3))
                        nc.vector.scalar_tensor_tensor(out=xl[:, bass.ds(t, 1)], in0=x[:, bass.ds(t, 1)],
                                                       scalar=gaincol(st, t), in1=xh[:, bass.ds(t, 1)],
                                                       op0=ALU.mult, op1=ALU.subtract).then_inc(split, 1)
            elif st.kind in ("gelu", "sigm", "gelusq", "spill"):
                for mt in range(2):
                    dve.wait_ge(acted, p.i * 2 + (st.a0 + 2 * p.c + mt + 1))
                    nc.vector.tensor_tensor(tmp[:, mt, 0:T], ps[b + mt][:], rs[:], ALU.mult).then_inc(evac, 1)
            elif st.kind == "scale":
                for mt in range(2):
                    nc.vector.tensor_tensor(dest[:, bass.ds(t0 + mt, 1)],
                                            ps[b + mt][:].rearrange("p (a n) -> p a n", a=1),
                                            rs[:].rearrange("p (a n) -> p a n", a=1), ALU.mult).then_inc(evac, 1)
        run_groups(dve, st, body)


    prm_rows = [
        [(a["norm_mix_g"], 32), (a["norm_mlp_g"], 32), (a["final_norm_g"], 8), (a["b_norm_g"], 8), (a["norm_mix_g_2"], 8),
         (a["norm_x_g_2"], 8), (a["norm_mem_g_2"], 8), (a["norm_ffn_g_2"], 8), (a["norm_final_g_2"], 8)],
        [(a["a_conv_w"], 80), (a["a_conv_b"], 20)],
        [(a["a_gate_a_b"], 20), (a["a_gate_x_b"], 20), (a["a_lambda"], 20), (a["c_conv_w"], 24), (a["w0_2"], 8), (a["a0_2"], 8),
         (a["k_k_2"], 8), (a["k_a_2"], 8)],
        [(a["r_k_2"], 8), (a["gn_w_2"], 8), (a["gn_b_2"], 8), (a["shift_mu_2"][0, 0:26 * P], 26),
         (a["shift_mu_2"][0, 25 * P + 32:26 * P + 32], 1)],
    ]
    CONVW, CONVB = 0, 80
    GAB, GXB, LAM, CCONV, W0C, A0C, KKC, KAC = 0, 20, 40, 60, 84, 92, 100, 108
    RKC, GNW, GNB, MU = 0, 8, 16, 24
    n_rows = [sum(n for _, n in r) for r in prm_rows]

    def flat(ap):
        n = len(ap.shape)
        if n == 1:
            return ap
        names_ = " ".join("abcd"[:n])
        return ap.rearrange(f"{names_} -> ({names_})")

    def sp_init(sp):
        sp.dma_start(xtok[:], a["x"][0].rearrange("(c p) d -> p c d", p=P)).then_inc(s("x_landed"), 16)
        for i, r in enumerate(prm_rows):
            at_ = 0
            for v, n in r:
                sp.dma_start(rows[at_:at_ + n, i, :], flat(v).rearrange("(r p) -> r p", p=P)).then_inc(s("rows_landed"), 16)
                at_ += n

    N_ROW_DMAS = sum(len(r) for r in prm_rows)

    def pool_init(pool):
        pool.sem_inc(lower, 2)
        pool.sem_inc(units, 2)
        pool.sem_inc(evac, 4)
        pool.sem_inc(acted, 2)
        made = s("constants_made")
        nc.gpsimd.memset(ident[:], 0.0).then_inc(made, 1)
        nc.gpsimd.memset(ones[:], 1.0).then_inc(made, 1)
        nc.gpsimd.memset(headones[:], 0.0).then_inc(made, 1)
        nc.gpsimd.memset(small[:, 0:1], EPS).then_inc(made, 1)
        nc.gpsimd.memset(small[:, 1:2], GN_EPS).then_inc(made, 1)
        pool.wait_ge(made, 5)
        nc.gpsimd.affine_select(out=ident[:], in_=ident[:], compare_op=ALU.not_equal, fill=1.0, base=0,
                                pattern=[[-1, P]], channel_multiplier=1).then_inc(made, 1)
        pool.wait_ge(made, 6)
        nc.gpsimd.memset(headones[0:64, 0:64], 1.0).then_inc(made, 1)
        pool.wait_ge(made, 7)
        nc.gpsimd.memset(headones[64:P, 64:P], 1.0).then_inc(made, 1)
        pool.wait_ge(made, 8)
        pool_squares(pool, stages["init"])

    def pool_squares(pool, norm):
        q0, n = norm[0], norm[1]
        pool_norm_start(pool, n)
        for t in range(ND):
            pool.wait_ge(squared, 8 * n + t + 1)
            pool.wait_ge(pooled, q0 + t + 1)
            nc.gpsimd.tensor_tensor(acc[:], acc[:], sq[:, t % 2], ALU.add).then_inc(pooled, 1)

    def pe_init(pe):
        pe.wait_ge(s("constants_made"), 8)
        pe.wait_ge(s("rows_landed"), 16 * N_ROW_DMAS)
        for i in range(4):
            last = nc.tensor.transpose(ps[7][:, i * P:i * P + n_rows[i]], rows[0:n_rows[i], i, :],
                                       ident[0:n_rows[i], 0:n_rows[i]])
        last.then_inc(s("rows_turned"), 1)
        pe.wait_ge(s("x_landed"), 16)
        for t in range(ND):
            if t >= 3:
                pe.wait_ge(s("x_set"), t - 2)
            for c in range(4):
                last = nc.tensor.transpose(ps[4 + t % 3][:, c * P:c * P + P], xtok[:, c, t * P:t * P + P], ident[:])
            last.then_inc(s("x_turned"), 1)

    def act_resplit(act, norm, g, first):
        q0, n, a0, _ = norm
        for t in range(ND):
            act.wait_ge(s("x_set"), first + t + 1)
            nc.scalar.activation(xh[:, t], x[:, t], ACT.Copy, scale=col(0, g + t)).then_inc(acted, 1)
            if q0 + t > 0:
                act.wait_ge(pooled, q0 + t)
            nc.scalar.activation(sq[:, t % 2], x[:, t], ACT.Square).then_inc(squared, 1)

    def dve_lower(dve, norm, g, t):
        dve.wait_ge(acted, norm[2] + t + 3)
        nc.vector.scalar_tensor_tensor(out=xl[:, t], in0=x[:, t], scalar=col(0, g + t), in1=xh[:, t],
                                       op0=ALU.mult, op1=ALU.subtract).then_inc(split, 1)

    def dve_init(dve):
        dve.wait_ge(s("rows_turned"), 1)
        for i in range(4):
            nc.vector.tensor_copy(prm[i][:, 0:n_rows[i]], ps[7][:, i * P:i * P + n_rows[i]]).then_inc(s("prm_ready"), 1)
        dve.wait_ge(s("prm_ready"), 4)
        for t in range(ND):
            dve.wait_ge(s("x_turned"), t + 1)
            nc.vector.tensor_copy(x[:, t], ps[4 + t % 3][:]).then_inc(s("x_set"), 1)
            if t:
                dve_lower(dve, stages["init"], G_MIX, t - 1)
        dve_lower(dve, stages["init"], G_MIX, ND - 1)

    def act_init(act):
        act.wait_ge(s("prm_ready"), 4)
        act_resplit(act, stages["init"], G_MIX, 0)
        act.wait_ge(s("lambda_abs"), 1)
        nc.scalar.activation(small[:, 24:44], small[:, 4:24], ACT.Exp, scale=-1.0).then_inc(s("lambda_exp"), 1)

    def dve_softplus(dve):
        lam = prm[2][:, LAM:LAM + 20]
        lab, e, z, z2, q = (small[:, 4:24], small[:, 24:44], small[:, 44:64], c8[:, 0], c8[:, 1])
        link(nc.vector.tensor_scalar(z, lam, -1.0, None, ALU.mult))
        link(nc.vector.tensor_tensor(lab, lam, z, ALU.max))
        nc.vector.tensor_copy(lab, lab).then_inc(s("lambda_abs"), 1)
        dve.wait_ge(s("lambda_exp"), 1)
        link(nc.vector.tensor_scalar(z, e, 2.0, None, ALU.add))
        link(nc.vector.reciprocal(z, z))
        link(nc.vector.tensor_tensor(z, z, e, ALU.mult))
        link(nc.vector.tensor_tensor(z2, z, z, ALU.mult))
        link(nc.vector.tensor_scalar(q, z2, 1.0 / 21, 1.0 / 19, ALU.mult, ALU.add))
        for k in range(17, 0, -2):
            link(nc.vector.tensor_tensor(q, q, z2, ALU.mult))
            link(nc.vector.tensor_scalar(q, q, 1.0 / k, None, ALU.add))
        link(nc.vector.tensor_tensor(q, q, z, ALU.mult))
        link(nc.vector.tensor_scalar(z, lam, -1.0, 0.0, ALU.mult, ALU.max))
        link(nc.vector.scalar_tensor_tensor(out=q, in0=q, scalar=2.0, in1=z, op0=ALU.mult, op1=ALU.add))
        link(nc.vector.tensor_scalar(z2, q, -8.0, None, ALU.mult))
        link(nc.vector.tensor_scalar(q, q, 8.0, None, ALU.mult))
        nc.vector.tensor_copy(small[:, 4:5], q[:, 0:1]).then_inc(s("c8_ready"), 1)

    alinks = [0]

    def alink(ins):
        alinks[0] += 1
        ins.then_inc(s("scalar_chain"), 1)
        nc.scalar.wait_ge(s("scalar_chain"), alinks[0])

    plinks = [0]

    def plink(ins):
        plinks[0] += 1
        ins.then_inc(s("pool_chain"), 1)
        nc.gpsimd.wait_ge(s("pool_chain"), plinks[0])

    def act_upper(act, name, t, f, src=None, to=None):
        act.wait_ge(s(name + "_y"), src if src is not None else t + 1)
        nc.scalar.activation((yh if to is None else to)[:, t], f, ACT.Copy).then_inc(acted, 1)

    def dve_lower_y(dve, name, t, f):
        dve.wait_ge(acted, stages[name][1] + t + 3)
        nc.vector.tensor_tensor(yl[:, t], f, yh[:, t], ALU.subtract).then_inc(split, 1)

    band = [(i, o) for o in range(5) for i in range(o * P // HDA * HDA // P, -(-(-(-(o + 1) * P // HDA) * HDA) // P))]
    assert len(band) == 13

    def band_pieces(h):
        def cuts(lo):
            b = [lo] + [m for m in range(P, 5 * P, P) if lo < m < lo + HDA] + [lo + HDA]
            return list(zip(b, b[1:]))
        for r0, r1 in cuts(h * HDA):
            for c0, c1 in cuts(h * HDA):
                yield band.index((r0 // P, c0 // P)), r0, r1, c0, c1

    def pool_a(pool, l):
        j = l // 3
        n = f"l{l}"
        nc.gpsimd.memset(gw[:], 0.0).then_inc(s(n + "gw_zero"), 1)
        pool.wait_ge(s(n + "gw_zero"), 1)
        for grp in range(2):
            if grp:
                pool.wait_ge(s(n + "_band"), 5)
            for g, w in enumerate((a["a_gate_a_w"], a["a_gate_x_w"])):
                for h in range(8):
                    for blk, r0, r1, c0, c1 in band_pieces(h):
                        b = h * HDA
                        pool.dma_start(gw[r0 % P:r0 % P + r1 - r0, g, blk, c0 % P:c0 % P + c1 - c0],
                                       w[j, grp * 8 + h, r0 - b:r1 - b, c0 - b:c1 - b]).then_inc(s(f"{n}_gw{grp}"), 16)
        for t in range(NR):
            pool.wait_ge(s(n + "_exp"), t + 1)
            nc.gpsimd.tensor_tensor(ig[:, t], ig[:, t], xc[:, t], ALU.mult).then_inc(s(n + "_gated"), 1)

    N_PIECES = 2 * sum(1 for h in range(8) for _ in band_pieces(h))

    def dve_conv4(l):
        n, j = f"l{l}", l // 3

        def custom(p, b):
            if p.c == 0:
                for mt in range(2):
                    link(nc.vector.memset(xpad[:, mt, 0:3], 0.0))
            for mt in range(2):
                t = 2 * p.j + mt
                w = lambda k: col(1, CONVW + (j * 4 + k) * NR + t)
                nc.vector.tensor_tensor(xpad[:, mt, 3:3 + T], ps[b + mt][:], rs[:], ALU.mult).then_inc(evac, 1)
                nc.vector.wait_ge(evac, p.group() * 2 + 5 + mt)
                link(nc.vector.tensor_scalar(xc[:, t], xpad[:, mt, 3:3 + T], w(3), col(1, CONVB + j * NR + t), ALU.mult, ALU.add))
                for k in (2, 1):
                    link(nc.vector.scalar_tensor_tensor(out=xc[:, t], in0=xpad[:, mt, k:k + T], scalar=w(k), in1=xc[:, t],
                                                        op0=ALU.mult, op1=ALU.add))
                nc.vector.scalar_tensor_tensor(out=xc[:, t], in0=xpad[:, mt, 0:T], scalar=w(0), in1=xc[:, t],
                                               op0=ALU.mult, op1=ALU.add).then_inc(s(n + "_xc"), 1)
                nc.vector.wait_ge(s(n + "_xc"), t + 1)
        return custom

    def pe_a(pe, l):
        n = f"l{l}"
        for t in range(NR):
            grp, o = t // 5, t % 5
            if o == 0:
                pe.wait_ge(s(f"{n}_gw{grp}"), 16 * N_PIECES)
            if t == 0:
                pe.wait_ge(s(n + "_xc"), NR)
            if t >= 2:
                pe.wait_ge(s(n + "_gates"), 2 * (t - 1))
            mine = [(b, i) for b, (i, oo) in enumerate(band) if oo == o]
            for g in range(2):
                for m, (b, i) in enumerate(mine):
                    last = nc.tensor.matmul(ps[4 + 2 * (t % 2) + g][:], gw[:, g, b], xc[:, 5 * grp + i],
                                            start=m == 0, stop=m == len(mine) - 1)
            last.then_inc(s(n + "_band"), 1)

    def act_a(act, l):
        n, j = f"l{l}", l // 3
        for t in range(NR):
            act.wait_ge(s(n + "_band"), t + 1)
            b = 4 + 2 * (t % 2)
            nc.scalar.activation(ra[:, t], ps[b][:], ACT.Sigmoid, bias=col(2, GAB + j * NR + t)).then_inc(s(n + "_gates"), 1)
            nc.scalar.activation(ig[:, t], ps[b + 1][:], ACT.Sigmoid, bias=col(2, GXB + j * NR + t)).then_inc(s(n + "_gates"), 1)
        act.wait_ge(s("c8_ready"), 1)
        for t in range(NR):
            act.wait_ge(s(n + "_gates"), 2 * t + 2)
            k = j * NR + t
            alink(nc.scalar.activation(th[:, t], ra[:, t], ACT.Tanh, scale=c8[:, 1, k:k + 1]))
            nc.scalar.activation(ra[:, t], ra[:, t], ACT.Exp, scale=c8[:, 0, k:k + 1]).then_inc(s(n + "_exp"), 1)
        for t in range(NR):
            act.wait_ge(s(n + "_var"), t + 1)
            nc.scalar.activation(th[:, t], th[:, t], ACT.Sqrt).then_inc(s(n + "_root"), 1)
        for t in range(NR):
            act_upper(act, n, t, ga[:, t])

    def dve_a(dve, l):
        n = f"l{l}"
        for t in range(NR):
            dve.wait_ge(s(n + "_exp"), t + 1)
            link(nc.vector.tensor_tensor(tmp[:, t % 2, 0:T], ra[:, t], ra[:, t], ALU.mult))
            nc.vector.scalar_tensor_tensor(out=th[:, t], in0=tmp[:, t % 2, 0:T], scalar=1.0, in1=th[:, t],
                                           op0=ALU.add, op1=ALU.mult).then_inc(s(n + "_var"), 1)
        for t in range(NR + 1):
            if t < NR:
                dve.wait_ge(s(n + "_root"), t + 1)
                dve.wait_ge(s(n + "_gated"), t + 1)
                link(nc.vector.tensor_tensor(th[:, t], th[:, t], ig[:, t], ALU.mult))
                link(nc.vector.tensor_tensor_scan(xc[:, t], ra[:, t], th[:, t], 0.0, ALU.mult, ALU.add))
                nc.vector.tensor_tensor(ga[:, t], xc[:, t], ga[:, t], ALU.mult).then_inc(s(n + "_y"), 1)
            if t:
                dve.wait_ge(s(n + "_y"), t)
                dve_lower_y(dve, n + "_mix", t - 1, ga[:, t - 1])

    def sp_b(sp):
        sp.dma_start(wsr[:], a["b_w_s"][0].rearrange("g t s -> t g s")).then_inc(s("ws_landed"), 16)
        sp.dma_start(sbrow[:], a["b_s_bias"][0].rearrange("(a g) t -> a (g t)", a=1)).then_inc(s("sb_landed"), 16)

    def pool_b(pool):
        pool.wait_ge(s("ws_landed"), 16)
        nc.gpsimd.affine_select(out=wsr[:], in_=wsr[:], compare_op=ALU.is_ge, fill=0.0, base=0,
                                pattern=[[0, 8], [-1, P]], channel_multiplier=1).then_inc(s("ws_masked"), 1)

    def pe_b(pe, norm):
        pe.wait_ge(s("ws_masked"), 1)
        for g in range(8):
            last = nc.tensor.transpose(ps[5 + g // 4][:, g % 4 * P:g % 4 * P + P], wsr[:, g], ident[:])
        last.then_inc(s("ws_turned"), 1)
        pe_norm(pe, norm)
        pe.wait_ge(s("sb_landed"), 16)
        pe.wait_ge(s("wsT_ready"), 2)
        for g in range(8):
            pe.wait_ge(s("v_normed"), g + 1)
            if g >= 2:
                pe.wait_ge(s("vtok_ready"), g - 1)
            for c in range(4):
                last = nc.tensor.transpose(ps[4 + g % 2][:, c * P:c * P + P], vv[:, g, c * P:c * P + P], ident[:])
            last.then_inc(s("v_turned"), 1)
            pe.wait_ge(s("vtok_ready"), g + 1)
            if g >= 2:
                pe.wait_ge(s("l1_y"), g - 1)
            for c in range(4):
                o = ps[6 + g % 2][:, c * P:c * P + P]
                nc.tensor.matmul(o, ones[0:1, :], sbrow[0:1, g * P:g * P + P], start=True, stop=False)
                last = nc.tensor.matmul(o, vtok[:, g % 2, c], wsT[:, g], start=False, stop=True)
            last.then_inc(s("mixed"), 1)

    def act_b(act, norm):
        act_norm(act, norm)
        for g in range(8):
            act.wait_ge(s("v_turned"), g + 1)
            if g >= 2:
                act.wait_ge(s("mixed"), g - 1)
            nc.scalar.activation(vtok[:, g % 2], ps[4 + g % 2][:].rearrange("p (c n) -> p c n", c=4), ACT.Copy)\
                .then_inc(s("vtok_ready"), 1)
            if g:
                act_upper(act, "l1", g - 1, uu[:, g - 1])
        act_upper(act, "l1", 7, uu[:, 7])

    def dve_b(dve, norm):
        dve.wait_ge(s("ws_turned"), 1)
        for h in range(2):
            nc.vector.tensor_copy(wsT[:, 4 * h:4 * h + 4], ps[5 + h][:].rearrange("p (c n) -> p c n", c=4))\
                .then_inc(s("wsT_ready"), 1)
        dve_norm(dve, norm)
        dve.wait_ge(acted, stages["l1_u"].a0 + 10)
        for g in range(8):
            nc.vector.scalar_tensor_tensor(out=vv[:, g], in0=vv[:, g], scalar=col(0, G_B + g), in1=rs[:],
                                           op0=ALU.mult, op1=ALU.mult).then_inc(s("v_normed"), 1)
        for g in range(9):
            if g < 8:
                dve.wait_ge(s("mixed"), g + 1)
                nc.vector.tensor_tensor(uu[:, g], uu[:, g], ps[6 + g % 2][:], ALU.mult).then_inc(s("l1_y"), 1)
            if g:
                dve.wait_ge(s("l1_y"), g)
                dve_lower_y(dve, "l1_mix", g - 1, uu[:, g - 1])

    def dve_conv3(p, b):
        which, t0 = p.j % 3, p.j // 3 * 2
        if p.j == 0:
            for mt in range(2):
                link(nc.vector.memset(pc[:, mt, 0:2], 0.0))
        for mt in range(2):
            t = t0 + mt
            w = lambda k: col(2, CCONV + k * 8 + t)
            if which == 0:
                nc.vector.tensor_tensor(gcs[:, mt], ps[b + mt][:], rs[:], ALU.mult).then_inc(evac, 1)
            elif which == 1:
                nc.vector.tensor_tensor(tmp[:, mt, 0:T], ps[b + mt][:], rs[:], ALU.mult).then_inc(evac, 1)
                nc.vector.wait_ge(evac, p.group() * 2 + 5 + mt)
                link(nc.vector.tensor_tensor(pc[:, mt, 2:2 + T], tmp[:, mt, 0:T], gcs[:, mt], ALU.mult))
                link(nc.vector.tensor_scalar(cv[:, mt], pc[:, mt, 2:2 + T], w(2), None, ALU.mult))
                for k in (1, 0):
                    link(nc.vector.scalar_tensor_tensor(out=cv[:, mt], in0=pc[:, mt, k:k + T], scalar=w(k), in1=cv[:, mt],
                                                        op0=ALU.mult, op1=ALU.add))
            else:
                nc.vector.tensor_tensor(tmp[:, mt, 0:T], ps[b + mt][:], rs[:], ALU.mult).then_inc(evac, 1)
                nc.vector.wait_ge(evac, p.group() * 2 + 5 + mt)
                nc.vector.tensor_tensor(cv[:, mt], cv[:, mt], tmp[:, mt, 0:T], ALU.mult).then_inc(s("l2_y"), 1)
                nc.vector.wait_ge(s("l2_y"), t + 1)
                dve_lower_y(nc.vector, "l2_mix", t, cv[:, mt])

    def act_conv3(p):
        if p.j % 3 == 2:
            for mt in range(2):
                t = p.j // 3 * 2 + mt
                act_upper(nc.scalar, "l2", t, cv[:, mt])


    def pool_dist(pool):
        pool.wait_ge(s("dist_free"), 1)
        plink(nc.gpsimd.iota(disti[:], pattern=[[-1, T]], base=384, channel_multiplier=1))
        nc.gpsimd.iota(distf[:], pattern=[[-1, T]], base=384, channel_multiplier=1,
                       allow_small_or_imprecise_dtypes=True).then_inc(s("dist_iota"), 1)

    def dve_dist(dve):
        dve.wait_ge(s("dist_iota"), 1)
        link(nc.vector.tensor_scalar(d0[:], distf[:], 0.0, NEG, ALU.is_lt, ALU.mult))
        link(nc.vector.tensor_tensor(d0[:], d0[:], distf[:], ALU.add))
        link(nc.vector.tensor_scalar(distf[:], distf[:], 128.0, NEG, ALU.is_gt, ALU.mult))
        link(nc.vector.tensor_tensor(dist[:, 0], d0[:], distf[:], ALU.add))
        for g, m in ((1, 3), (2, 15)):
            link(nc.vector.tensor_scalar(distm[:], disti[:], m, None, ALU.bitwise_and))
            link(nc.vector.tensor_copy(distf[:], distm[:]))
            link(nc.vector.tensor_scalar(distf[:], distf[:], 0.0, NEG, ALU.is_gt, ALU.mult))
            link(nc.vector.tensor_tensor(dist[:, g], d0[:], distf[:], ALU.add))

    MIDPREV = (stages["mid"][0], stages["mid"][1] - 1)

    def dve_mid(dve):
        dve_norm(dve, MIDPREV)
        for t in range(ND):
            nc.vector.scalar_tensor_tensor(out=x[:, t], in0=x[:, t], scalar=col(0, G_FIN + t), in1=rs[:],
                                           op0=ALU.mult, op1=ALU.mult).then_inc(s("x_set"), 1)
            if t:
                dve_lower(dve, stages["mid"], G_MIX2, t - 1)
        dve_lower(dve, stages["mid"], G_MIX2, ND - 1)

    def dve_tok(p, b):
        for tt in range(4):
            ins = nc.vector.tensor_scalar(vt[:, tt, p.j * 256:p.j * 256 + 256], ps[b + tt // 2][:, tt % 2 * 256:tt % 2 * 256 + 256],
                                          rscol[:, tt:tt + 1], None, ALU.mult)
            if tt % 2:
                ins.then_inc(evac, 1)

    def pe_rscol(pe):
        pe.wait_ge(evac, stages["q"].g0 * 2 + 6)
        for tt in range(4):
            last = nc.tensor.matmul(ps[5][:, tt:tt + 1], rs[0:1, tt * P:tt * P + P], ones[0:1, 0:1], start=True, stop=True)
        last.then_inc(s("rs_turned"), 1)

    def dve_rscol(dve):
        dve.wait_ge(s("rs_turned"), 1)
        link(nc.vector.tensor_copy(rscol[:, 0:4], ps[5][:, 0:4]))

    combos = [(h, i) for h in range(4) for i in range(4)]
    slopes = [2.0 ** (-8.0 * (k + 1) / 12) for k in range(12)]

    def segments(i):
        out_, at_ = [], 0
        for g in range(3):
            k0 = max(i - 1, 0) if g == 0 else 0
            out_.append((g, k0, at_))
            at_ += (i + 1 - k0) * P
        return out_, at_

    def pe_attn(pe):
        pe.wait_ge(evac, (stages["v"].g0 + 3) * 2 + 4)

        def scores(n):
            h, i = combos[n]
            lo = 64 * (h % 2)
            if n:
                pe.wait_ge(s("at_scored"), n)
            for g, k0, _ in segments(i)[0]:
                ti = (4 * g + h) // 2
                last = nc.tensor.matmul(ps[4 + g][:, 0:(i + 1 - k0) * P], qT[lo:lo + 64, ti, i * P:i * P + P],
                                        kT[lo:lo + 64, ti, k0 * P:(i + 1) * P], start=True, stop=True)
            last.then_inc(s("at_scores"), 1)

        scores(0)
        for n, (h, i) in enumerate(combos):
            if n + 1 < 16:
                scores(n + 1)
            segs, width = segments(i)
            nb = width // P
            pe.wait_ge(s("at_probs"), n + 1)
            if n:
                pe.wait_ge(s("at_pt"), n)
            for b in range(nb):
                last = nc.tensor.transpose(ps[(7, 0, 1)[b // 4]][:, b % 4 * P:b % 4 * P + P], sc[:, n % 2, b * P:b * P + P], ident[:])
            last.then_inc(s("at_turned"), 1)
            pe.wait_ge(s("at_pt"), n + 1)
            o = ps[2 + h // 2][64 * (h % 2):64 * (h % 2) + 64, i * P:i * P + P]
            for g, k0, at_ in segs:
                for k in range(k0, i + 1):
                    b = at_ // P + k - k0
                    last = nc.tensor.matmul(o, vt[:, k, (4 * g + h) * 64:(4 * g + h) * 64 + 64], pt[:, b],
                                            start=b == 0, stop=b == nb - 1)
            last.then_inc(s("at_pv"), 1)
        pe.wait_ge(s("at_done"), 2)

    def dve_attn(dve):
        def score(n):
            h, i = combos[n]
            segs, width = segments(i)
            dve.wait_ge(s("at_scores"), n + 1)
            if n >= 2:
                dve.wait_ge(s("at_turned"), n - 1)
            for g, k0, at_ in segs:
                w = (i + 1 - k0) * P
                x0 = k0 * P + P * (3 - i)
                ins = nc.vector.scalar_tensor_tensor(out=sc[:, n % 2, at_:at_ + w], in0=dist[:, g, x0:x0 + w],
                                                     scalar=-8.0 * slopes[4 * g + h], in1=ps[4 + g][:, 0:w],
                                                     op0=ALU.mult, op1=ALU.add)
            ins.then_inc(s("at_scored"), 1)
            dve.wait_ge(s("at_scored"), n + 1)
            link(nc.vector.tensor_reduce(stat[:, n % 2:n % 2 + 1], sc[:, n % 2, 0:width], AX.X, ALU.max))
            nc.vector.tensor_scalar(stat[:, 2 + n % 2:3 + n % 2], stat[:, n % 2:n % 2 + 1], -0.125, None, ALU.mult)\
                .then_inc(s("at_max"), 1)

        score(0)
        for n, (h, i) in enumerate(combos):
            if n + 1 < 16:
                score(n + 1)
            _, width = segments(i)
            dve.wait_ge(s("at_exp"), n + 1)
            link(nc.vector.reciprocal(den[:, 2 + n % 2:3 + n % 2], den[:, n % 2:n % 2 + 1]))
            nc.vector.tensor_scalar(sc[:, n % 2, 0:width], sc[:, n % 2, 0:width], den[:, 2 + n % 2:3 + n % 2], None, ALU.mult)\
                .then_inc(s("at_probs"), 1)
        dve.wait_ge(s("at_pv"), 16)
        for h in range(2):
            nc.vector.tensor_copy(ya[:, h], ps[2 + h][:]).then_inc(s("at_done"), 1)

    def act_attn(act):
        def exp(n):
            _, width = segments(combos[n][1])
            act.wait_ge(s("at_max"), n + 1)
            nc.scalar.activation(sc[:, n % 2, 0:width], sc[:, n % 2, 0:width], ACT.Exp, scale=0.125,
                                 bias=stat[:, 2 + n % 2:3 + n % 2], accum_out=den[:, n % 2:n % 2 + 1]).then_inc(s("at_exp"), 1)

        exp(0)
        for n, (h, i) in enumerate(combos):
            if n + 1 < 16:
                exp(n + 1)
            nb = segments(i)[1] // P
            act.wait_ge(s("at_turned"), n + 1)
            if n:
                act.wait_ge(s("at_pv"), n)
            for b in range(0, nb, 4):
                m = min(4, nb - b)
                ins = nc.scalar.activation(pt[:, b:b + m], ps[(7, 0, 1)[b // 4]][:, 0:m * P].rearrange("p (a n) -> p a n", n=P), ACT.Copy)
            ins.then_inc(s("at_pt"), 1)

    def act_gates(p):
        act = nc.scalar
        for mt in range(2):
            t = 2 * p.j + mt
            act.wait_ge(evac, p.group() * 2 + 5 + mt)
            if t >= 2:
                act.wait_ge(s(f"gate_stored{mt}"), 16 * (t // 2))
            act.activation(gsp[:, mt], tmp[:, mt, 0:T], ACT.Sigmoid).then_inc(acted, 1)
            act.wait_ge(acted, stages["gates"].a0 + t + 3)
            act.dma_start(gate_spill[t], gsp[:, mt]).then_inc(s(f"gate_stored{mt}"), 16)

    def shift(p, b, mt, mu, dest, done=None):
        nc.vector.tensor_tensor(tmp[:, mt, 1:T + 1], ps[b + mt][:], rs[:], ALU.mult).then_inc(evac, 1)
        nc.vector.wait_ge(evac, p.group() * 2 + 5 + mt)
        link(nc.vector.tensor_tensor(hf[:, mt], tmp[:, mt, 0:T], tmp[:, mt, 1:T + 1], ALU.subtract))
        ins = nc.vector.scalar_tensor_tensor(out=dest, in0=hf[:, mt], scalar=col(3, mu), in1=tmp[:, mt, 1:T + 1],
                                             op0=ALU.mult, op1=ALU.add)
        if done:
            ins.then_inc(s(done), 1)
        else:
            link(ins)

    def dve_lora(p, b):
        if p.j == 0:
            nc.vector.wait_ge(acted, stages["gates"].a0 + 18)
            nc.vector.wait_ge(s("gate_stored0"), 128)
            nc.vector.wait_ge(s("gate_stored1"), 128)
            nc.vector.wait_ge(s("x_stored"), 16)
            for mt in range(2):
                link(nc.vector.memset(tmp[:, mt, 0:1], 0.0))
            shift(p, b, 0, MU + 24, wda[:], "lora_shifted")
            shift(p, b, 1, MU + 25, gd[:, 0], "lora_shifted")
        else:
            nc.vector.memset(small[:, 44:45], 0.0).then_inc(evac, 1)
            shift(p, b, 1, MU + 26, gd[:, 1], "lora_shifted")

    def act_lora(p):
        act = nc.scalar
        if p.j == 0:
            act.wait_ge(s("lora_shifted"), 1)
            act.activation(wda[0:64], wda[0:64], ACT.Tanh).then_inc(s("lora_ready"), 1)
            act.wait_ge(s("lora_shifted"), 2)
            act.activation(gd[:, 0], gd[:, 0], ACT.Sigmoid).then_inc(s("lora_ready"), 1)
        else:
            act.wait_ge(s("lora_shifted"), 3)
            act.activation(gd[:, 1], gd[:, 1], ACT.Sigmoid).then_inc(s("lora_ready"), 1)

    T1, T2, T3, T4, T5, T6 = rt[:, 4], rt[:, 5], rt[:, 6], rt[:, 7], hf[:, 0], hf[:, 1]
    rmask = acc

    def pe_pair(pe, q):
        cs = slice(q * P, q * P + P)
        if q == 0:
            pe.wait_ge(s("lora_landed"), 32)
            pe.wait_ge(s("lora_ready"), 1)
        else:
            pe.wait_ge(s("pair_gates"), 2 * q)
        nc.tensor.matmul(ps[4][:], w2a2[0:64, cs], wda[0:64], start=True, stop=True)
        nc.tensor.matmul(ps[5][:], w2a2[64:P, cs], wda[64:P], start=True, stop=True).then_inc(s("pair_lora"), 1)
        pe.wait_ge(s("pair_kk"), q + 1)
        nc.tensor.matmul(ps[6][:], headones[:], T6, start=True, stop=True).then_inc(s("pair_sum"), 1)
        pe.wait_ge(s("pair_rk"), q + 1)
        if q:
            pe.wait_ge(s("pair_bonus"), q)
        nc.tensor.matmul(ps[7][:], headones[:], T1, start=True, stop=True).then_inc(s("pair_rksum"), 1)

    def act_pair(act, q):
        k = rt[:, 2 + q % 2]
        act.wait_ge(s("pair_lora"), q + 1)
        act.activation(T1, ps[4][:], ACT.Sigmoid, bias=col(2, W0C + q)).then_inc(s("pair_gates"), 1)
        act.activation(T4, ps[5][:], ACT.Sigmoid, bias=col(2, A0C + q)).then_inc(s("pair_gates"), 1)
        act.wait_ge(s("pair_start"), q + 1)
        act.activation(T6, k, ACT.Square, scale=col(2, KKC + q)).then_inc(s("pair_kk"), 1)
        act.wait_ge(s("pair_cum"), q + 1)
        act.activation(T5, T2, ACT.Exp, scale=-LOG_DECAY).then_inc(s("pair_exp"), 1)
        act.activation(T3, T3, ACT.Exp, scale=-LOG_DECAY).then_inc(s("pair_exp"), 1)
        act.wait_ge(s("pair_exp"), 3 * q + 2)
        act.activation(T2, T2, ACT.Exp, scale=LOG_DECAY).then_inc(s("pair_exp"), 1)
        act.wait_ge(s("pair_sum"), q + 1)
        act.activation(T6, ps[6][:], ACT.Sqrt).then_inc(s("pair_root"), 1)
        act.wait_ge(s("pair_bonus"), q + 1)
        act.dma_start(bonus_spill[q], T3).then_inc(s("bonus_stored"), 16)

    def c3(t_):
        return t_.rearrange("p (c n) -> p c n", c=NC)

    def dve_pair(dve, q):
        r, k = rt[:, q % 2], rt[:, 2 + q % 2]
        nc.vector.memset(small[:, 46:47], 0.0).then_inc(s("pair_start"), 1)
        dve.wait_ge(s("pair_gates"), 2 * q + 1)
        if q:
            dve.wait_ge(s("bonus_stored"), 16 * q)
        link(nc.vector.tensor_tensor_scan(T2, rmask[:], T1, 0.0, ALU.mult, ALU.add))
        nc.vector.tensor_tensor(T3, T2, T1, ALU.subtract).then_inc(s("pair_cum"), 1)
        dve.wait_ge(s("pair_root"), q + 1)
        dve.wait_ge(s("pair_cum"), q + 1)
        link(nc.vector.tensor_scalar(T1, T6, 1e-12, None, ALU.max))
        link(nc.vector.reciprocal(T1, T1))
        link(nc.vector.scalar_tensor_tensor(out=T6, in0=k, scalar=col(2, KKC + q), in1=T1, op0=ALU.mult, op1=ALU.mult))
        link(nc.vector.tensor_tensor(T1, T6, T4, ALU.mult))
        dve.wait_ge(s("pair_exp"), 3 * q + 3)
        nc.vector.scalar_tensor_tensor(out=AR[:, :, q, 0, :], in0=c3(T6), scalar=-1.0, in1=c3(T3), op0=ALU.mult, op1=ALU.mult)
        link(nc.vector.tensor_tensor(BT[:, :, q, :], c3(T1), c3(T2), ALU.mult))
        link(nc.vector.tensor_scalar(T4, T4, -1.0, col(2, KAC + q), ALU.add, ALU.mult))
        link(nc.vector.scalar_tensor_tensor(out=T4, in0=T4, scalar=1.0, in1=k, op0=ALU.add, op1=ALU.mult))
        nc.vector.tensor_tensor(KT[:, :, q, :], c3(T4), c3(T2), ALU.mult)
        nc.vector.tensor_tensor(AR[:, :, q, 1, :], c3(r), c3(T5), ALU.mult)
        link(nc.vector.tensor_copy(PCt[:, :, q:q + 1], c3(T5)[:, :, CH - 1:CH]))
        nc.vector.scalar_tensor_tensor(out=T1, in0=r, scalar=col(3, RKC + q), in1=T4, op0=ALU.mult, op1=ALU.mult)\
            .then_inc(s("pair_rk"), 1)
        dve.wait_ge(s("pair_rksum"), q + 1)
        nc.vector.tensor_tensor(T3, ps[7][:], VT[:, q], ALU.mult).then_inc(s("pair_bonus"), 1)

    def dve_rkv(p, b):
        which, jj = p.j % 3, p.j // 3
        if p.j == 0:
            link(nc.vector.memset(rmask[:], 1.0))
            link(nc.vector.memset(c3(rmask[:])[:, :, 0:1], 0.0))
        for mt in range(2):
            q = 2 * jj + mt
            dest = (rt[:, mt], rt[:, 2 + mt], VT[:, q])[which]
            if q >= 2 and which == 0 and mt == 0:
                nc.vector.wait_ge(s("pair_bonus"), q)
            shift(p, b, mt, MU + which * 8 + q, dest, "k_shifted" if which == 1 else None)
        if which == 1:
            nc.vector.wait_ge(s("k_shifted"), 2 * jj + 2)
        if which == 2:
            dve_pair(nc.vector, 2 * jj)
            dve_pair(nc.vector, 2 * jj + 1)

    def act_rkv(p):
        if p.j % 3 == 2:
            act_pair(nc.scalar, p.j // 3 * 2)
            act_pair(nc.scalar, p.j // 3 * 2 + 1)

    Vt, Bt, Kt, TM, X, Z, Yt, W0, U, ST = (ck[n_] for n_ in names)
    HP = (slice(0, 64), slice(64, P))
    cols = lambda q: slice(q * CH, q * CH + CH)

    def dve_chunk_masks(dve):
        link(nc.vector.tensor_copy(i64[0:64], ident[0:64, 0:64]))
        link(nc.vector.tensor_copy(i64[64:P], ident[64:P, 64:P]))
        dve.wait_ge(s("token_numbers"), 3)
        link(nc.vector.tensor_tensor(mk[:, 0], srcf[:], tgtf[:], ALU.is_lt))
        link(nc.vector.tensor_tensor(mk[:, 1], srcf[:], tgtf[:], ALU.is_le))
        for l in range(6):
            if l == 5:
                link(nc.vector.tensor_copy(mk[:, 7], mk[:, 0]))
            else:
                link(nc.vector.tensor_scalar(inta[:], srci[:], l + 1, None, ALU.logical_shift_right))
                link(nc.vector.tensor_scalar(intb[:], tgti[:], l + 1, None, ALU.logical_shift_right))
                link(nc.vector.tensor_tensor(mk[:, 2 + l], inta[:], intb[:], ALU.is_equal))
                link(nc.vector.tensor_tensor(mk[:, 2 + l], mk[:, 2 + l], mk[:, 0], ALU.mult))
        for l in range(5, 0, -1):
            link(nc.vector.tensor_tensor(mk[:, 2 + l], mk[:, 2 + l], mk[:, 1 + l], ALU.subtract))
        link(nc.vector.memset(ST[:], 0.0))

    def pool_tokens(pool):
        pool.wait_ge(s("rkv_done"), 1)
        plink(nc.gpsimd.iota(srci[0:64], pattern=[[0, CH]], base=0, channel_multiplier=1))
        plink(nc.gpsimd.iota(srci[64:P], pattern=[[0, CH]], base=0, channel_multiplier=1))
        nc.gpsimd.iota(tgti[:], pattern=[[1, CH]], base=0, channel_multiplier=0).then_inc(s("token_numbers"), 1)
        pool.wait_ge(s("token_numbers"), 1)
        nc.gpsimd.tensor_copy(srcf[:], srci[:]).then_inc(s("token_numbers"), 1)
        pool.wait_ge(s("token_numbers"), 2)
        nc.gpsimd.tensor_copy(tgtf[:], tgti[:]).then_inc(s("token_numbers"), 1)

    def each_head(fn):
        for hp in range(2):
            for q in range(NH2):
                last = fn(HP[hp], q)
        return last

    mm = nc.tensor.matmul

    def pe_chunks(pe):
        pe.wait_ge(s("chunk_masks"), 1)
        for c in range(NC):
            n = 64 * c
            if c:
                pe.wait_ge(s("ck_turned_copied"), 3 * c)
                pe.wait_ge(s("ck_out"), c)
                pe.wait_ge(s("ck_state"), c)
            for src, bank in ((lambda h, q: VT[h, q, c * CH:c * CH + CH], 4), (lambda h, q: BT[h, c, q], 5), (lambda h, q: KT[h, c, q], 6)):
                last = each_head(lambda h, q: mm(ps[bank][h, cols(q)], src(h, q), i64[h, :], start=True, stop=True))
            last.then_inc(s("ck_turned"), 1)
            for src, bank in ((BT, 0), (KT, 2)):
                last = each_head(lambda h, q: mm(ps[bank + q // 4][h, q % 4 * P:q % 4 * P + P], src[h, c, q], AR[h, c, q].rearrange("p a n -> p (a n)"),
                                                 start=True, stop=True))
            last.then_inc(s("ck_products"), 1)
            pe.wait_ge(s("ck_level"), 6 * c + 1)
            each_head(lambda h, q: mm(ps[7][h, cols(q)], TM[h, q], i64[h, :], start=True, stop=True)).then_inc(s("ck_inv"), 1)
            pe.wait_ge(s("ck_turned_copied"), 3 * c + 3)
            for l in range(1, 6):
                pe.wait_ge(s("ck_level"), 6 * c + l + 1)
                each_head(lambda h, q: mm(ps[4][h, cols(q)], TM[h, q], X[h, q], start=True, stop=True)).then_inc(s("ck_y"), 1)
                pe.wait_ge(s("ck_y_copied"), 5 * c + l)
                if l < 5:
                    each_head(lambda h, q: mm(ps[5][h, cols(q)], Z[h, q], Yt[h, q], start=True, stop=True))
                each_head(lambda h, q: mm(ps[6][h, cols(q)], Yt[h, q], Z[h, q], start=True, stop=True)).then_inc(s("ck_inv"), 1)
            pe.wait_ge(s("ck_inverse"), c + 1)
            for hp in range(2):
                h = HP[hp]
                for q in range(NH2):
                    mm(ps[7][h, cols(q)], AR[h, c, q, 0], ST[h, q], start=True, stop=False)
                    last = mm(ps[7][h, cols(q)], TLK[h, q, 0], Vt[h, q], start=False, stop=True)
            last.then_inc(s("ck_w0"), 1)
            pe.wait_ge(s("ck_w0_copied"), c + 1)
            each_head(lambda h, q: mm(ps[4][h, cols(q)], Z[h, q], W0[h, q], start=True, stop=True)).then_inc(s("ck_u"), 1)
            pe.wait_ge(s("ck_u_copied"), c + 1)
            for hp in range(2):
                h = HP[hp]
                for q in range(NH2):
                    mm(ps[5][h, cols(q)], Bt[h, q], U[h, q], start=True, stop=False)
                    last = mm(ps[5][h, cols(q)], Kt[h, q], Vt[h, q], start=False, stop=True)
            last.then_inc(s("ck_ds"), 1)
            for hp in range(2):
                h = HP[hp]
                for q in range(NH2):
                    mm(ps[6][h, cols(q)], ST[h, q], AR[h, c, q, 1], start=True, stop=False)
                    mm(ps[6][h, cols(q)], U[h, q], TLB[h, q, 1], start=False, stop=False)
                    last = mm(ps[6][h, cols(q)], Vt[h, q], TLK[h, q, 1], start=False, stop=True)
            last.then_inc(s("ck_yout"), 1)
        pe.wait_ge(s("ck_out"), NC)
        pe.wait_ge(s("ck_state"), NC)

    def b3(bank, n_=CH):
        return ps[bank][:].rearrange("p (q n) -> p q n", n=n_)

    def act_chunks(act):
        for c in range(NC):
            act.wait_ge(s("ck_turned"), c + 1)
            if c:
                act.wait_ge(s("ck_yout"), c)
            for dst, bank in ((Vt, 4), (Bt, 5), (Kt, 6)):
                act.activation(dst[:], b3(bank), ACT.Copy).then_inc(s("ck_turned_copied"), 1)
            for l in range(1, 6):
                act.wait_ge(s("ck_y"), 5 * c + l)
                act.activation(Yt[:], b3(4), ACT.Copy).then_inc(s("ck_y_copied"), 1)
            act.wait_ge(s("ck_w0"), c + 1)
            act.activation(W0[:], b3(7), ACT.Copy).then_inc(s("ck_w0_copied"), 1)
            act.wait_ge(s("ck_u"), c + 1)
            act.activation(U[:], b3(4), ACT.Copy).then_inc(s("ck_u_copied"), 1)
            act.wait_ge(s("ck_yout"), c + 1)
            act.activation(VT[:, :, c * CH:c * CH + CH], b3(6), ACT.Copy).then_inc(s("ck_out"), 1)

    def dve_chunks(dve):
        dve_chunk_masks(dve)
        nc.vector.memset(small[:, 44:45], 0.0).then_inc(s("chunk_masks"), 1)
        bc = lambda m, n_: m.unsqueeze(1).to_broadcast([P, n_, CH])
        pair = mk[:, 0:2].unsqueeze(1).to_broadcast([P, 4, 2, CH])
        for c in range(NC):
            dve.wait_ge(s("ck_products"), c + 1)
            if c:
                dve.wait_ge(s("ck_yout"), c)
            for dst, bank in ((TLB, 0), (TLK, 2)):
                for hf_ in range(2):
                    ins = nc.vector.tensor_tensor(dst[:, 4 * hf_:4 * hf_ + 4], ps[bank + hf_][:].rearrange("p (q a n) -> p q a n", q=4, a=2),
                                                  pair, ALU.mult)
                link(ins)
            link(nc.vector.tensor_tensor(TM[:], TLB[:, :, 0], bc(mk[:, 2], NH2), ALU.mult))
            nc.vector.tensor_tensor(Z[:], TM[:], bc(i64[:], NH2), ALU.add).then_inc(s("ck_level"), 1)
            dve.wait_ge(s("ck_inv"), 6 * c + 1)
            link(nc.vector.tensor_tensor(X[:], b3(7), bc(i64[:], NH2), ALU.add))
            for l in range(1, 6):
                nc.vector.tensor_tensor(TM[:], TLB[:, :, 0], bc(mk[:, 2 + l], NH2), ALU.mult).then_inc(s("ck_level"), 1)
                dve.wait_ge(s("ck_inv"), 6 * c + l + 1)
                if l < 5:
                    nc.vector.tensor_tensor(X[:], X[:], b3(5), ALU.add)
                    link(nc.vector.tensor_tensor(Z[:], Z[:], b3(6), ALU.add))
                else:
                    nc.vector.tensor_tensor(Z[:], Z[:], b3(6), ALU.add).then_inc(s("ck_inverse"), 1)
            dve.wait_ge(s("ck_yout"), c + 1)
            link(nc.vector.tensor_tensor(ST[:], ST[:], b3(5), ALU.add))
            nc.vector.tensor_tensor(ST[:], ST[:], PCt[:, c, :].unsqueeze(2).to_broadcast([P, NH2, CH]), ALU.mult)\
                .then_inc(s("ck_state"), 1)

    def pe_heads(pe):
        pe.wait_ge(s("g2_landed"), 32)
        for q in range(ND):
            cs = slice(q * P, q * P + P)
            if q:
                pe.wait_ge(s("hd_centred"), q)
            mm(ps[4][:], headones[:], VT[:, q], start=True, stop=True).then_inc(s("hd_mean"), 1)
            if q:
                pe.wait_ge(s("ysplit_y"), q)
            mm(ps[6][:], g2s[:, 0, cs], gd[:, 0], start=True, stop=False)
            mm(ps[6][:], g2s[96:P, 1, cs], gd[96:P, 1], start=False, stop=True).then_inc(s("hd_gate"), 1)
            pe.wait_ge(s("hd_squared"), q + 1)
            mm(ps[5][:], headones[:], gns[:, 1], start=True, stop=True).then_inc(s("hd_var"), 1)

    def act_heads(act):
        for q in range(ND):
            act.wait_ge(s("hd_centred"), q + 1)
            act.activation(gns[:, 1], VT[:, q], ACT.Square).then_inc(s("hd_squared"), 1)
            act.wait_ge(s("hd_var"), q + 1)
            act.activation(gns[:, 0], ps[5][:], ACT.Sqrt, scale=1.0 / 64, bias=small[:, 1:2]).then_inc(s("hd_root"), 1)
            act_upper(act, "ysplit", q, VT[:, q])
        for h in range(2):
            act.activation(yh[:, ND + h], ya[:, h], ACT.Copy).then_inc(acted, 1)

    def dve_heads(dve):
        for q in range(ND):
            dve.wait_ge(s("hd_mean"), q + 1)
            nc.vector.scalar_tensor_tensor(out=VT[:, q], in0=ps[4][:], scalar=-1.0 / 64, in1=VT[:, q], op0=ALU.mult, op1=ALU.add)\
                .then_inc(s("hd_centred"), 1)
            dve.wait_ge(s("hd_root"), q + 1)
            link(nc.vector.reciprocal(gns[:, 2], gns[:, 0]))
            link(nc.vector.scalar_tensor_tensor(out=VT[:, q], in0=VT[:, q], scalar=col(3, GNW + q), in1=gns[:, 2], op0=ALU.mult, op1=ALU.mult))
            dve.wait_ge(s(f"bonus_back{q % 2}"), 16 * (q // 2 + 1))
            link(nc.vector.scalar_tensor_tensor(out=VT[:, q], in0=VT[:, q], scalar=col(3, GNB + q), in1=bon[:, q % 2], op0=ALU.add, op1=ALU.add))
            dve.wait_ge(s("hd_gate"), q + 1)
            nc.vector.tensor_tensor(VT[:, q], VT[:, q], ps[6][:], ALU.mult).then_inc(s("ysplit_y"), 1)
            dve_lower_y(dve, "ysplit", q, VT[:, q])
        dve.wait_ge(split, stages["ysplit"][0] + ND)
        for h in range(2):
            dve_lower_y(dve, "ysplit", ND + h, ya[:, h])

    def pool_heads(pool):
        pool.wait_ge(s("ck_state"), NC)
        pool.wait_ge(s("ck_out"), NC)
        pool.dma_start(g2s[:, 0], a["g2_2"][0, 0:P]).then_inc(s("g2_landed"), 16)
        pool.dma_start(g2s[96:P, 1], a["g2_2"][0, P:P + 32]).then_inc(s("g2_landed"), 16)
        pool.wait_ge(s("bonus_stored"), 16 * ND)
        for q in range(ND):
            if q >= 2:
                pool.wait_ge(s("ysplit_y"), q - 1)
            pool.dma_start(bon[:, q % 2], bonus_spill[q]).then_inc(s(f"bonus_back{q % 2}"), 16)
        pool.wait_ge(s("gate_stored0"), 128)
        pool.wait_ge(s("gate_stored1"), 128)
        pool.dma_start(gl[:], gate_spill.rearrange("t p n -> p t n")).then_inc(s("gates_back"), 16)
        pool.wait_ge(s("x_stored"), 16)
        pool.dma_start(x[:], x_spill).then_inc(s("x_back"), 16)

    def dve_merge(p, b):
        dve = nc.vector
        if p.j == 0:
            dve.wait_ge(s("gates_back"), 16)
        for mt in range(2):
            t = p.j // 2 * 2 + mt
            if p.j % 2 == 0:
                dve.tensor_tensor(mg[:, t], ps[b + mt][:], gl[:, t], ALU.mult).then_inc(evac, 1)
            else:
                if mt == 0:
                    dve.wait_ge(evac, p.group() * 2 + 4)
                dve.tensor_tensor(gl[:, t], ps[b + mt][:], gl[:, ND + t], ALU.mult).then_inc(evac, 1)
                dve.wait_ge(evac, p.group() * 2 + 5 + mt)
                dve.tensor_tensor(mg[:, t], mg[:, t], gl[:, t], ALU.add).then_inc(s("msplit_y"), 1)

    def act_msplit(act):
        act.wait_ge(units, stages["merge"].u0 + 10)
        for t in range(ND):
            act_upper(act, "msplit", t, mg[:, t])

    def dve_msplit(dve):
        dve.wait_ge(s("x_back"), 16)
        for t in range(ND):
            dve_lower_y(dve, "msplit", t, mg[:, t])

    def sp_mem(sp):
        sp.dma_start(mtok[:], a["mem_2"][0].rearrange("(c p) d -> p c d", p=P)).then_inc(s("mem_landed"), 16)

    def pe_mem(pe):
        for c in range(2):
            pe.wait_ge(s("mem_normed"), c + 1)
        for t in range(ND):
            if t >= 2:
                pe.wait_ge(s("mem_split"), t - 1)
            for c in range(2):
                last = nc.tensor.transpose(ps[4 + t % 2][:, c * P:c * P + P], mtok[:, c, t * P:t * P + P], ident[:])
            last.then_inc(s("mem_turned"), 1)
        pe.wait_ge(s("mem_split"), ND)

    def act_mem(act):
        act.wait_ge(s("mem_landed"), 16)
        for c in range(2):
            act.activation(mjunk[:], mtok[:, c], ACT.Square, accum_out=msq[:, c:c + 1]).then_inc(s("mem_summed"), 1)
            act.wait_ge(s("mem_summed"), c + 1)
        act.activation(msq[:, 2:4], msq[:, 0:2], ACT.Sqrt, scale=1.0 / D, bias=small[:, 0:1]).then_inc(s("mem_root"), 1)
        for t in range(ND):
            act.wait_ge(s("mem_turned"), t + 1)
            act.activation(mh[:, t], ps[4 + t % 2][:, 0:MEM], ACT.Copy, scale=col(0, G_MEM + t)).then_inc(s("mem_upper"), 1)

    def dve_mem(dve):
        dve.wait_ge(s("mem_root"), 1)
        link(nc.vector.reciprocal(msq[:, 4:6], msq[:, 2:4]))
        for c in range(2):
            nc.vector.tensor_scalar(mtok[:, c], mtok[:, c], msq[:, 4 + c:5 + c], None, ALU.mult).then_inc(s("mem_normed"), 1)
        for t in range(ND):
            dve.wait_ge(s("mem_upper"), t + 1)
            nc.vector.scalar_tensor_tensor(out=ml[:, t], in0=ps[4 + t % 2][:, 0:MEM], scalar=col(0, G_MEM + t), in1=mh[:, t],
                                           op0=ALU.mult, op1=ALU.subtract).then_inc(s("mem_split"), 1)

    def dve_memk(p, b):
        for mt in range(2):
            nc.vector.tensor_copy(kx[:, 2 * p.j + mt], ps[b + mt][:, 0:MEM]).then_inc(evac, 1)

    def dve_memv(p, b):
        for tt in range(2):
            nc.vector.tensor_copy(vx[:, tt, p.j * 256:p.j * 256 + 256], ps[b + tt][:, 0:256]).then_inc(evac, 1)

    def pe_cross(pe):
        pe.wait_ge(evac, (stages["memv"].g0 + 4) * 2 + 4)

        def scores(n):
            h, i = n // 4, n % 4
            if n >= 2:
                pe.wait_ge(s("cx_max"), n - 1)
                pe.wait_ge(s("cx_exp"), n - 1)
            for t in range(2):
                last = mm(ps[4 + n % 2][:, 0:MEM], qx[:, 2 * h + t, i * P:i * P + P], kx[:, 2 * h + t], start=t == 0, stop=t == 1)
            last.then_inc(s("cx_scores"), 1)

        scores(0)
        scores(1)
        for n in range(16):
            h, i = n // 4, n % 4
            if n + 2 < 16:
                scores(n + 2)
            pe.wait_ge(s("cx_probs"), n + 1)
            if h and i == 0:
                pe.wait_ge(s("cx_pt"), 2 * h)
            for t in range(2):
                last = nc.tensor.transpose(ps[6 + t][:, i * P:i * P + P], sx[:, n % 4, t * P:t * P + P], ident[:])
            last.then_inc(s("cx_turned"), 1)
            if i == 3:
                pe.wait_ge(s("cx_pt"), 2 * h + 2)
                if h:
                    pe.wait_ge(s("cx_y"), 2 * h)
                for ct in range(2):
                    for t in range(2):
                        c0 = h * 256 + ct * P
                        last = mm(ps[ct][:], vx[:, t, c0:c0 + P], ptx[:, t], start=t == 0, stop=t == 1)
                last.then_inc(s("cx_out"), 1)
        pe.wait_ge(s("cx_y"), 8)

    def act_cross(act):
        for n in range(17):
            if n < 16:
                act.wait_ge(s("cx_max"), n + 1)
                act.activation(sx[:, n % 4], ps[4 + n % 2][:, 0:MEM], ACT.Exp, scale=1.0 / 16, bias=stx[:, 4 + n % 4:5 + n % 4],
                               accum_out=stx[:, 8 + n % 4:9 + n % 4]).then_inc(s("cx_exp"), 1)
            if n and n % 4 == 0:
                h = n // 4 - 1
                act.wait_ge(s("cx_turned"), 4 * h + 4)
                if h:
                    act.wait_ge(s("cx_out"), h)
                for t in range(2):
                    act.activation(ptx[:, t], ps[6 + t][:], ACT.Copy).then_inc(s("cx_pt"), 1)
        for t in range(ND):
            act.wait_ge(s("cx_y"), t + 1)
            act.activation(yh[:, t], qx[:, t], ACT.Copy).then_inc(acted, 1)

    def dve_cross(dve):
        def out_tiles(h):
            dve.wait_ge(s("cx_out"), h + 1)
            for ct in range(2):
                nc.vector.tensor_copy(qx[:, 2 * h + ct], ps[ct][:]).then_inc(s("cx_y"), 1)

        def top(n):
            dve.wait_ge(s("cx_scores"), n + 1)
            if n >= 4:
                dve.wait_ge(s("cx_turned"), n - 3)
            link(nc.vector.tensor_reduce(stx[:, n % 4:n % 4 + 1], ps[4 + n % 2][:, 0:MEM], AX.X, ALU.max))
            nc.vector.tensor_scalar(stx[:, 4 + n % 4:5 + n % 4], stx[:, n % 4:n % 4 + 1], -1.0 / 16, None, ALU.mult).then_inc(s("cx_max"), 1)

        top(0)
        for n in range(16):
            if n + 1 < 16:
                top(n + 1)
            dve.wait_ge(s("cx_exp"), n + 1)
            link(nc.vector.reciprocal(stx[:, 12 + n % 4:13 + n % 4], stx[:, 8 + n % 4:9 + n % 4]))
            nc.vector.tensor_scalar(sx[:, n % 4], sx[:, n % 4], stx[:, 12 + n % 4:13 + n % 4], None, ALU.mult).then_inc(s("cx_probs"), 1)
            if n % 4 == 0 and n:
                out_tiles(n // 4 - 1)
        out_tiles(3)
        for t in range(ND):
            dve.wait_ge(acted, stages["xsplit"][1] + t + 3)
            nc.vector.tensor_tensor(yl[:, t], qx[:, t], yh[:, t], ALU.subtract).then_inc(split, 1)

    def sp_extra(sp, name):
        if name == "gates":
            sp.wait_ge(s("at_done"), 2)
            sp.dma_start(w2a2[0:64], a["w2_2"][0]).then_inc(s("lora_landed"), 16)
            sp.dma_start(w2a2[64:P], a["a2_2"][0]).then_inc(s("lora_landed"), 16)
            sp.dma_start(x_spill, x[:]).then_inc(s("x_stored"), 16)
        if name == "wq":
            sp.wait_ge(units, stages["wq"].u0 + 2)
            sp_mem(sp)

    def pool_second(pool):
        pool_squares(pool, G["mid"])
        pool_dist(pool)
        pool_tokens(pool)
        pool_heads(pool)
        pool_stage(pool, G["out2"])
        pool_stage(pool, G["xo"])
        pool_mlp(pool, "ffn")

    def pe_second(pe):
        pe_norm(pe, MIDPREV)
        pe_stage(pe, G["q"])
        pe_rscol(pe)
        pe_stage(pe, G["k"])
        pe_stage(pe, G["v"])
        pe_attn(pe)
        pe_stage(pe, G["gates"])
        pe_stage(pe, G["lora"])
        pe_stage(pe, G["rkv"])
        pe_chunks(pe)
        pe_heads(pe)
        pe_stage(pe, G["merge"])
        pe_stage(pe, G["out2"])
        pe_stage(pe, G["wq"])
        pe_mem(pe)
        pe_stage(pe, G["memk"])
        pe_stage(pe, G["memv"])
        pe_cross(pe)
        pe_stage(pe, G["xo"])
        for h in range(2):
            pe_stage(pe, G[f"ffn_up{h}"])
            pe_stage(pe, G[f"ffn_down{h}"])

    def act_second(act):
        act_norm(act, MIDPREV)
        act_resplit(act, G["mid"], G_MIX2, ND)
        act_stage(act, G["q"])
        act_stage(act, G["k"])
        act_stage(act, G["v"])
        act_attn(act)
        act_stage(act, G["gates"], custom=act_gates)
        act_stage(act, G["lora"], custom=act_lora)
        act_stage(act, G["rkv"], custom=act_rkv)
        act_chunks(act)
        act_heads(act)
        act_stage(act, G["merge"], custom=lambda p: None)
        act_msplit(act)
        act_stage(act, G["out2"])
        act_stage(act, G["wq"])
        act_mem(act)
        act_stage(act, G["memk"])
        act_stage(act, G["memv"])
        act_cross(act)
        act_stage(act, G["xo"])
        for h in range(2):
            act_stage(act, G[f"ffn_up{h}"])
            act_stage(act, G[f"ffn_down{h}"])

    def dve_second(dve):
        dve_mid(dve)
        nc.vector.memset(small[:, 45:46], 0.0).then_inc(s("dist_free"), 1)
        dve_stage(dve, G["q"], qT)
        dve_rscol(dve)
        dve_stage(dve, G["k"], kT)
        dve_stage(dve, G["v"], custom=dve_tok)
        dve_dist(dve)
        dve_attn(dve)
        dve_stage(dve, G["gates"])
        dve_stage(dve, G["lora"], custom=dve_lora)
        dve_stage(dve, G["rkv"], custom=dve_rkv)
        nc.vector.memset(small[:, 45:46], 0.0).then_inc(s("rkv_done"), 1)
        dve_chunks(dve)
        dve_heads(dve)
        dve_stage(dve, G["merge"], custom=dve_merge)
        dve_msplit(dve)
        dve_stage(dve, G["out2"])
        dve_stage(dve, G["wq"], qx)
        dve_mem(dve)
        dve_stage(dve, G["memk"], custom=dve_memk)
        dve_stage(dve, G["memv"], custom=dve_memv)
        dve_cross(dve)
        dve_stage(dve, G["xo"])
        for h in range(2):
            dve_stage(dve, G[f"ffn_up{h}"])
            dve_stage(dve, G[f"ffn_down{h}"])

    def pe_final(pe):
        pe_norm(pe, final_norm)
        for c in range(4):
            for half in range(2):
                n_ = 2 * c + half
                if n_ >= 4:
                    pe.wait_ge(s("out_copied"), n_ - 3)
                if n_ < 2:
                    pe.wait_ge(s("out_scaled"), 4 * half + 4)
                for k in range(4):
                    last = nc.tensor.transpose(ps[4 + n_ % 4][:, k * P:k * P + P], fo[:, 4 * half + k, c * P:c * P + P], ident[:])
                last.then_inc(s("out_turned"), 1)

    def dve_final(dve):
        dve_norm(dve, final_norm)
        for t in range(ND):
            nc.vector.scalar_tensor_tensor(out=fo[:, t], in0=x[:, t], scalar=col(0, G_OUT + t), in1=rs[:],
                                           op0=ALU.mult, op1=ALU.mult).then_inc(s("out_scaled"), 1)

    def act_final(act):
        act_norm(act, final_norm)
        for n_ in range(8):
            act.wait_ge(s("out_turned"), n_ + 1)
            nc.scalar.activation(xtok[:, n_ // 2, n_ % 2 * T:n_ % 2 * T + T], ps[4 + n_ % 4][:], ACT.Copy).then_inc(s("out_copied"), 1)

    def sp_final(sp):
        o = out[0].rearrange("(c p) d -> p c d", p=P)
        for c in range(4):
            sp.wait_ge(s("out_copied"), 2 * c + 2)
            sp.dma_start(o[:, c], xtok[:, c]).then_inc(s("out_stored"), 16)
        sp.wait_ge(s("out_stored"), 64)

    block = ctx.enter_context(nc.Block())
    G = stages

    def pool_mlp(pool, n):
        for h in range(2):
            pool_stage(pool, G[f"{n}_up{h}"])
            pool_stage(pool, G[f"{n}_down{h}"])

    @block.sync
    def _(sp):
        sp_init(sp)
        for st in order:
            sp_stage(sp, st)
            if st.name == "l1_v":
                sp_b(sp)
            sp_extra(sp, st.name)
        sp_final(sp)

    @block.gpsimd
    def _(pool):
        pool_init(pool)
        for l in range(4):
            if l % 3 == 0:
                pool_a(pool, l)
            if l == 1:
                pool_stage(pool, G["l1_v"])
                pool_b(pool)
            pool_stage(pool, G[f"l{l}_out"])
            pool_mlp(pool, f"l{l}_mlp")
        pool_second(pool)

    @block.tensor
    def _(pe):
        pe_init(pe)
        for l in range(4):
            if l % 3 == 0:
                pe_stage(pe, G[f"l{l}_branch"])
                pe_stage(pe, G[f"l{l}_gate"])
                pe_a(pe, l)
            elif l == 1:
                pe_stage(pe, G["l1_v"])
                pe_stage(pe, G["l1_u"])
                pe_b(pe, G["l1_u"].norm)
            else:
                pe_stage(pe, G["l2_in"])
            pe_stage(pe, G[f"l{l}_out"])
            for h in range(2):
                pe_stage(pe, G[f"l{l}_mlp_up{h}"])
                pe_stage(pe, G[f"l{l}_mlp_down{h}"])
        pe_second(pe)
        pe_final(pe)

    @block.scalar
    def _(act):
        act_split(act, At(order[0], 0, 0, 0), 0)
        act_init(act)
        for l in range(4):
            if l % 3 == 0:
                act_stage(act, G[f"l{l}_branch"])
                act_stage(act, G[f"l{l}_gate"], ga, ACT.Gelu_apprx_tanh)
                act_a(act, l)
            elif l == 1:
                act_stage(act, G["l1_v"], vv, ACT.Gelu_apprx_tanh)
                act_stage(act, G["l1_u"], uu, ACT.Gelu_apprx_tanh)
                act_b(act, G["l1_u"].norm)
            else:
                act_stage(act, G["l2_in"], custom=act_conv3)
            act_stage(act, G[f"l{l}_out"])
            for h in range(2):
                act_stage(act, G[f"l{l}_mlp_up{h}"])
                act_stage(act, G[f"l{l}_mlp_down{h}"])
        act_second(act)
        act_final(act)

    @block.vector
    def _(dve):
        dve_split(dve, At(order[0], 0, 0, 0), 0)
        dve_init(dve)
        dve_softplus(dve)
        for l in range(4):
            if l % 3 == 0:
                dve_stage(dve, G[f"l{l}_branch"], custom=dve_conv4(l))
                dve_stage(dve, G[f"l{l}_gate"])
                dve_a(dve, l)
            elif l == 1:
                dve_stage(dve, G["l1_v"])
                dve_stage(dve, G["l1_u"])
                dve_b(dve, G["l1_u"].norm)
            else:
                dve_stage(dve, G["l2_in"], custom=dve_conv3)
            dve_stage(dve, G[f"l{l}_out"])
            for h in range(2):
                dve_stage(dve, G[f"l{l}_mlp_up{h}"])
                dve_stage(dve, G[f"l{l}_mlp_down{h}"])
        dve_second(dve)
        dve_final(dve)

    ctx.close()


_INS = [
    "x", "norm_mix_g", "norm_mlp_g", "final_norm_g", "a_w_in", "a_conv_w", "a_conv_b", "a_gate_a_w", "a_gate_a_b",
    "a_gate_x_w", "a_gate_x_b", "a_lambda", "a_w_out", "b_w_in", "b_norm_g", "b_w_s", "b_s_bias", "b_w_out",
    "c_w_in", "c_conv_w", "c_w_out", "mlp_w1", "mlp_w2", "mem_2", "norm_mix_g_2", "w_in_2", "shift_mu_2", "w0_2",
    "w2_2", "a0_2", "a2_2", "g2_2", "k_k_2", "k_a_2", "r_k_2", "gn_w_2", "gn_b_2", "p_rwkv_2", "p_attn_2", "w_out_2",
    "norm_x_g_2", "norm_mem_g_2", "xa_wq_2", "xa_wkv_2", "xa_wo_2", "norm_ffn_g_2", "ffn_w1_2", "ffn_w2_2",
    "norm_final_g_2",
]


def kernel(**inputs):
    import numpy as np
    import concourse.bacc as bacc
    from concourse.bass_utils import run_bass_kernel_spmd

    nc = bacc.Bacc("TRN2", target_bir_lowering=False, num_devices=1)
    arrays, aps = {}, {}
    for name in _INS:
        v = np.ascontiguousarray(inputs[name])
        arrays[f"in_{name}"] = v
        aps[name] = nc.dram_tensor(f"in_{name}", v.shape, mybir.dt.from_np(v.dtype), kind="ExternalInput").ap()
    out = nc.dram_tensor("out", (1, T, D), F32, kind="ExternalOutput").ap()
    build(nc, aps, out)
    r = run_bass_kernel_spmd(nc, [arrays], core_ids=[0])
    return r.results[0]["out"]
```

```python
import math
from contextlib import ExitStack

import concourse.bass as bass
from concourse import mybir

ALU = mybir.AluOpType
ACT = mybir.ActivationFunctionType
AX = mybir.AxisListType
F32 = mybir.dt.float32
F32R = mybir.dt.float32r

P = 128
T = 512
D = 1024
ND = D // P
FF = 4 * D
DRNN = 1280
NR = DRNN // P
HDA = 80
EPS = 1e-6
LOG_DECAY = math.exp(-0.5)
GN_EPS = 64 * 1e-5
CH = 64
NC = T // CH
NH2 = 8
MEM = 256
NEG = 1e30
KIB = 1024


BAND = [(i, o) for o in range(5) for i in range(o * P // HDA * HDA // P, -(-(-(-(o + 1) * P // HDA) * HDA) // P))]


class Stage:

    def __init__(self, name, w, groups, upg, kb, col, row0=0, rhs="x", kind="plain", period=None, swap=False,
                 n=T, only1=False, hook=False):
        self.name, self.w, self.groups, self.upg, self.kb, self.col, self.row0 = name, w, groups, upg, kb, col, row0
        self.rhs, self.kind, self.period, self.swap, self.n, self.only1, self.hook = rhs, kind, period, swap, n, only1, hook


class At:

    def __init__(self, st, i, c, half):
        self.j, self.st, self.c, self.i, self.half_i = i + c, st, c, i, half

    def unit(self, s):
        return self.i * self.st.upg + (self.st.u0 + self.c * self.st.upg + s)

    def slot(self, s):
        return (self.st.u0 + self.c * self.st.upg + s) % 2

    def turn(self, s):
        return self.half_i * self.st.upg + (self.st.u0 + self.c * self.st.upg + s) // 2

    def group(self):
        return self.i + (self.st.g0 + self.c)

    def pair(self):
        return (self.st.g0 + self.c) % 2


def run_groups(eng, st, body):
    c = 0
    if st.hook:
        body(At(st, 0, 0, 0), True)
        c = 1
    per = st.period or 2
    n = (st.groups - c) // per if st.loop else 0
    if n >= 2:
        with eng.Fori(0, n) as i:
            for s in range(per):
                body(At(st, i * per, c + s, i * (per // 2)), False)
        c += n * per
    while c < st.groups:
        body(At(st, 0, c, 0), False)
        c += 1


def build(nc, a, out):
    ctx = ExitStack()
    base = nc.sbuf_base
    PERS = (base + 63) // 32 * 32
    used = [PERS]

    def pers(name, shape, dt=F32):
        n = 4
        for s in shape[1:]:
            n *= s
        off = used[0]
        used[0] += (n + 31) // 32 * 32
        return nc.alloc_sbuf_tensor_at(name, shape, dt, offset=off)

    def sem(name):
        return ctx.enter_context(nc.semaphore(name))

    raw = pers("raw", [P, 2, 8, 256])
    WH_AT = used[0]
    wh = pers("wh", [P, 2, 8, 256], F32R)
    wl = pers("wl", [P, 2, 8, 256], F32R)
    x = pers("x", [P, ND, T])
    XH_AT = used[0]
    xh = pers("xh", [P, ND, T], F32R)
    xl = pers("xl", [P, ND, T], F32R)
    ident = pers("ident", [P, P])
    ones = pers("ones", [P, P])
    headones = pers("headones", [P, P])
    rs = pers("rs", [P, T])
    acc = pers("acc", [P, T])
    tmp = pers("tmp", [P, 2, T + 8])
    hf = pers("hf", [P, 2, T])
    sq = hf
    sd = hf
    prm = [pers(f"prm{i}", [P, P]) for i in range(4)]
    small = pers("small", [P, 64])
    c8 = pers("c8", [P, 2, 2 * NR])
    ARENA = used[0]
    LIMIT = nc.sbuf_top

    def at(name, kib, shape, dt=F32, base_at=None):
        n = 4
        for s in shape[1:]:
            n *= s
        off = (ARENA if base_at is None else base_at) + int(kib * KIB)
        assert base_at is not None or off + n <= LIMIT, (name, off + n, LIMIT)
        return nc.alloc_sbuf_tensor_at(name, shape, dt, offset=off)

    hh = at("hh", 0, [P, 16, T], F32R)
    hl = at("hl", 32, [P, 16, T], F32R)
    yh = at("yh", 40, [P, NR, T], F32R)
    yl = at("yl", 60, [P, NR, T], F32R)
    xtok = at("xtok", 0, [P, 4, D])
    rows = at("rows", 16, [P, 4, P])
    ga = at("ga", 0, [P, NR, T])
    xc = at("xc", 20, [P, NR, T])
    ra = at("ra", 40, [P, NR, T])
    ig = at("ig", 60, [P, NR, T])
    gw = at("gw", 80, [P, len(BAND), 2, P])
    th = ga
    xpad = at("xpad", 72, [P, 2, T + 8])
    vv = at("vv", 0, [P, ND, T])
    uu = at("uu", 16, [P, ND, T])
    wsT = at("wsT", 32, [P, 8, P])
    wsr = at("wsr", 36, [P, 8, P])
    vtok = at("vtok", 80, [P, 2, 4, P])
    sbrow = at("sbrow", 84, [1, 8 * P])
    gcs = at("gcs", 0, [P, 2, T])
    pc = at("pc", 4, [P, 2, T + 8])
    cv = at("cv", 9, [P, 2, T])

    qT = at("qT", 0, [P, 6, T])
    kT = at("kT", 12, [P, 6, T])
    vt = at("vt", 24, [P, 4, 768])
    dist = at("dist", 36, [P, 3, T])
    sc = at("sc", 42, [P, 2, 1280])
    pt = at("pt", 52, [P, 10, P])
    I32 = mybir.dt.int32
    disti = at("disti", 60, [P, T], I32)
    distm = at("distm", 62, [P, T], I32)
    distf = at("distf", 64, [P, T])
    d0 = at("d0", 66, [P, T])
    den = at("den", 59.5, [P, 4])
    rscol = at("rscol", 59, [P, 8])
    stat = at("stat", 59.25, [P, 4])
    ya = at("ya", 80, [P, 2, T])
    AR = at("AR", 0, [P, NC, NH2, 2, CH])
    BT = at("BT", 32, [P, NC, NH2, CH])
    KT = at("KT", 48, [P, NC, NH2, CH])
    VT = at("VT", 64, [P, NH2, T])
    gd = at("gd", 84, [P, 2, T])
    w2a2 = at("w2a2", 88, [P, D])
    wda = at("wda", 92, [P, T])
    PCt = at("PC", 94, [P, NC, NH2])
    XT_AT = XH_AT - 16 * KIB
    rt = at("rt", 0, [P, 8, T], base_at=XT_AT)
    ck = {n_: at("c" + n_, 2 * i_, [P, NH2, CH], base_at=XH_AT) for i_, n_ in enumerate(["X", "Z", "Yt", "W0", "U", "ST"])}
    Vt, Bt, Kt, TM = ([at(f"c{n_}{i_}", 2 * k_ + (12, 8)[i_], [P, NH2, CH], base_at=(XH_AT, XT_AT)[i_]) for i_ in range(2)]
                      for k_, n_ in enumerate(["Vt", "Bt", "Kt", "TM"]))
    TLB, TLK = ([at(f"{n_}{i_}", 4 * k_ + (20, 0)[i_], [P, NH2, 2, CH], base_at=(XH_AT, XT_AT)[i_]) for i_ in range(2)]
                for k_, n_ in enumerate(["TLB", "TLK"]))
    VS, BS, KS = (at(n_, 4 * i_, [P, NH2, P], base_at=WH_AT) for i_, n_ in enumerate(["VS", "BS", "KS"]))
    mk = at("mk", 28, [P, 8, CH], base_at=XH_AT)
    i64 = at("i64", 30.25, [P, CH], base_at=XH_AT)
    srci = at("srci", 30.5, [P, CH], mybir.dt.int32, base_at=XH_AT)
    tgti = at("tgti", 30.75, [P, CH], mybir.dt.int32, base_at=XH_AT)
    inta = at("inta", 31, [P, CH], mybir.dt.int32, base_at=XH_AT)
    intb = at("intb", 31.25, [P, CH], mybir.dt.int32, base_at=XH_AT)
    srcf = at("srcf", 31.5, [P, CH], base_at=XH_AT)
    tgtf = at("tgtf", 31.75, [P, CH], base_at=XH_AT)
    gl = at("gl", 0, [P, 16, T], base_at=XH_AT)
    mg = at("mg", 0, [P, ND, T])
    g2s = at("g2s", 0, [P, 2, D])
    gns = at("gns", 8, [P, 3, T])
    bon = at("bon", 14, [P, 2, T])
    qx = at("qx", 0, [P, ND, T])
    kx = at("kx", 16, [P, ND, MEM])
    vx = at("vx", 24, [P, 2, D])
    mh = at("mh", 32, [P, ND, MEM], F32R)
    ml = at("ml", 76, [P, ND, MEM], F32R)
    mtok = at("mtok", 40, [P, 2, D])
    msq = at("msq", 56, [P, 8])
    sx = at("sx", 84, [P, 4, MEM])
    ptx = at("ptx", 88, [P, 2, T])
    stx = at("stx", 92, [P, 16])
    mjunk = at("mjunk", 84, [P, D])
    fo = at("fo", 16, [P, ND, T])

    ps = [ctx.enter_context(nc.psum_tensor(f"ps{i}", [P, T], F32)) for i in range(8)]

    x_spill = nc.dram_tensor("x_spill", [P, ND, T], F32).ap()
    gate_spill = nc.dram_tensor("gate_spill", [16, P, T], F32).ap()
    bonus_spill = nc.dram_tensor("bonus_spill", [ND, P, T], F32).ap()

    landed = [sem("weights_landed_0"), sem("weights_landed_1")]
    upper = sem("weights_upper")
    lower = sem("weights_lower")
    units = sem("units_multiplied")
    evac = sem("tiles_evacuated")
    acted = sem("tiles_acted")
    pooled = sem("pool_done")
    squared = sem("squares_ready")
    split = sem("operands_split")
    ssum = sem("square_sums")
    rooted = sem("roots_ready")
    chain = sem("vector_chain")
    S = {}

    def s(name):
        if name not in S:
            S[name] = sem(name)
        return S[name]

    stages = {}
    order = []
    count = dict(u=0, g=0, a=0, q=0, t=0, n=0)

    def stage(name, *args, **kw):
        st = Stage(name, *args, **kw)
        st.u0, st.g0, st.a0, st.q0, st.t0, st.n0 = (count[k] for k in "ugaqtn")
        st.norm = (count["q"], count["n"] - 1)
        back = {"x": ND, "h": 16, "y": 5 * st.upg if st.upg == 2 else ND + 2 * (name == "merge"), "m": None}[st.rhs]
        st.need0 = count["t"] - back if (st.hook or st.rhs in "hy") and back else None
        st.s0 = 8 * count["n"]
        st.nosplit = name in ("l3_mlp_down1", "ffn_down1")
        st.loop = st.kind in ("relu", "resid", "fin", "gelu", "sigm", "scale", "gelusq")
        tiles = 2 * st.groups
        if st.nosplit:
            st.kind = "last"
        count["u"] += st.groups * st.upg
        count["g"] += st.groups
        count["a"] += {"relu": tiles, "fin": tiles, "gelu": tiles, "gelusq": tiles, "sigm": tiles, "spill": tiles, "y": tiles}.get(st.kind, 0) + kw.get("extra_a", 0)
        count["q"] += {"relu": tiles, "fin": tiles + 1, "last": tiles + 1, "gelusq": tiles + 1}.get(st.kind, 0)
        count["t"] += {"relu": tiles, "fin": tiles}.get(st.kind, 0)
        count["n"] += {"fin": 1, "last": 1, "gelusq": 1}.get(st.kind, 0)
        if st.nosplit:
            st.kind = "fin"
        stages[name] = st
        order.append(st)
        return st

    def tiles_split(name, n):
        stages[name] = (count["t"], count["a"])
        count["t"] += n
        count["a"] += n

    lin = lambda c0: (lambda j: j * 256 + c0)

    def norm_from_pool(name):
        stages[name] = (count["q"], count["n"], count["a"], count["t"])
        count["q"] += ND + 1
        count["n"] += 1
        count["a"] += ND
        count["t"] += ND

    norm_from_pool("init")
    G_MIX, G_MLP, G_FIN, G_B, G_MIX2, G_X, G_MEM, G_FFN, G_FIN2 = 0, 32, 64, 72, 80, 88, 96, 104, 112
    gain = lambda c: (0, c)

    def mlp(name, w1, w2, g):
        for h in range(2):
            stage(f"{name}_up{h}", w1, 8, 1, 8, lin(h * 2048), kind="relu", hook=h == 0)
            stage(f"{name}_down{h}", w2, 4, 2, 8, lin(0), row0=h * 16, rhs="h", kind="fin" if h else "resid")
            stages[f"{name}_down{h}"].gain = g

    for l in range(4):
        kind, j = l % 3, l // 3
        if kind == 0:
            w = a["a_w_in"][j]
            stage(f"l{l}_branch", w, 5, 1, 8, lin(DRNN), kind="conv4", hook=True)
            stage(f"l{l}_gate", w, 5, 1, 8, lin(0), kind="agate")
            tiles_split(f"l{l}_mix", NR)
            stage(f"l{l}_out", a["a_w_out"][j], 4, 2, 5, lin(0), rhs="y", kind="fin")
        elif kind == 1:
            stage(f"l{l}_v", a["b_w_in"][0], 4, 1, 8, lin(D), kind="gelusq", hook=True)
            stage(f"l{l}_u", a["b_w_in"][0], 4, 1, 8, lin(0), kind="gelu")
            tiles_split(f"l{l}_mix", ND)
            stage(f"l{l}_out", a["b_w_out"][0], 4, 1, 8, lin(0), rhs="y", kind="fin")
        else:
            stage(f"l{l}_in", a["c_w_in"][0], 12, 1, 8, lambda j: [1, 2, 0][j % 3] * D + j // 3 * 256, kind="conv3", hook=True)
            tiles_split(f"l{l}_mix", ND)
            stage(f"l{l}_out", a["c_w_out"][0], 4, 1, 8, lin(0), rhs="y", kind="fin")
        stages[f"l{l}_out"].gain = G_MLP + 8 * l
        mlp(f"l{l}_mlp", a["mlp_w1"][l], a["mlp_w2"][l], G_MIX + 8 * (l + 1) if l < 3 else None)
        if l == 3:
            stages["l3_mlp_down1"].gain = G_FIN
    norm_from_pool("mid")
    w2nd = a["w_in_2"][0]
    Q0 = 3 * D + 288
    stage("q", w2nd, 3, 1, 8, lin(Q0), kind="scale", hook=True)
    stage("k", w2nd, 3, 1, 8, lin(Q0 + 768), kind="scale")
    stage("v", w2nd, 3, 1, 8, lin(Q0 + 1536), kind="tok", swap=True)
    stage("lora", w2nd, 2, 1, 8, lambda j: [3 * D, 3 * D + 32][j], kind="lora")
    stage("rkv", w2nd, 12, 1, 8, lambda j: j % 3 * D + j // 3 * 256, kind="rkv")
    stage("gates", w2nd, 8, 1, 8, lin(Q0 + 2304), kind="spill")
    tiles_split("ysplit", ND + 2)
    stage("merge", None, 8, 1, None, lin(0), rhs="y", kind="merge")
    tiles_split("msplit", ND)
    stage("out2", a["w_out_2"][0], 4, 1, 8, lin(0), rhs="y", kind="fin").gain = G_X
    stage("wq", a["xa_wq_2"][0], 4, 1, 8, lin(0), kind="scale", hook=True)
    stage("memk", a["xa_wkv_2"][0], 4, 1, 8, lin(0), rhs="m", kind="memk", n=MEM)
    stage("memv", a["xa_wkv_2"][0], 4, 1, 8, lin(D), rhs="m", kind="memv", swap=True)
    tiles_split("xsplit", ND)
    stage("xo", a["xa_wo_2"][0], 4, 1, 8, lin(0), rhs="y", kind="fin").gain = G_FFN
    mlp("ffn", a["ffn_w1_2"][0], a["ffn_w2_2"][0], G_FIN2)
    U_TOTAL = count["u"]
    final_norm, G_OUT = (count["q"], count["n"] - 1), G_FIN2
    order[-1].loop = False

    def weights(st, j, su):
        if st.kind == "merge":
            return (a["p_rwkv_2"][0], 0, 8, j // 2 * 256) if j % 2 == 0 else (a["p_attn_2"][0], 0, 2, j // 2 * 256)
        return st.w, st.row0 + su * st.kb, st.kb, st.col(j)

    srcs = {"x": (xh, xl), "h": (hh, hl), "y": (yh, yl), "m": (mh, ml)}


    def sp_stage(sp, st):
        def body(p, first):
            for su in range(st.upg):
                w, r, kb, c = weights(st, p.j, su)
                src = w.rearrange("(k p) n -> p k n", p=P)[:, r:r + kb, bass.ds(c, 256)]
                sp.wait_ge(lower, p.unit(su) + 1)
                sp.dma_start(raw[:, p.slot(su), 0:kb], src).then_inc(landed[p.slot(su)], 16)
        run_groups(sp, st, body)

    def act_split(act, p, su):
        act.wait_ge(landed[p.slot(su)], p.turn(su) * 16 + 16)
        act.wait_ge(units, p.unit(su) + 1)
        nc.scalar.activation(wh[:, p.slot(su)], raw[:, p.slot(su)], ACT.Copy).then_inc(upper, 1)

    def dve_split(dve, p, su):
        dve.wait_ge(upper, p.unit(su) + 1)
        nc.vector.tensor_tensor(wl[:, p.slot(su)], raw[:, p.slot(su)], wh[:, p.slot(su)],
                                ALU.subtract).then_inc(lower, 1)

    def split_next(fn, eng, p, st):
        for su in range(st.upg):
            if st is order[-1] and p.c == st.groups - 1 and su == st.upg - 1:
                return
            if st.name == "gates" and p.c == st.groups - 1:
                return
            fn(eng, p, su + 1)

    def pe_stage(pe, st):
        ops = srcs[st.rhs]
        need = (lambda k: st.need0 + k + 1) if st.need0 is not None else None

        def body(p, first):
            banks = [ps[2 * p.pair()], ps[2 * p.pair() + 1]]
            pe.wait_ge(evac, p.group() * 2 + 2)
            for su in range(st.upg):
                slot = p.slot(su)
                kb = st.kb if st.kind != "merge" else (8, 2)[p.c % 2]
                pe.wait_ge(lower, p.unit(su) + 3)
                k0 = su * kb
                terms = ((wh, 0), (wh, 1), (wl, 0))
                if st.swap:
                    nt = 4 if st.rhs == "x" else 2
                    for tt in range(nt):
                        bank = banks[tt // (nt // 2)]
                        o = bank[:, tt % (nt // 2) * 256:tt % (nt // 2) * 256 + 256]
                        for k in range(kb):
                            if need and tt == 0 and p.c == 0:
                                pe.wait_ge(split, need(k))
                            for n_, (wt, oi) in enumerate(terms):
                                last = nc.tensor.matmul(o, ops[oi][:, k, tt * P:tt * P + P], wt[:, slot, k],
                                                        start=k == 0 and n_ == 0, stop=k == kb - 1 and n_ == 2)
                    last.then_inc(units, 1)
                    continue
                mts = (1,) if st.kind == "lora" and p.c == 1 else (0, 1)
                for k in range(kb):
                    kk = k0 + k
                    if st.kind == "merge" and p.c % 2:
                        kk = ND + k
                    if need and (p.c < 1 or st.kind == "merge"):
                        pe.wait_ge(split, need(kk))
                    for mt in mts:
                        for n_, (wt, oi) in enumerate(terms):
                            last = nc.tensor.matmul(banks[mt][:, 0:st.n], wt[:, slot, k, mt * P:mt * P + P],
                                                    ops[oi][:, kk, 0:st.n],
                                                    start=k == 0 and su == 0 and n_ == 0,
                                                    stop=k == kb - 1 and su == st.upg - 1 and n_ == 2)
                last.then_inc(units, 1)
            if first:
                pe_norm(pe, st.norm)
            if st.kind == "rkv":
                pe_pairs(pe, p.c)
            if st.kind == "spill" and p.c < 2:
                pe_pairs(pe, 12 + p.c)
        run_groups(pe, st, body)

    def pe_norm(pe, n):
        pe.wait_ge(pooled, n[0])
        nc.tensor.matmul(ps[4][:], ones[:], acc[:], start=True, stop=True).then_inc(ssum, 1)

    def act_norm(act, n):
        act.wait_ge(ssum, n[1] + 1)
        nc.scalar.activation(sd[:, 0], ps[4][:], ACT.Sqrt, scale=1.0 / D, bias=small[:, 0:1]).then_inc(rooted, 1)

    def dve_norm(dve, n):
        dve.wait_ge(rooted, n[1] + 1)
        link(nc.vector.reciprocal(rs[:], sd[:, 0]))

    links = [0]

    def link(ins):
        links[0] += 1
        ins.then_inc(chain, 1)
        nc.vector.wait_ge(chain, links[0])

    def col(k, c):
        return prm[k][:, c:c + 1]

    def gaincol(st, t):
        return prm[0][:, bass.ds(t + st.gain, 1)]

    def act_stage(act, st, dest=None, fn=None, custom=None):
        def body(p, first):
            split_next(act_split, act, p, st)
            if first:
                act_norm(act, st.norm)
            if custom:
                custom(p)
            for mt in range(2):
                t = p.j * 2 + mt
                if custom or st.kind in ("scale", "resid", "conv4", "tok", "memk", "memv"):
                    continue
                act.wait_ge(evac, p.group() * 2 + 5 + mt)
                if st.kind in ("fin", "gelusq"):
                    act.wait_ge(pooled, p.i * 2 + (st.q0 + 2 * p.c + mt))
                act.wait_ge(evac, 1)
                if st.kind == "relu":
                    nc.scalar.activation(hh[:, bass.ds(t, 1)], tmp[:, mt:mt + 1, 0:T], ACT.Square).then_inc(acted, 1)
                elif st.kind == "fin":
                    if not st.nosplit:
                        nc.scalar.activation(xh[:, bass.ds(t, 1)], x[:, bass.ds(t, 1)], ACT.Copy,
                                             scale=gaincol(st, t)).then_inc(acted, 1)
                    nc.scalar.activation(sq[:, mt:mt + 1], x[:, bass.ds(t, 1)], ACT.Square).then_inc(squared, 1)
                elif st.kind == "gelusq":
                    nc.scalar.activation(dest[:, bass.ds(t, 1)], tmp[:, mt:mt + 1, 0:T], fn).then_inc(acted, 1)
                    act.wait_ge(acted, p.i * 2 + (st.a0 + 2 * p.c + mt + 3))
                    nc.scalar.activation(sq[:, mt:mt + 1], dest[:, bass.ds(t, 1)], ACT.Square).then_inc(squared, 1)
                elif st.kind in ("gelu", "sigm"):
                    nc.scalar.activation(dest[:, bass.ds(t, 1)], tmp[:, mt:mt + 1, 0:T], fn).then_inc(acted, 1)
        run_groups(act, st, body)

    def pool_stage(pool, st):
        if st.kind not in ("relu", "fin", "gelusq"):
            return
        if st.kind in ("fin", "gelusq"):
            pool_norm_start(pool, st.n0)

        def body(p, first):
            for mt in range(2):
                if st.kind == "relu":
                    pool.wait_ge(evac, p.group() * 2 + 5 + mt)
                    nc.gpsimd.tensor_tensor(hf[:, mt], tmp[:, mt, 0:T], tmp[:, mt, 0:T], ALU.mult).then_inc(pooled, 1)
                else:
                    pool.wait_ge(squared, p.i * 2 + (st.s0 + 2 * p.c + mt + 1))
                    pool.wait_ge(pooled, p.i * 2 + (st.q0 + 2 * p.c + mt + 1))
                    nc.gpsimd.tensor_tensor(acc[:], acc[:], sq[:, mt], ALU.add).then_inc(pooled, 1)
        run_groups(pool, st, body)

    def pool_norm_start(pool, n):
        if n:
            pool.wait_ge(ssum, n)
        nc.gpsimd.memset(acc[:], 0.0).then_inc(pooled, 1)

    def dve_stage(dve, st, dest=None, custom=None):
        def body(p, first):
            split_next(dve_split, dve, p, st)
            if first:
                dve_norm(dve, st.norm)
            dve.wait_ge(units, p.unit(st.upg - 1) + 3)
            b = 2 * p.pair()
            t0 = p.j * 2
            if custom:
                custom(p, b)
            elif st.kind == "relu":
                for mt in range(2):
                    nc.vector.scalar_tensor_tensor(out=tmp[:, mt, 0:T], in0=ps[b + mt][:], scalar=0.0, in1=rs[:],
                                                   op0=ALU.max, op1=ALU.mult).then_inc(evac, 1)
                for mt in range(2):
                    dve.wait_ge(acted, p.i * 2 + (st.a0 + 2 * p.c + mt + 3))
                    dve.wait_ge(pooled, p.i * 2 + (st.q0 + 2 * p.c + mt + 1))
                    t = t0 + mt
                    nc.vector.tensor_tensor(hl[:, bass.ds(t, 1)], hf[:, mt:mt + 1], hh[:, bass.ds(t, 1)],
                                            ALU.subtract).then_inc(split, 1)
            elif st.kind in ("resid", "fin"):
                for mt in range(2):
                    xt = x[:, bass.ds(t0 + mt, 1)]
                    nc.vector.tensor_tensor(xt, xt, ps[b + mt][:].rearrange("p (a n) -> p a n", a=1),
                                            ALU.add).then_inc(evac, 1)
                if st.kind == "fin" and not st.nosplit:
                    for mt in range(2):
                        t = t0 + mt
                        dve.wait_ge(acted, p.i * 2 + (st.a0 + 2 * p.c + mt + 3))
                        nc.vector.scalar_tensor_tensor(out=xl[:, bass.ds(t, 1)], in0=x[:, bass.ds(t, 1)],
                                                       scalar=gaincol(st, t), in1=xh[:, bass.ds(t, 1)],
                                                       op0=ALU.mult, op1=ALU.subtract).then_inc(split, 1)
            elif st.kind in ("gelu", "sigm", "gelusq", "spill"):
                for mt in range(2):
                    dve.wait_ge(acted, p.i * 2 + (st.a0 + 2 * p.c + mt + 1))
                    nc.vector.tensor_tensor(tmp[:, mt, 0:T], ps[b + mt][:], rs[:], ALU.mult).then_inc(evac, 1)
            elif st.kind == "scale":
                for mt in range(2):
                    nc.vector.tensor_tensor(dest[:, bass.ds(t0 + mt, 1)],
                                            ps[b + mt][:].rearrange("p (a n) -> p a n", a=1),
                                            rs[:].rearrange("p (a n) -> p a n", a=1), ALU.mult).then_inc(evac, 1)
        run_groups(dve, st, body)


    prm_rows = [
        [(a["norm_mix_g"], 32), (a["norm_mlp_g"], 32), (a["final_norm_g"], 8), (a["b_norm_g"], 8), (a["norm_mix_g_2"], 8),
         (a["norm_x_g_2"], 8), (a["norm_mem_g_2"], 8), (a["norm_ffn_g_2"], 8), (a["norm_final_g_2"], 8)],
        [(a["a_conv_w"], 80), (a["a_conv_b"], 20)],
        [(a["a_gate_a_b"], 20), (a["a_gate_x_b"], 20), (a["a_lambda"], 20), (a["c_conv_w"], 24), (a["w0_2"], 8), (a["a0_2"], 8),
         (a["k_k_2"], 8), (a["k_a_2"], 8)],
        [(a["r_k_2"], 8), (a["gn_w_2"], 8), (a["gn_b_2"], 8), (a["shift_mu_2"][0, 0:26 * P], 26),
         (a["shift_mu_2"][0, 25 * P + 32:26 * P + 32], 1)],
    ]
    CONVW, CONVB = 0, 80
    GAB, GXB, LAM, CCONV, W0C, A0C, KKC, KAC = 0, 20, 40, 60, 84, 92, 100, 108
    RKC, GNW, GNB, MU = 0, 8, 16, 24
    n_rows = [sum(n for _, n in r) for r in prm_rows]

    def flat(ap):
        n = len(ap.shape)
        if n == 1:
            return ap
        names_ = " ".join("abcd"[:n])
        return ap.rearrange(f"{names_} -> ({names_})")

    def sp_init(sp):
        sp.dma_start(xtok[:], a["x"][0].rearrange("(c p) d -> p c d", p=P)).then_inc(s("x_landed"), 16)
        for i, r in enumerate(prm_rows):
            at_ = 0
            for v, n in r:
                sp.dma_start(rows[at_:at_ + n, i, :], flat(v).rearrange("(r p) -> r p", p=P)).then_inc(s("rows_landed"), 16)
                at_ += n

    N_ROW_DMAS = sum(len(r) for r in prm_rows)

    def pool_init(pool):
        pool.sem_inc(lower, 2)
        pool.sem_inc(units, 2)
        pool.sem_inc(evac, 4)
        pool.sem_inc(acted, 2)
        made = s("constants_made")
        nc.gpsimd.memset(ident[:], 0.0).then_inc(made, 1)
        nc.gpsimd.memset(ones[:], 1.0).then_inc(made, 1)
        nc.gpsimd.memset(headones[:], 0.0).then_inc(made, 1)
        nc.gpsimd.memset(small[:, 0:1], EPS).then_inc(made, 1)
        nc.gpsimd.memset(small[:, 1:2], GN_EPS).then_inc(made, 1)
        pool.wait_ge(made, 5)
        nc.gpsimd.affine_select(out=ident[:], in_=ident[:], compare_op=ALU.not_equal, fill=1.0, base=0,
                                pattern=[[-1, P]], channel_multiplier=1).then_inc(made, 1)
        pool.wait_ge(made, 6)
        nc.gpsimd.memset(headones[0:64, 0:64], 1.0).then_inc(made, 1)
        pool.wait_ge(made, 7)
        nc.gpsimd.memset(headones[64:P, 64:P], 1.0).then_inc(made, 1)
        pool.wait_ge(made, 8)
        pool_squares(pool, stages["init"])

    def pool_squares(pool, norm):
        q0, n = norm[0], norm[1]
        pool_norm_start(pool, n)
        for t in range(ND):
            pool.wait_ge(squared, 8 * n + t + 1)
            pool.wait_ge(pooled, q0 + t + 1)
            nc.gpsimd.tensor_tensor(acc[:], acc[:], sq[:, t % 2], ALU.add).then_inc(pooled, 1)

    def pe_init(pe):
        pe.wait_ge(s("constants_made"), 8)
        pe.wait_ge(s("rows_landed"), 16 * N_ROW_DMAS)
        for i in range(4):
            last = nc.tensor.transpose(ps[7][:, i * P:i * P + n_rows[i]], rows[0:n_rows[i], i, :],
                                       ident[0:n_rows[i], 0:n_rows[i]])
        last.then_inc(s("rows_turned"), 1)
        pe.wait_ge(s("x_landed"), 16)
        for t in range(ND):
            if t >= 3:
                pe.wait_ge(s("x_set"), t - 2)
            for c in range(4):
                last = nc.tensor.transpose(ps[4 + t % 3][:, c * P:c * P + P], xtok[:, c, t * P:t * P + P], ident[:])
            last.then_inc(s("x_turned"), 1)

    def act_resplit(act, norm, g, first):
        q0, n, a0, _ = norm
        for t in range(ND):
            act.wait_ge(s("x_set"), first + t + 1)
            nc.scalar.activation(xh[:, t], x[:, t], ACT.Copy, scale=col(0, g + t)).then_inc(acted, 1)
            if q0 + t > 0:
                act.wait_ge(pooled, q0 + t)
            nc.scalar.activation(sq[:, t % 2], x[:, t], ACT.Square).then_inc(squared, 1)

    def dve_lower(dve, norm, g, t):
        dve.wait_ge(acted, norm[2] + t + 3)
        nc.vector.scalar_tensor_tensor(out=xl[:, t], in0=x[:, t], scalar=col(0, g + t), in1=xh[:, t],
                                       op0=ALU.mult, op1=ALU.subtract).then_inc(split, 1)

    def dve_init(dve):
        dve.wait_ge(s("rows_turned"), 1)
        for i in range(4):
            nc.vector.tensor_copy(prm[i][:, 0:n_rows[i]], ps[7][:, i * P:i * P + n_rows[i]]).then_inc(s("prm_ready"), 1)
        dve.wait_ge(s("prm_ready"), 4)
        for t in range(ND):
            dve.wait_ge(s("x_turned"), t + 1)
            nc.vector.tensor_copy(x[:, t], ps[4 + t % 3][:]).then_inc(s("x_set"), 1)
            if t:
                dve_lower(dve, stages["init"], G_MIX, t - 1)
        dve_lower(dve, stages["init"], G_MIX, ND - 1)

    def act_init(act):
        act.wait_ge(s("prm_ready"), 4)
        act_resplit(act, stages["init"], G_MIX, 0)
        act.wait_ge(s("lambda_abs"), 1)
        nc.scalar.activation(small[:, 24:44], small[:, 4:24], ACT.Exp, scale=-1.0).then_inc(s("lambda_exp"), 1)

    def dve_softplus(dve):
        lam = prm[2][:, LAM:LAM + 20]
        lab, e, z, z2, q = (small[:, 4:24], small[:, 24:44], small[:, 44:64], c8[:, 0], c8[:, 1])
        link(nc.vector.tensor_scalar(z, lam, -1.0, None, ALU.mult))
        link(nc.vector.tensor_tensor(lab, lam, z, ALU.max))
        nc.vector.tensor_copy(lab, lab).then_inc(s("lambda_abs"), 1)
        dve.wait_ge(s("lambda_exp"), 1)
        link(nc.vector.tensor_scalar(z, e, 2.0, None, ALU.add))
        link(nc.vector.reciprocal(z, z))
        link(nc.vector.tensor_tensor(z, z, e, ALU.mult))
        link(nc.vector.tensor_tensor(z2, z, z, ALU.mult))
        link(nc.vector.tensor_scalar(q, z2, 1.0 / 21, 1.0 / 19, ALU.mult, ALU.add))
        for k in range(17, 0, -2):
            link(nc.vector.tensor_tensor(q, q, z2, ALU.mult))
            link(nc.vector.tensor_scalar(q, q, 1.0 / k, None, ALU.add))
        link(nc.vector.tensor_tensor(q, q, z, ALU.mult))
        link(nc.vector.tensor_scalar(z, lam, -1.0, 0.0, ALU.mult, ALU.max))
        link(nc.vector.scalar_tensor_tensor(out=q, in0=q, scalar=2.0, in1=z, op0=ALU.mult, op1=ALU.add))
        link(nc.vector.tensor_scalar(z2, q, -8.0, None, ALU.mult))
        link(nc.vector.tensor_scalar(q, q, 8.0, None, ALU.mult))
        nc.vector.tensor_copy(small[:, 4:5], q[:, 0:1]).then_inc(s("c8_ready"), 1)

    alinks = [0]

    def alink(ins):
        alinks[0] += 1
        ins.then_inc(s("scalar_chain"), 1)
        nc.scalar.wait_ge(s("scalar_chain"), alinks[0])

    plinks = [0]

    def plink(ins):
        plinks[0] += 1
        ins.then_inc(s("pool_chain"), 1)
        nc.gpsimd.wait_ge(s("pool_chain"), plinks[0])

    def act_upper(act, name, t, f, src=None, to=None):
        act.wait_ge(s(name + "_y"), src if src is not None else t + 1)
        nc.scalar.activation((yh if to is None else to)[:, t], f, ACT.Copy).then_inc(acted, 1)

    def dve_lower_y(dve, name, t, f):
        dve.wait_ge(acted, stages[name][1] + t + 3)
        nc.vector.tensor_tensor(yl[:, t], f, yh[:, t], ALU.subtract).then_inc(split, 1)

    def pool_a(pool, l):
        n = f"l{l}"
        for grp in range(2):
            for o in range(5):
                if grp:
                    pool.wait_ge(s(n + "_band"), o + 1)
                mine = [b for b, (_, oo) in enumerate(BAND) if oo == o]
                bs = slice(mine[0], mine[-1] + 1)
                pool.dma_start(gw[:, bs], a["gate_band"][l // 3, grp, :, bs]).then_inc(s(f"gates_landed{o}"), 16)
        for t in range(NR):
            pool.wait_ge(s(n + "_gates"), 2 * t + 2)
            nc.gpsimd.tensor_tensor(ig[:, t], ig[:, t], xc[:, t], ALU.mult).then_inc(s(n + "_gated"), 1)

    def dve_conv4(l):
        n, j = f"l{l}", l // 3

        def custom(p, b):
            if p.c == 0:
                for mt in range(2):
                    link(nc.vector.memset(xpad[:, mt, 0:3], 0.0))
            for mt in range(2):
                t = 2 * p.j + mt
                w = lambda k: col(1, CONVW + (j * 4 + k) * NR + t)
                nc.vector.tensor_tensor(xpad[:, mt, 3:3 + T], ps[b + mt][:], rs[:], ALU.mult).then_inc(evac, 1)
                nc.vector.wait_ge(evac, p.group() * 2 + 5 + mt)
                link(nc.vector.tensor_scalar(xc[:, t], xpad[:, mt, 3:3 + T], w(3), col(1, CONVB + j * NR + t), ALU.mult, ALU.add))
                for k in (2, 1):
                    link(nc.vector.scalar_tensor_tensor(out=xc[:, t], in0=xpad[:, mt, k:k + T], scalar=w(k), in1=xc[:, t],
                                                        op0=ALU.mult, op1=ALU.add))
                nc.vector.scalar_tensor_tensor(out=xc[:, t], in0=xpad[:, mt, 0:T], scalar=w(0), in1=xc[:, t],
                                               op0=ALU.mult, op1=ALU.add).then_inc(s(n + "_xc"), 1)
                nc.vector.wait_ge(s(n + "_xc"), t + 1)
        return custom

    def pe_a(pe, l):
        n = f"l{l}"
        for t in range(NR):
            grp, o = t // 5, t % 5
            pe.wait_ge(s(f"gates_landed{o}"), 16 * (2 * (l // 3) + grp + 1))
            pe.wait_ge(s(n + "_xc"), 5 * grp + 5)
            if t >= 2:
                pe.wait_ge(s(n + "_gates"), 2 * (t - 1))
            mine = [(b, i) for b, (i, oo) in enumerate(BAND) if oo == o]
            for g in range(2):
                for m, (b, i) in enumerate(mine):
                    last = nc.tensor.matmul(ps[4 + 2 * (t % 2) + g][:], gw[:, b, g], xc[:, 5 * grp + i],
                                            start=m == 0, stop=m == len(mine) - 1)
            last.then_inc(s(n + "_band"), 1)

    def act_a(act, l):
        n, j = f"l{l}", l // 3
        for t0 in range(0, NR, 2):
            for t in (t0, t0 + 1):
                act.wait_ge(s(n + "_band"), t + 1)
                b = 4 + 2 * (t % 2)
                nc.scalar.activation(ra[:, t], ps[b][:], ACT.Sigmoid, bias=col(2, GAB + j * NR + t)).then_inc(s(n + "_gates"), 1)
                nc.scalar.activation(ig[:, t], ps[b + 1][:], ACT.Sigmoid, bias=col(2, GXB + j * NR + t)).then_inc(s(n + "_gates"), 1)
            if t0 == 0:
                act.wait_ge(s("c8_ready"), 1)
            for t in (t0, t0 + 1):
                act.wait_ge(s(n + "_gates"), 2 * t + 2)
                k = j * NR + t
                alink(nc.scalar.activation(th[:, t], ra[:, t], ACT.Tanh, scale=c8[:, 1, k:k + 1]))
                nc.scalar.activation(ra[:, t], ra[:, t], ACT.Exp, scale=c8[:, 0, k:k + 1]).then_inc(s(n + "_exp"), 1)
        for t in range(NR):
            act.wait_ge(s(n + "_var"), t + 1)
            nc.scalar.activation(th[:, t], th[:, t], ACT.Sqrt).then_inc(s(n + "_root"), 1)

    def dve_a(dve, l):
        n = f"l{l}"
        for t in range(NR):
            dve.wait_ge(s(n + "_exp"), t + 1)
            link(nc.vector.tensor_tensor(tmp[:, t % 2, 0:T], ra[:, t], ra[:, t], ALU.mult))
            nc.vector.scalar_tensor_tensor(out=th[:, t], in0=tmp[:, t % 2, 0:T], scalar=1.0, in1=th[:, t],
                                           op0=ALU.add, op1=ALU.mult).then_inc(s(n + "_var"), 1)
        for t in range(NR):
            dve.wait_ge(s(n + "_root"), t + 1)
            dve.wait_ge(s(n + "_gated"), t + 1)
            nc.vector.tensor_tensor(ig[:, t], th[:, t], ig[:, t], ALU.mult).then_inc(s(n + "_u"), 1)

    def act_gate(l):
        n = f"l{l}"

        def custom(p):
            for mt in range(2):
                t = 2 * p.j + mt
                nc.scalar.wait_ge(evac, p.group() * 2 + 5 + mt)
                nc.scalar.activation(ga[:, t], tmp[:, mt, 0:T], ACT.Gelu_apprx_tanh).then_inc(s(n + "_gelu"), 1)
            for t in range(2 * p.j - 2, 2 * p.j):
                if t >= 0:
                    act_upper(nc.scalar, n, t, ga[:, t])
            if p.j == 4:
                for t in (8, 9):
                    act_upper(nc.scalar, n, t, ga[:, t])
        return custom

    def dve_gate(l):
        n = f"l{l}"

        def outputs(ts):
            for t in ts:
                nc.vector.wait_ge(s(n + "_gelu"), t + 1)
                nc.vector.wait_ge(s(n + "_h"), t + 1)
                nc.vector.tensor_tensor(ga[:, t], xc[:, t], ga[:, t], ALU.mult).then_inc(s(n + "_y"), 1)

        def lowers(ts):
            for t in ts:
                dve_lower_y(nc.vector, n + "_mix", t, ga[:, t])

        def custom(p, b):
            j = p.j
            for mt in range(2):
                if j:
                    nc.vector.wait_ge(s(n + "_gelu"), 2 * j - 1 + mt)
                nc.vector.tensor_tensor(tmp[:, mt, 0:T], ps[b + mt][:], rs[:], ALU.mult).then_inc(evac, 1)
            if j:
                outputs((2 * j - 2, 2 * j - 1))
            for t in (2 * j, 2 * j + 1):
                nc.vector.wait_ge(s(n + "_u"), t + 1)
                nc.vector.tensor_tensor_scan(xc[:, t], ra[:, t], ig[:, t], 0.0, ALU.mult, ALU.add).then_inc(s(n + "_h"), 1)
            if j:
                lowers((2 * j - 2, 2 * j - 1))
            if j == 4:
                outputs((8, 9))
                lowers((8, 9))
        return custom

    def sp_b(sp):
        sp.dma_start(wsr[:], a["b_w_s"][0].rearrange("g t s -> t g s")).then_inc(s("ws_landed"), 16)
        sp.dma_start(sbrow[:], a["b_s_bias"][0].rearrange("(a g) t -> a (g t)", a=1)).then_inc(s("sb_landed"), 16)

    def pool_b(pool):
        pool.wait_ge(s("ws_landed"), 16)
        nc.gpsimd.affine_select(out=wsr[:], in_=wsr[:], compare_op=ALU.is_ge, fill=0.0, base=0,
                                pattern=[[0, 8], [-1, P]], channel_multiplier=1).then_inc(s("ws_masked"), 1)

    def pe_b(pe, norm):
        pe.wait_ge(s("ws_masked"), 1)
        for g in range(8):
            last = nc.tensor.transpose(ps[5 + g // 4][:, g % 4 * P:g % 4 * P + P], wsr[:, g], ident[:])
        last.then_inc(s("ws_turned"), 1)
        pe_norm(pe, norm)
        pe.wait_ge(s("sb_landed"), 16)
        pe.wait_ge(s("wsT_ready"), 2)
        for g in range(8):
            pe.wait_ge(s("v_normed"), g + 1)
            if g >= 2:
                pe.wait_ge(s("vtok_ready"), g - 1)
            for c in range(4):
                last = nc.tensor.transpose(ps[4 + g % 2][:, c * P:c * P + P], vv[:, g, c * P:c * P + P], ident[:])
            last.then_inc(s("v_turned"), 1)
            pe.wait_ge(s("vtok_ready"), g + 1)
            if g >= 2:
                pe.wait_ge(s("l1_y"), g - 1)
            for c in range(4):
                o = ps[6 + g % 2][:, c * P:c * P + P]
                nc.tensor.matmul(o, ones[0:1, :], sbrow[0:1, g * P:g * P + P], start=True, stop=False)
                last = nc.tensor.matmul(o, vtok[:, g % 2, c], wsT[:, g], start=False, stop=True)
            last.then_inc(s("mixed"), 1)

    def act_b(act, norm):
        act_norm(act, norm)
        for g in range(8):
            act.wait_ge(s("v_turned"), g + 1)
            if g >= 2:
                act.wait_ge(s("mixed"), g - 1)
            nc.scalar.activation(vtok[:, g % 2], ps[4 + g % 2][:].rearrange("p (c n) -> p c n", c=4), ACT.Copy)\
                .then_inc(s("vtok_ready"), 1)
            if g:
                act_upper(act, "l1", g - 1, uu[:, g - 1])
        act_upper(act, "l1", 7, uu[:, 7])

    def dve_b(dve, norm):
        dve.wait_ge(s("ws_turned"), 1)
        for h in range(2):
            nc.vector.tensor_copy(wsT[:, 4 * h:4 * h + 4], ps[5 + h][:].rearrange("p (c n) -> p c n", c=4))\
                .then_inc(s("wsT_ready"), 1)
        dve_norm(dve, norm)
        dve.wait_ge(acted, stages["l1_u"].a0 + 10)
        for g in range(8):
            nc.vector.scalar_tensor_tensor(out=vv[:, g], in0=vv[:, g], scalar=col(0, G_B + g), in1=rs[:],
                                           op0=ALU.mult, op1=ALU.mult).then_inc(s("v_normed"), 1)
        for g in range(9):
            if g < 8:
                dve.wait_ge(s("mixed"), g + 1)
                nc.vector.tensor_tensor(uu[:, g], uu[:, g], ps[6 + g % 2][:], ALU.mult).then_inc(s("l1_y"), 1)
            if g:
                dve.wait_ge(s("l1_y"), g)
                dve_lower_y(dve, "l1_mix", g - 1, uu[:, g - 1])

    def dve_conv3(p, b):
        which, t0 = p.j % 3, p.j // 3 * 2
        if p.j == 0:
            for mt in range(2):
                link(nc.vector.memset(pc[:, mt, 0:2], 0.0))
        for mt in range(2):
            t = t0 + mt
            w = lambda k: col(2, CCONV + k * 8 + t)
            if which == 0:
                nc.vector.tensor_tensor(gcs[:, mt], ps[b + mt][:], rs[:], ALU.mult).then_inc(evac, 1)
            elif which == 1:
                nc.vector.tensor_tensor(tmp[:, mt, 0:T], ps[b + mt][:], rs[:], ALU.mult).then_inc(evac, 1)
                nc.vector.wait_ge(evac, p.group() * 2 + 5 + mt)
                link(nc.vector.tensor_tensor(pc[:, mt, 2:2 + T], tmp[:, mt, 0:T], gcs[:, mt], ALU.mult))
                link(nc.vector.tensor_scalar(cv[:, mt], pc[:, mt, 2:2 + T], w(2), None, ALU.mult))
                for k in (1, 0):
                    link(nc.vector.scalar_tensor_tensor(out=cv[:, mt], in0=pc[:, mt, k:k + T], scalar=w(k), in1=cv[:, mt],
                                                        op0=ALU.mult, op1=ALU.add))
            else:
                nc.vector.tensor_tensor(tmp[:, mt, 0:T], ps[b + mt][:], rs[:], ALU.mult).then_inc(evac, 1)
                nc.vector.wait_ge(evac, p.group() * 2 + 5 + mt)
                nc.vector.tensor_tensor(cv[:, mt], cv[:, mt], tmp[:, mt, 0:T], ALU.mult).then_inc(s("l2_y"), 1)
                nc.vector.wait_ge(s("l2_y"), t + 1)
                dve_lower_y(nc.vector, "l2_mix", t, cv[:, mt])

    def act_conv3(p):
        if p.j % 3 == 2:
            for mt in range(2):
                t = p.j // 3 * 2 + mt
                act_upper(nc.scalar, "l2", t, cv[:, mt])


    def pool_dist(pool):
        pool.wait_ge(s("dist_free"), 1)
        plink(nc.gpsimd.iota(disti[:], pattern=[[-1, T]], base=384, channel_multiplier=1))
        nc.gpsimd.iota(distf[:], pattern=[[-1, T]], base=384, channel_multiplier=1,
                       allow_small_or_imprecise_dtypes=True).then_inc(s("dist_iota"), 1)

    def dve_dist(dve):
        dve.wait_ge(s("dist_iota"), 1)
        link(nc.vector.tensor_scalar(d0[:], distf[:], 0.0, NEG, ALU.is_lt, ALU.mult))
        link(nc.vector.tensor_tensor(d0[:], d0[:], distf[:], ALU.add))
        link(nc.vector.tensor_scalar(distf[:], distf[:], 128.0, NEG, ALU.is_gt, ALU.mult))
        link(nc.vector.tensor_tensor(dist[:, 0], d0[:], distf[:], ALU.add))
        for g, m in ((1, 3), (2, 15)):
            link(nc.vector.tensor_scalar(distm[:], disti[:], m, None, ALU.bitwise_and))
            link(nc.vector.tensor_copy(distf[:], distm[:]))
            link(nc.vector.tensor_scalar(distf[:], distf[:], 0.0, NEG, ALU.is_gt, ALU.mult))
            link(nc.vector.tensor_tensor(dist[:, g], d0[:], distf[:], ALU.add))

    MIDPREV = (stages["mid"][0], stages["mid"][1] - 1)

    def dve_mid(dve):
        dve_norm(dve, MIDPREV)
        for t in range(ND):
            nc.vector.scalar_tensor_tensor(out=x[:, t], in0=x[:, t], scalar=col(0, G_FIN + t), in1=rs[:],
                                           op0=ALU.mult, op1=ALU.mult).then_inc(s("x_set"), 1)
            if t:
                dve_lower(dve, stages["mid"], G_MIX2, t - 1)
        dve_lower(dve, stages["mid"], G_MIX2, ND - 1)

    def dve_tok(p, b):
        for tt in range(4):
            ins = nc.vector.tensor_scalar(vt[:, tt, p.j * 256:p.j * 256 + 256], ps[b + tt // 2][:, tt % 2 * 256:tt % 2 * 256 + 256],
                                          rscol[:, tt:tt + 1], None, ALU.mult)
            if tt % 2:
                ins.then_inc(evac, 1)

    def pe_rscol(pe):
        pe.wait_ge(evac, stages["q"].g0 * 2 + 6)
        for tt in range(4):
            last = nc.tensor.matmul(ps[5][:, tt:tt + 1], rs[0:1, tt * P:tt * P + P], ones[0:1, 0:1], start=True, stop=True)
        last.then_inc(s("rs_turned"), 1)

    def dve_rscol(dve):
        dve.wait_ge(s("rs_turned"), 1)
        link(nc.vector.tensor_copy(rscol[:, 0:4], ps[5][:, 0:4]))

    combos = [(h, i) for h in range(4) for i in range(4)]
    slopes = [2.0 ** (-8.0 * (k + 1) / 12) for k in range(12)]

    def segments(i):
        out_, at_ = [], 0
        for g in range(3):
            k0 = max(i - 1, 0) if g == 0 else 0
            out_.append((g, k0, at_))
            at_ += (i + 1 - k0) * P
        return out_, at_

    def pe_attn(pe):
        pe.wait_ge(evac, (stages["v"].g0 + 3) * 2 + 4)

        def scores(n):
            h, i = combos[n]
            lo = 64 * (h % 2)
            if n:
                pe.wait_ge(s("at_scored"), n)
            for g, k0, _ in segments(i)[0]:
                ti = (4 * g + h) // 2
                last = nc.tensor.matmul(ps[4 + g][:, 0:(i + 1 - k0) * P], qT[lo:lo + 64, ti, i * P:i * P + P],
                                        kT[lo:lo + 64, ti, k0 * P:(i + 1) * P], start=True, stop=True)
            last.then_inc(s("at_scores"), 1)

        scores(0)
        for n, (h, i) in enumerate(combos):
            if n + 1 < 16:
                scores(n + 1)
            segs, width = segments(i)
            nb = width // P
            pe.wait_ge(s("at_probs"), n + 1)
            if n:
                pe.wait_ge(s("at_pt"), n)
            for b in range(nb):
                last = nc.tensor.transpose(ps[(7, 0, 1)[b // 4]][:, b % 4 * P:b % 4 * P + P], sc[:, n % 2, b * P:b * P + P], ident[:])
            last.then_inc(s("at_turned"), 1)
            pe.wait_ge(s("at_pt"), n + 1)
            o = ps[2 + h // 2][64 * (h % 2):64 * (h % 2) + 64, i * P:i * P + P]
            for g, k0, at_ in segs:
                for k in range(k0, i + 1):
                    b = at_ // P + k - k0
                    last = nc.tensor.matmul(o, vt[:, k, (4 * g + h) * 64:(4 * g + h) * 64 + 64], pt[:, b],
                                            start=b == 0, stop=b == nb - 1)
            last.then_inc(s("at_pv"), 1)
        pe.wait_ge(s("at_done"), 2)

    def dve_attn(dve):
        def score(n):
            h, i = combos[n]
            segs, width = segments(i)
            dve.wait_ge(s("at_scores"), n + 1)
            if n >= 2:
                dve.wait_ge(s("at_turned"), n - 1)
            for g, k0, at_ in segs:
                w = (i + 1 - k0) * P
                x0 = k0 * P + P * (3 - i)
                ins = nc.vector.scalar_tensor_tensor(out=sc[:, n % 2, at_:at_ + w], in0=dist[:, g, x0:x0 + w],
                                                     scalar=-8.0 * slopes[4 * g + h], in1=ps[4 + g][:, 0:w],
                                                     op0=ALU.mult, op1=ALU.add)
            ins.then_inc(s("at_scored"), 1)
            dve.wait_ge(s("at_scored"), n + 1)
            link(nc.vector.tensor_reduce(stat[:, n % 2:n % 2 + 1], sc[:, n % 2, 0:width], AX.X, ALU.max))
            nc.vector.tensor_scalar(stat[:, 2 + n % 2:3 + n % 2], stat[:, n % 2:n % 2 + 1], -0.125, None, ALU.mult)\
                .then_inc(s("at_max"), 1)

        score(0)
        for n, (h, i) in enumerate(combos):
            _, width = segments(i)
            dve.wait_ge(s("at_exp"), n + 1)
            link(nc.vector.reciprocal(den[:, 2 + n % 2:3 + n % 2], den[:, n % 2:n % 2 + 1]))
            nc.vector.tensor_scalar(sc[:, n % 2, 0:width], sc[:, n % 2, 0:width], den[:, 2 + n % 2:3 + n % 2], None, ALU.mult)\
                .then_inc(s("at_probs"), 1)
            if n + 1 < 16:
                score(n + 1)
        dve.wait_ge(s("at_pv"), 16)
        for h in range(2):
            nc.vector.tensor_copy(ya[:, h], ps[2 + h][:]).then_inc(s("at_done"), 1)

    def act_attn(act):
        def exp(n):
            _, width = segments(combos[n][1])
            act.wait_ge(s("at_max"), n + 1)
            nc.scalar.activation(sc[:, n % 2, 0:width], sc[:, n % 2, 0:width], ACT.Exp, scale=0.125,
                                 bias=stat[:, 2 + n % 2:3 + n % 2], accum_out=den[:, n % 2:n % 2 + 1]).then_inc(s("at_exp"), 1)

        exp(0)
        for n, (h, i) in enumerate(combos):
            nb = segments(i)[1] // P
            act.wait_ge(s("at_turned"), n + 1)
            if n:
                act.wait_ge(s("at_pv"), n)
            for b in range(0, nb, 4):
                m = min(4, nb - b)
                ins = nc.scalar.activation(pt[:, b:b + m], ps[(7, 0, 1)[b // 4]][:, 0:m * P].rearrange("p (a n) -> p a n", n=P), ACT.Copy)
            ins.then_inc(s("at_pt"), 1)
            if n + 1 < 16:
                exp(n + 1)

    def act_gates(p):
        act = nc.scalar
        if p.j == 0:
            act_pair(act, ND - 1)
        for mt in range(2):
            t = p.j * 2 + mt
            act.wait_ge(evac, p.group() * 2 + 5 + mt)
            act.activation(tmp[:, mt, 0:T], tmp[:, mt, 0:T], ACT.Sigmoid).then_inc(acted, 1)
            act.wait_ge(acted, stages["gates"].a0 + t + 3)
            act.dma_start(gate_spill[t], tmp[:, mt, 0:T]).then_inc(s(f"gate_stored{mt}"), 16)

    def dve_gates(p, b):
        if p.j == 0:
            dve_pair(nc.vector, ND - 1)
        for mt in range(2):
            if p.j:
                nc.vector.wait_ge(s(f"gate_stored{mt}"), 16 * p.j)
            nc.vector.tensor_tensor(tmp[:, mt, 0:T], ps[b + mt][:], rs[:], ALU.mult).then_inc(evac, 1)

    def shift(p, b, mt, mu, dest, done=None):
        nc.vector.tensor_tensor(tmp[:, mt, 1:T + 1], ps[b + mt][:], rs[:], ALU.mult).then_inc(evac, 1)
        nc.vector.wait_ge(evac, p.group() * 2 + 5 + mt)
        link(nc.vector.tensor_tensor(hf[:, mt], tmp[:, mt, 0:T], tmp[:, mt, 1:T + 1], ALU.subtract))
        ins = nc.vector.scalar_tensor_tensor(out=dest, in0=hf[:, mt], scalar=col(3, mu), in1=tmp[:, mt, 1:T + 1],
                                             op0=ALU.mult, op1=ALU.add)
        if done:
            ins.then_inc(s(done), 1)
        else:
            link(ins)

    def dve_lora(p, b):
        if p.j == 0:
            nc.vector.wait_ge(s("x_stored"), 16)
            for mt in range(2):
                link(nc.vector.memset(tmp[:, mt, 0:1], 0.0))
            shift(p, b, 0, MU + 24, wda[:], "lora_shifted")
            shift(p, b, 1, MU + 25, gd[:, 0], "lora_shifted")
        else:
            nc.vector.memset(small[:, 44:45], 0.0).then_inc(evac, 1)
            shift(p, b, 1, MU + 26, gd[:, 1], "lora_shifted")

    def act_lora(p):
        act = nc.scalar
        if p.j == 0:
            act.wait_ge(s("lora_shifted"), 1)
            act.activation(wda[0:64], wda[0:64], ACT.Tanh).then_inc(s("lora_ready"), 1)
            act.wait_ge(s("lora_shifted"), 2)
            act.activation(gd[:, 0], gd[:, 0], ACT.Sigmoid).then_inc(s("lora_ready"), 1)
        else:
            act.wait_ge(s("lora_shifted"), 3)
            act.activation(gd[:, 1], gd[:, 1], ACT.Sigmoid).then_inc(s("lora_ready"), 1)

    T1, T2, T3, T4, T5, T6 = rt[:, 4], rt[:, 5], rt[:, 6], rt[:, 7], hf[:, 0], hf[:, 1]
    rmask = acc

    def pe_pair(pe, q):
        cs = slice(q * P, q * P + P)
        if q == 0:
            pe.wait_ge(s("lora_landed"), 32)
            pe.wait_ge(s("lora_ready"), 1)
        else:
            pe.wait_ge(s("pair_gates"), 2 * q)
        nc.tensor.matmul(ps[4][:], w2a2[0:64, cs], wda[0:64], start=True, stop=True)
        nc.tensor.matmul(ps[5][:], w2a2[64:P, cs], wda[64:P], start=True, stop=True).then_inc(s("pair_lora"), 1)
        pe.wait_ge(s("pair_kk"), q + 1)
        nc.tensor.matmul(ps[6][:], headones[:], T6, start=True, stop=True).then_inc(s("pair_sum"), 1)

    def pe_bonus(pe, q):
        pe.wait_ge(s("pair_rk"), q + 1)
        if q:
            pe.wait_ge(s("pair_bonus"), q)
        nc.tensor.matmul(ps[7][:], headones[:], T1, start=True, stop=True).then_inc(s("pair_rksum"), 1)

    def pe_pairs(pe, c):
        q = c // 3 * 2
        if c % 3 == 2:
            pe_pair(pe, q)
        elif c % 3 == 0 and c:
            pe_bonus(pe, q - 2)
            pe_pair(pe, q - 1)
        elif c > 1:
            pe_bonus(pe, q - 1)

    def act_pair(act, q):
        k = rt[:, 2 + q % 2]
        act.wait_ge(s("pair_lora"), q + 1)
        if q:
            act.wait_ge(s("pair_pooled"), 2 * q)
        act.activation(T1, ps[4][:], ACT.Sigmoid, bias=col(2, W0C + q)).then_inc(s("pair_gates"), 1)
        act.activation(T4, ps[5][:], ACT.Sigmoid, bias=col(2, A0C + q)).then_inc(s("pair_gates"), 1)
        act.wait_ge(s("pair_start"), q + 1)
        act.activation(T6, k, ACT.Square, scale=col(2, KKC + q)).then_inc(s("pair_kk"), 1)
        act.wait_ge(s("pair_cum"), q + 1)
        act.activation(T5, T2, ACT.Exp, scale=-LOG_DECAY).then_inc(s("pair_exp"), 1)
        act.activation(T3, T3, ACT.Exp, scale=-LOG_DECAY).then_inc(s("pair_exp"), 1)
        act.wait_ge(s("pair_exp"), 3 * q + 2)
        act.activation(T2, T2, ACT.Exp, scale=LOG_DECAY).then_inc(s("pair_exp"), 1)
        act.wait_ge(s("pair_sum"), q + 1)
        act.activation(T6, ps[6][:], ACT.Sqrt).then_inc(s("pair_root"), 1)
        act.wait_ge(s("pair_bonus"), q + 1)
        act.dma_start(bonus_spill[q], T3).then_inc(s("bonus_stored"), 16)

    def c3(t_):
        return t_.rearrange("p (c n) -> p c n", c=NC)

    def dve_pair(dve, q):
        r, k = rt[:, q % 2], rt[:, 2 + q % 2]
        nc.vector.memset(small[:, 46:47], 0.0).then_inc(s("pair_start"), 1)
        dve.wait_ge(s("pair_gates"), 2 * q + 1)
        if q:
            dve.wait_ge(s("bonus_stored"), 16 * q)
            dve.wait_ge(s("pair_pooled"), 2 * q)
        link(nc.vector.tensor_tensor_scan(T2, rmask[:], T1, 0.0, ALU.mult, ALU.add))
        nc.vector.tensor_tensor(T3, T2, T1, ALU.subtract).then_inc(s("pair_cum"), 1)
        dve.wait_ge(s("pair_root"), q + 1)
        dve.wait_ge(s("pair_cum"), q + 1)
        link(nc.vector.tensor_scalar(T1, T6, 1e-12, None, ALU.max))
        link(nc.vector.reciprocal(T1, T1))
        link(nc.vector.scalar_tensor_tensor(out=T6, in0=k, scalar=col(2, KKC + q), in1=T1, op0=ALU.mult, op1=ALU.mult))
        link(nc.vector.tensor_tensor(T1, T6, T4, ALU.mult))
        dve.wait_ge(s("pair_exp"), 3 * q + 3)
        nc.vector.scalar_tensor_tensor(out=AR[:, :, q, 0, :], in0=c3(T6), scalar=-1.0, in1=c3(T3), op0=ALU.mult, op1=ALU.mult)
        link(nc.vector.tensor_tensor(BT[:, :, q, :], c3(T1), c3(T2), ALU.mult))
        link(nc.vector.tensor_scalar(T4, T4, -1.0, col(2, KAC + q), ALU.add, ALU.mult))
        link(nc.vector.scalar_tensor_tensor(out=T4, in0=T4, scalar=1.0, in1=k, op0=ALU.add, op1=ALU.mult))
        link(nc.vector.tensor_copy(PCt[:, :, q:q + 1], c3(T5)[:, :, CH - 1:CH]))
        nc.vector.scalar_tensor_tensor(out=T1, in0=r, scalar=col(3, RKC + q), in1=T4, op0=ALU.mult, op1=ALU.mult)\
            .then_inc(s("pair_rk"), 1)
        dve.wait_ge(s("pair_rksum"), q + 1)
        nc.vector.tensor_tensor(T3, ps[7][:], VT[:, q], ALU.mult).then_inc(s("pair_bonus"), 1)

    def pool_pairs(pool):
        for q in range(ND):
            pool.wait_ge(s("pair_start"), q + 1)
            pool.wait_ge(s("pair_exp"), 3 * q + 1)
            nc.gpsimd.tensor_tensor(AR[:, :, q, 1, :], c3(rt[:, q % 2]), c3(T5), ALU.mult).then_inc(s("pair_pooled"), 1)
            pool.wait_ge(s("pair_rk"), q + 1)
            pool.wait_ge(s("pair_exp"), 3 * q + 3)
            nc.gpsimd.tensor_tensor(KT[:, :, q, :], c3(T4), c3(T2), ALU.mult).then_inc(s("pair_pooled"), 1)

    def dve_rkv(p, b):
        which, jj = p.j % 3, p.j // 3
        if which == 0 and jj:
            dve_pair(nc.vector, 2 * jj - 1)
        if p.j == 0:
            link(nc.vector.memset(rmask[:], 1.0))
            link(nc.vector.memset(c3(rmask[:])[:, :, 0:1], 0.0))
        for mt in range(2):
            q = 2 * jj + mt
            dest = (rt[:, mt], rt[:, 2 + mt], VT[:, q])[which]
            if q >= 2 and which == 0 and mt == 0:
                nc.vector.wait_ge(s("pair_bonus"), q)
                nc.vector.wait_ge(s("pair_pooled"), 2 * q - 1)
            shift(p, b, mt, MU + which * 8 + q, dest, "k_shifted" if which == 1 else None)
        if which == 1:
            nc.vector.wait_ge(s("k_shifted"), 2 * jj + 2)
        if which == 2:
            dve_pair(nc.vector, 2 * jj)

    def act_rkv(p):
        jj = p.j // 3
        if p.j % 3 == 0 and jj:
            act_pair(nc.scalar, 2 * jj - 1)
        if p.j % 3 == 2:
            act_pair(nc.scalar, 2 * jj)

    X, Z, Yt, W0, U, ST = (ck[n_] for n_ in ("X", "Z", "Yt", "W0", "U", "ST"))
    HP = (slice(0, 64), slice(64, P))
    cols = lambda q: slice(q * CH, q * CH + CH)

    def dve_chunk_masks(dve):
        link(nc.vector.tensor_copy(i64[0:64], ident[0:64, 0:64]))
        link(nc.vector.tensor_copy(i64[64:P], ident[64:P, 64:P]))
        dve.wait_ge(s("token_numbers"), 3)
        link(nc.vector.tensor_tensor(mk[:, 0], srcf[:], tgtf[:], ALU.is_lt))
        link(nc.vector.tensor_tensor(mk[:, 1], srcf[:], tgtf[:], ALU.is_le))
        for l in range(6):
            if l == 5:
                link(nc.vector.tensor_copy(mk[:, 7], mk[:, 0]))
            else:
                link(nc.vector.tensor_scalar(inta[:], srci[:], l + 1, None, ALU.logical_shift_right))
                link(nc.vector.tensor_scalar(intb[:], tgti[:], l + 1, None, ALU.logical_shift_right))
                link(nc.vector.tensor_tensor(mk[:, 2 + l], inta[:], intb[:], ALU.is_equal))
                link(nc.vector.tensor_tensor(mk[:, 2 + l], mk[:, 2 + l], mk[:, 0], ALU.mult))
        for l in range(5, 0, -1):
            link(nc.vector.tensor_tensor(mk[:, 2 + l], mk[:, 2 + l], mk[:, 1 + l], ALU.subtract))
        link(nc.vector.memset(ST[:], 0.0))

    def pool_tokens(pool):
        pool.wait_ge(s("rkv_done"), 1)
        plink(nc.gpsimd.iota(srci[0:64], pattern=[[0, CH]], base=0, channel_multiplier=1))
        plink(nc.gpsimd.iota(srci[64:P], pattern=[[0, CH]], base=0, channel_multiplier=1))
        nc.gpsimd.iota(tgti[:], pattern=[[1, CH]], base=0, channel_multiplier=0).then_inc(s("token_numbers"), 1)
        pool.wait_ge(s("token_numbers"), 1)
        nc.gpsimd.tensor_copy(srcf[:], srci[:]).then_inc(s("token_numbers"), 1)
        pool.wait_ge(s("token_numbers"), 2)
        nc.gpsimd.tensor_copy(tgtf[:], tgti[:]).then_inc(s("token_numbers"), 1)

    def heads_of(g, fn):
        for h in HP:
            for q in range(4 * g, 4 * g + 4):
                last = fn(h, q)
        return last

    mm = nc.tensor.matmul
    PB = (0, 1)
    PK = (6, 2)
    YB, XB, ZB = (4, 0), (5, 1), (6, 2)
    WB, UB = (7, 3), (4, 5)
    DSB, OB = 7, 3
    TURN = (4, 5, 0)

    def diag(t_, hp):
        return t_[HP[hp], :, hp * CH:hp * CH + CH]

    def pool_fill(dst, src):
        for hp, h in enumerate(HP):
            ins = nc.gpsimd.tensor_copy(diag(dst, hp), src(h))
        ins.then_inc(s("ck_filled"), 1)

    def pool_chunks(pool):
        pool.wait_ge(units, stages["merge"].u0 + 2)
        for t_ in (BS, KS, VS):
            plink(nc.gpsimd.memset(t_[:], 0.0))
        for c in range(NC):
            if c:
                pool.wait_ge(s("ck_turned"), 3 * c)
            pool_fill(BS, lambda h: BT[h, c])
            pool_fill(KS, lambda h: KT[h, c])
            pool_fill(VS, lambda h: VT[h, :, c * CH:c * CH + CH])
        pool.wait_ge(s("ck_filled"), 3 * NC)

    def pe_turns(pe, c):
        pe.wait_ge(s("ck_filled"), 3 * c + 3)
        for i_, src in enumerate((VS, BS, KS)):
            if i_ == 2:
                pe.wait_ge(s("ck_bmasked"), c + 1)
            for q in range(NH2):
                last = mm(ps[TURN[i_]][:, cols(q)], src[:, q], i64[:], start=True, stop=True)
            last.then_inc(s("ck_turned"), 1)

    def pe_products(pe, c, which, banks, done):
        pe.wait_ge(s("ck_filled"), 3 * c + which + 1)
        for q in range(NH2):
            last = mm(ps[banks[q // 4]][:, q % 4 * P:q % 4 * P + P], (BS, KS)[which][:, q],
                      AR[:, c, q].rearrange("p a n -> p (a n)"), start=True, stop=True)
        last.then_inc(s(done), 1)

    def pe_chunks(pe):
        pe.wait_ge(s("chunk_masks"), 1)
        pe_products(pe, 0, 0, PB, "ck_bprod")
        pe_products(pe, 0, 1, PK, "ck_kprod")
        pe_turns(pe, 0)
        for c in range(NC):
            b = c % 2
            pe.wait_ge(s("ck_kmasked"), c + 1)
            for g in range(2):
                pe.wait_ge(s(f"ck_z{g}"), 6 * c + 1)
                heads_of(g, lambda h, q: mm(ps[ZB[g]][h, cols(q)], TM[0][h, q], i64[h, :], start=True, stop=True)).then_inc(s(f"ck_inv{g}"), 1)
            for l in range(1, 6):
                for g in range(2):
                    if l == 1:
                        pe.wait_ge(s("ck_turned_copied"), 3 * c + 1 + 2 * g)
                    pe.wait_ge(s(f"ck_x{g}"), 5 * c + l)
                    heads_of(g, lambda h, q: mm(ps[YB[g]][h, cols(q)], TM[l % 2][h, q], X[h, q], start=True, stop=True)).then_inc(s(f"ck_y{g}"), 1)
                if l in (2, 3):
                    g = l - 2
                    if c:
                        pe.wait_ge(s("ck_state"), c)
                        pe.wait_ge(s("ck_out"), c)
                    for h in HP:
                        for q in range(4 * g, 4 * g + 4):
                            mm(ps[WB[g]][h, cols(q)], AR[h, c, q, 0], ST[h, q], start=True, stop=False)
                            last = mm(ps[WB[g]][h, cols(q)], TLK[b][h, q, 0], Vt[b][h, q], start=False, stop=True)
                    last.then_inc(s("ck_w0"), 1)
                for g in range(2):
                    pe.wait_ge(s(f"ck_y_copied{g}"), 5 * c + l)
                    if l == 1 and g == 0:
                        pe.wait_ge(s("ck_turned_copied"), 3 * c + 2)
                    pe.wait_ge(s(f"ck_z{g}"), 6 * c + l)
                    if l < 5:
                        heads_of(g, lambda h, q: mm(ps[XB[g]][h, cols(q)], Z[h, q], Yt[h, q], start=True, stop=True))
                    heads_of(g, lambda h, q: mm(ps[ZB[g]][h, cols(q)], Yt[h, q], Z[h, q], start=True, stop=True)).then_inc(s(f"ck_inv{g}"), 1)
            if c < NC - 1:
                pe_products(pe, c + 1, 0, PB, "ck_bprod")
            pe.wait_ge(s("ck_w0_copied"), 2 * c + 2)
            for g in range(2):
                pe.wait_ge(s(f"ck_z{g}"), 6 * c + 6)
                heads_of(g, lambda h, q: mm(ps[UB[g]][h, cols(q)], Z[h, q], W0[h, q], start=True, stop=True)).then_inc(s("ck_u"), 1)
            if c < NC - 1:
                pe_products(pe, c + 1, 1, PK, "ck_kprod")
            pe.wait_ge(s("ck_u_copied"), 2 * c + 2)
            for h in HP:
                for q in range(NH2):
                    mm(ps[DSB][h, cols(q)], Bt[b][h, q], U[h, q], start=True, stop=False)
                    last = mm(ps[DSB][h, cols(q)], Kt[b][h, q], Vt[b][h, q], start=False, stop=True)
            last.then_inc(s("ck_ds"), 1)
            for h in HP:
                for q in range(NH2):
                    mm(ps[OB][h, cols(q)], ST[h, q], AR[h, c, q, 1], start=True, stop=False)
                    mm(ps[OB][h, cols(q)], U[h, q], TLB[b][h, q, 1], start=False, stop=False)
                    last = mm(ps[OB][h, cols(q)], Vt[b][h, q], TLK[b][h, q, 1], start=False, stop=True)
            last.then_inc(s("ck_yout"), 1)
            if c < NC - 1:
                pe_turns(pe, c + 1)
        pe.wait_ge(s("ck_out"), NC)
        pe.wait_ge(s("ck_state"), NC)

    def b3(bank, n_=CH):
        return ps[bank][:].rearrange("p (q n) -> p q n", n=n_)

    def half(t_, g):
        return t_[:, 4 * g:4 * g + 4]

    def act_turns(act, c):
        for i_, dst in enumerate((Vt, Bt, Kt)):
            act.wait_ge(s("ck_turned"), 3 * c + i_ + 1)
            act.activation(dst[c % 2][:], b3(TURN[i_]), ACT.Copy).then_inc(s("ck_turned_copied"), 1)

    def act_chunks(act):
        act_turns(act, 0)
        for c in range(NC):
            for l in range(1, 6):
                for g in range(2):
                    act.wait_ge(s(f"ck_y{g}"), 5 * c + l)
                    act.activation(half(Yt, g), half(b3(YB[g]), g), ACT.Copy).then_inc(s(f"ck_y_copied{g}"), 1)
                if l in (2, 3):
                    act.wait_ge(s("ck_w0"), 2 * c + l - 1)
                    act.activation(half(W0, l - 2), half(b3(WB[l - 2]), l - 2), ACT.Copy).then_inc(s("ck_w0_copied"), 1)
            for g in range(2):
                act.wait_ge(s("ck_u"), 2 * c + g + 1)
                act.activation(half(U, g), half(b3(UB[g]), g), ACT.Copy).then_inc(s("ck_u_copied"), 1)
            act.wait_ge(s("ck_yout"), c + 1)
            act.activation(VT[:, :, c * CH:c * CH + CH], b3(OB), ACT.Copy).then_inc(s("ck_out"), 1)
            if c == 0:
                act.wait_ge(s("bonus_stored"), 16 * ND)
            if c < NC - 1:
                act_turns(act, c + 1)

    def dve_chunks(dve):
        dve_chunk_masks(dve)
        dve.wait_ge(s("pair_pooled"), 2 * ND)
        nc.vector.memset(small[:, 44:45], 0.0).then_inc(s("chunk_masks"), 1)
        bc = lambda m, n_: m.unsqueeze(1).to_broadcast([P, n_, CH])
        pair = mk[:, 0:2].unsqueeze(1).to_broadcast([P, 4, 2, CH])

        def masked(dst, banks):
            for g in range(2):
                ins = nc.vector.tensor_tensor(half(dst, g), ps[banks[g]][:].rearrange("p (q a n) -> p q a n", q=4, a=2), pair, ALU.mult)
            return ins

        def prepare(c):
            b = c % 2
            dve.wait_ge(s("ck_bprod"), c + 1)
            if c >= 2:
                dve.wait_ge(s("ck_yout"), c - 1)
            masked(TLB[b], PB).then_inc(s("ck_bmasked"), 1)
            dve.wait_ge(s("ck_bmasked"), c + 1)
            link(nc.vector.tensor_tensor(TM[0][:], TLB[b][:, :, 0], bc(mk[:, 2], NH2), ALU.mult))
            for g in range(2):
                if c:
                    dve.wait_ge(s("ck_u"), 2 * c)
                nc.vector.tensor_tensor(half(Z, g), half(TM[0], g), bc(i64[:], 4), ALU.add).then_inc(s(f"ck_z{g}"), 1)
            nc.vector.tensor_tensor(TM[1][:], TLB[b][:, :, 0], bc(mk[:, 3], NH2), ALU.mult)
            dve.wait_ge(s("ck_kprod"), c + 1)
            masked(TLK[b], PK).then_inc(s("ck_kmasked"), 1)

        prepare(0)
        for c in range(NC):
            for g in range(2):
                dve.wait_ge(s(f"ck_inv{g}"), 6 * c + 1)
                nc.vector.tensor_tensor(half(X, g), half(b3(ZB[g]), g), bc(i64[:], 4), ALU.add).then_inc(s(f"ck_x{g}"), 1)
            for l in range(1, 6):
                if l < 5:
                    nc.vector.tensor_tensor(TM[(l + 1) % 2][:], TLB[c % 2][:, :, 0], bc(mk[:, 3 + l], NH2), ALU.mult)
                for g in range(2):
                    dve.wait_ge(s(f"ck_inv{g}"), 6 * c + l + 1)
                    if l < 5:
                        nc.vector.tensor_tensor(half(X, g), half(X, g), half(b3(XB[g]), g), ALU.add).then_inc(s(f"ck_x{g}"), 1)
                    nc.vector.tensor_tensor(half(Z, g), half(Z, g), half(b3(ZB[g]), g), ALU.add).then_inc(s(f"ck_z{g}"), 1)
            if c == 0:
                dve.wait_ge(s("bonus_stored"), 16 * ND)
            if c < NC - 1:
                prepare(c + 1)
            dve.wait_ge(s("ck_ds"), c + 1)
            dve.wait_ge(s("ck_yout"), c + 1)
            link(nc.vector.tensor_tensor(ST[:], ST[:], b3(DSB), ALU.add))
            nc.vector.tensor_tensor(ST[:], ST[:], PCt[:, c, :].unsqueeze(2).to_broadcast([P, NH2, CH]), ALU.mult)\
                .then_inc(s("ck_state"), 1)

    def pe_heads(pe):
        pe.wait_ge(s("g2_landed"), 32)

        def mean(q):
            if q >= 2:
                pe.wait_ge(s("hd_centred"), q - 1)
            mm(ps[(4, 7)[q % 2]][:], headones[:], VT[:, q], start=True, stop=True).then_inc(s("hd_mean"), 1)

        mean(0)
        for q in range(ND):
            cs = slice(q * P, q * P + P)
            if q + 1 < ND:
                mean(q + 1)
            pe.wait_ge(s("hd_squared"), q + 1)
            if q:
                pe.wait_ge(s("hd_root"), q)
            mm(ps[5][:], headones[:], gns[:, 2], start=True, stop=True).then_inc(s("hd_var"), 1)
            if q:
                pe.wait_ge(s("ysplit_y"), q)
            mm(ps[6][:], g2s[:, 0, cs], gd[:, 0], start=True, stop=False)
            mm(ps[6][:], g2s[96:P, 1, cs], gd[96:P, 1], start=False, stop=True).then_inc(s("hd_gate"), 1)

    def act_heads(act):
        act_split(act, At(stages["merge"], 0, 0, 0), 0)

        def root(q):
            act.wait_ge(s("hd_centred"), q + 1)
            act.activation(gns[:, 2], VT[:, q], ACT.Square).then_inc(s("hd_squared"), 1)
            act.wait_ge(s("hd_var"), q + 1)
            if q >= 2:
                act.wait_ge(s("ysplit_y"), q - 1)
            act.activation(gns[:, q % 2], ps[5][:], ACT.Sqrt, scale=1.0 / 64, bias=small[:, 1:2]).then_inc(s("hd_root"), 1)

        root(0)
        for q in range(ND):
            if q + 1 < ND:
                root(q + 1)
            act_upper(act, "ysplit", q, VT[:, q])
        for h in range(2):
            act.activation(yh[:, ND + h], ya[:, h], ACT.Copy).then_inc(acted, 1)

    def dve_heads(dve):
        dve_split(dve, At(stages["merge"], 0, 0, 0), 0)

        def centre(q):
            dve.wait_ge(s("hd_mean"), q + 1)
            nc.vector.scalar_tensor_tensor(out=VT[:, q], in0=ps[(4, 7)[q % 2]][:], scalar=-1.0 / 64, in1=VT[:, q],
                                           op0=ALU.mult, op1=ALU.add).then_inc(s("hd_centred"), 1)

        centre(0)
        for q in range(ND):
            if q + 1 < ND:
                centre(q + 1)
            root = gns[:, q % 2]
            dve.wait_ge(s("hd_root"), q + 1)
            link(nc.vector.reciprocal(root, root))
            link(nc.vector.scalar_tensor_tensor(out=VT[:, q], in0=VT[:, q], scalar=col(3, GNW + q), in1=root, op0=ALU.mult, op1=ALU.mult))
            dve.wait_ge(s(f"bonus_back{q % 2}"), 16 * (q // 2 + 1))
            link(nc.vector.scalar_tensor_tensor(out=VT[:, q], in0=VT[:, q], scalar=col(3, GNB + q), in1=bon[:, q % 2], op0=ALU.add, op1=ALU.add))
            dve.wait_ge(s("hd_gate"), q + 1)
            nc.vector.tensor_tensor(VT[:, q], VT[:, q], ps[6][:], ALU.mult).then_inc(s("ysplit_y"), 1)
            if q:
                dve_lower_y(dve, "ysplit", q - 1, VT[:, q - 1])
        dve_lower_y(dve, "ysplit", ND - 1, VT[:, ND - 1])
        dve.wait_ge(split, stages["ysplit"][0] + ND)
        for h in range(2):
            dve_lower_y(dve, "ysplit", ND + h, ya[:, h])

    def pool_heads(pool):
        pool.wait_ge(s("ck_state"), NC)
        pool.wait_ge(s("ck_out"), NC)
        pool.dma_start(g2s[:, 0], a["g2_2"][0, 0:P]).then_inc(s("g2_landed"), 16)
        pool.dma_start(g2s[96:P, 1], a["g2_2"][0, P:P + 32]).then_inc(s("g2_landed"), 16)
        pool.wait_ge(s("bonus_stored"), 16 * ND)
        for q in range(ND):
            if q >= 2:
                pool.wait_ge(s("ysplit_y"), q - 1)
            pool.dma_start(bon[:, q % 2], bonus_spill[q]).then_inc(s(f"bonus_back{q % 2}"), 16)
        pool.wait_ge(s("gate_stored0"), 128)
        pool.wait_ge(s("gate_stored1"), 128)
        pool.dma_start(gl[:], gate_spill.rearrange("t p n -> p t n")).then_inc(s("gates_back"), 16)
        pool.wait_ge(s("x_stored"), 16)
        pool.dma_start(x[:], x_spill).then_inc(s("x_back"), 16)

    def dve_merge(p, b):
        dve = nc.vector
        if p.j == 0:
            dve.wait_ge(s("gates_back"), 16)
        for mt in range(2):
            t = p.j // 2 * 2 + mt
            if p.j % 2 == 0:
                dve.tensor_tensor(mg[:, t], ps[b + mt][:], gl[:, t], ALU.mult).then_inc(evac, 1)
            else:
                if mt == 0:
                    dve.wait_ge(evac, p.group() * 2 + 4)
                dve.tensor_tensor(gl[:, t], ps[b + mt][:], gl[:, ND + t], ALU.mult).then_inc(evac, 1)
                dve.wait_ge(evac, p.group() * 2 + 5 + mt)
                dve.tensor_tensor(mg[:, t], mg[:, t], gl[:, t], ALU.add).then_inc(s("msplit_y"), 1)

    def act_msplit(act):
        act.wait_ge(units, stages["merge"].u0 + 10)
        for t in range(ND):
            act_upper(act, "msplit", t, mg[:, t])

    def dve_msplit(dve):
        dve.wait_ge(s("x_back"), 16)
        for t in range(ND):
            dve_lower_y(dve, "msplit", t, mg[:, t])

    def sp_mem(sp):
        sp.dma_start(mtok[:], a["mem_2"][0].rearrange("(c p) d -> p c d", p=P)).then_inc(s("mem_landed"), 16)

    def pe_mem(pe):
        for c in range(2):
            pe.wait_ge(s("mem_normed"), c + 1)
        for t in range(ND):
            if t >= 2:
                pe.wait_ge(s("mem_split"), t - 1)
            for c in range(2):
                last = nc.tensor.transpose(ps[4 + t % 2][:, c * P:c * P + P], mtok[:, c, t * P:t * P + P], ident[:])
            last.then_inc(s("mem_turned"), 1)
        pe.wait_ge(s("mem_split"), ND)

    def act_mem(act):
        act.wait_ge(s("mem_landed"), 16)
        for c in range(2):
            act.activation(mjunk[:], mtok[:, c], ACT.Square, accum_out=msq[:, c:c + 1]).then_inc(s("mem_summed"), 1)
            act.wait_ge(s("mem_summed"), c + 1)
        act.activation(msq[:, 2:4], msq[:, 0:2], ACT.Sqrt, scale=1.0 / D, bias=small[:, 0:1]).then_inc(s("mem_root"), 1)
        for t in range(ND):
            act.wait_ge(s("mem_turned"), t + 1)
            act.activation(mh[:, t], ps[4 + t % 2][:, 0:MEM], ACT.Copy, scale=col(0, G_MEM + t)).then_inc(s("mem_upper"), 1)

    def dve_mem(dve):
        dve.wait_ge(s("mem_root"), 1)
        link(nc.vector.reciprocal(msq[:, 4:6], msq[:, 2:4]))
        for c in range(2):
            nc.vector.tensor_scalar(mtok[:, c], mtok[:, c], msq[:, 4 + c:5 + c], None, ALU.mult).then_inc(s("mem_normed"), 1)
        for t in range(ND):
            dve.wait_ge(s("mem_upper"), t + 1)
            nc.vector.scalar_tensor_tensor(out=ml[:, t], in0=ps[4 + t % 2][:, 0:MEM], scalar=col(0, G_MEM + t), in1=mh[:, t],
                                           op0=ALU.mult, op1=ALU.subtract).then_inc(s("mem_split"), 1)

    def dve_memk(p, b):
        for mt in range(2):
            nc.vector.tensor_copy(kx[:, 2 * p.j + mt], ps[b + mt][:, 0:MEM]).then_inc(evac, 1)

    def dve_memv(p, b):
        for tt in range(2):
            nc.vector.tensor_copy(vx[:, tt, p.j * 256:p.j * 256 + 256], ps[b + tt][:, 0:256]).then_inc(evac, 1)

    def pe_cross(pe):
        pe.wait_ge(evac, (stages["memv"].g0 + 4) * 2 + 4)

        def scores(n):
            h, i = n // 4, n % 4
            if n >= 2:
                pe.wait_ge(s("cx_max"), n - 1)
                pe.wait_ge(s("cx_exp"), n - 1)
            for t in range(2):
                last = mm(ps[4 + n % 2][:, 0:MEM], qx[:, 2 * h + t, i * P:i * P + P], kx[:, 2 * h + t], start=t == 0, stop=t == 1)
            last.then_inc(s("cx_scores"), 1)

        scores(0)
        scores(1)
        for n in range(16):
            h, i = n // 4, n % 4
            if n + 2 < 16:
                scores(n + 2)
            pe.wait_ge(s("cx_probs"), n + 1)
            if h and i == 0:
                pe.wait_ge(s("cx_pt"), 2 * h)
            for t in range(2):
                last = nc.tensor.transpose(ps[6 + t][:, i * P:i * P + P], sx[:, n % 4, t * P:t * P + P], ident[:])
            last.then_inc(s("cx_turned"), 1)
            if i == 3:
                pe.wait_ge(s("cx_pt"), 2 * h + 2)
                if h:
                    pe.wait_ge(s("cx_y"), 2 * h)
                for ct in range(2):
                    for t in range(2):
                        c0 = h * 256 + ct * P
                        last = mm(ps[ct][:], vx[:, t, c0:c0 + P], ptx[:, t], start=t == 0, stop=t == 1)
                last.then_inc(s("cx_out"), 1)
        pe.wait_ge(s("cx_y"), 8)

    def act_cross(act):
        for n in range(17):
            if n < 16:
                act.wait_ge(s("cx_max"), n + 1)
                act.activation(sx[:, n % 4], ps[4 + n % 2][:, 0:MEM], ACT.Exp, scale=1.0 / 16, bias=stx[:, 4 + n % 4:5 + n % 4],
                               accum_out=stx[:, 8 + n % 4:9 + n % 4]).then_inc(s("cx_exp"), 1)
            if n and n % 4 == 0:
                h = n // 4 - 1
                act.wait_ge(s("cx_turned"), 4 * h + 4)
                if h:
                    act.wait_ge(s("cx_out"), h)
                for t in range(2):
                    act.activation(ptx[:, t], ps[6 + t][:], ACT.Copy).then_inc(s("cx_pt"), 1)
        for t in range(ND):
            act.wait_ge(s("cx_y"), t + 1)
            act.activation(yh[:, t], qx[:, t], ACT.Copy).then_inc(acted, 1)

    def dve_cross(dve):
        def out_tiles(h):
            dve.wait_ge(s("cx_out"), h + 1)
            for ct in range(2):
                nc.vector.tensor_copy(qx[:, 2 * h + ct], ps[ct][:]).then_inc(s("cx_y"), 1)

        def top(n):
            dve.wait_ge(s("cx_scores"), n + 1)
            if n >= 4:
                dve.wait_ge(s("cx_turned"), n - 3)
            link(nc.vector.tensor_reduce(stx[:, n % 4:n % 4 + 1], ps[4 + n % 2][:, 0:MEM], AX.X, ALU.max))
            nc.vector.tensor_scalar(stx[:, 4 + n % 4:5 + n % 4], stx[:, n % 4:n % 4 + 1], -1.0 / 16, None, ALU.mult).then_inc(s("cx_max"), 1)

        top(0)
        for n in range(16):
            if n + 1 < 16:
                top(n + 1)
            dve.wait_ge(s("cx_exp"), n + 1)
            link(nc.vector.reciprocal(stx[:, 12 + n % 4:13 + n % 4], stx[:, 8 + n % 4:9 + n % 4]))
            nc.vector.tensor_scalar(sx[:, n % 4], sx[:, n % 4], stx[:, 12 + n % 4:13 + n % 4], None, ALU.mult).then_inc(s("cx_probs"), 1)
            if n % 4 == 0 and n:
                out_tiles(n // 4 - 1)
        out_tiles(3)
        for t in range(ND):
            dve.wait_ge(acted, stages["xsplit"][1] + t + 3)
            nc.vector.tensor_tensor(yl[:, t], qx[:, t], yh[:, t], ALU.subtract).then_inc(split, 1)

    def sp_extra(sp, name):
        if name == "lora":
            sp.wait_ge(s("at_done"), 2)
            sp.dma_start(w2a2[0:64], a["w2_2"][0]).then_inc(s("lora_landed"), 16)
            sp.dma_start(w2a2[64:P], a["a2_2"][0]).then_inc(s("lora_landed"), 16)
            sp.dma_start(x_spill, x[:]).then_inc(s("x_stored"), 16)
        if name == "wq":
            sp.wait_ge(units, stages["wq"].u0 + 2)
            sp_mem(sp)

    def pool_second(pool):
        pool_squares(pool, G["mid"])
        pool_dist(pool)
        pool_pairs(pool)
        pool_tokens(pool)
        pool_chunks(pool)
        pool_heads(pool)
        pool_stage(pool, G["out2"])
        pool_stage(pool, G["xo"])
        pool_mlp(pool, "ffn")

    def pe_second(pe):
        pe_norm(pe, MIDPREV)
        pe_stage(pe, G["q"])
        pe_rscol(pe)
        pe_stage(pe, G["k"])
        pe_stage(pe, G["v"])
        pe_attn(pe)
        pe_stage(pe, G["lora"])
        pe_stage(pe, G["rkv"])
        pe_stage(pe, G["gates"])
        pe_chunks(pe)
        pe_heads(pe)
        pe_stage(pe, G["merge"])
        pe_stage(pe, G["out2"])
        pe_stage(pe, G["wq"])
        pe_mem(pe)
        pe_stage(pe, G["memk"])
        pe_stage(pe, G["memv"])
        pe_cross(pe)
        pe_stage(pe, G["xo"])
        for h in range(2):
            pe_stage(pe, G[f"ffn_up{h}"])
            pe_stage(pe, G[f"ffn_down{h}"])

    def act_second(act):
        act_norm(act, MIDPREV)
        act_resplit(act, G["mid"], G_MIX2, ND)
        act_stage(act, G["q"])
        act_stage(act, G["k"])
        act_stage(act, G["v"])
        act_attn(act)
        act_stage(act, G["lora"], custom=act_lora)
        act_stage(act, G["rkv"], custom=act_rkv)
        act_stage(act, G["gates"], custom=act_gates)
        act_chunks(act)
        act_heads(act)
        act_stage(act, G["merge"], custom=lambda p: None)
        act_msplit(act)
        act_stage(act, G["out2"])
        act_stage(act, G["wq"])
        act_mem(act)
        act_stage(act, G["memk"])
        act_stage(act, G["memv"])
        act_cross(act)
        act_stage(act, G["xo"])
        for h in range(2):
            act_stage(act, G[f"ffn_up{h}"])
            act_stage(act, G[f"ffn_down{h}"])

    def dve_second(dve):
        dve_mid(dve)
        nc.vector.memset(small[:, 45:46], 0.0).then_inc(s("dist_free"), 1)
        dve_stage(dve, G["q"], qT)
        dve_rscol(dve)
        dve_stage(dve, G["k"], kT)
        dve_stage(dve, G["v"], custom=dve_tok)
        dve_dist(dve)
        dve_attn(dve)
        dve_stage(dve, G["lora"], custom=dve_lora)
        dve_stage(dve, G["rkv"], custom=dve_rkv)
        dve_stage(dve, G["gates"], custom=dve_gates)
        nc.vector.memset(small[:, 45:46], 0.0).then_inc(s("rkv_done"), 1)
        dve_chunks(dve)
        dve_heads(dve)
        dve_stage(dve, G["merge"], custom=dve_merge)
        dve_msplit(dve)
        dve_stage(dve, G["out2"])
        dve_stage(dve, G["wq"], qx)
        dve_mem(dve)
        dve_stage(dve, G["memk"], custom=dve_memk)
        dve_stage(dve, G["memv"], custom=dve_memv)
        dve_cross(dve)
        dve_stage(dve, G["xo"])
        for h in range(2):
            dve_stage(dve, G[f"ffn_up{h}"])
            dve_stage(dve, G[f"ffn_down{h}"])

    def pe_final(pe):
        pe_norm(pe, final_norm)
        for c in range(4):
            for half in range(2):
                n_ = 2 * c + half
                if n_ >= 4:
                    pe.wait_ge(s("out_copied"), n_ - 3)
                if n_ < 2:
                    pe.wait_ge(s("out_scaled"), 4 * half + 4)
                for k in range(4):
                    last = nc.tensor.transpose(ps[4 + n_ % 4][:, k * P:k * P + P], fo[:, 4 * half + k, c * P:c * P + P], ident[:])
                last.then_inc(s("out_turned"), 1)

    def dve_final(dve):
        dve_norm(dve, final_norm)
        for t in range(ND):
            nc.vector.scalar_tensor_tensor(out=fo[:, t], in0=x[:, t], scalar=col(0, G_OUT + t), in1=rs[:],
                                           op0=ALU.mult, op1=ALU.mult).then_inc(s("out_scaled"), 1)

    def act_final(act):
        act_norm(act, final_norm)
        for n_ in range(8):
            act.wait_ge(s("out_turned"), n_ + 1)
            nc.scalar.activation(xtok[:, n_ // 2, n_ % 2 * T:n_ % 2 * T + T], ps[4 + n_ % 4][:], ACT.Copy).then_inc(s("out_copied"), 1)

    def sp_final(sp):
        o = out[0].rearrange("(c p) d -> p c d", p=P)
        for c in range(4):
            sp.wait_ge(s("out_copied"), 2 * c + 2)
            sp.dma_start(o[:, c], xtok[:, c]).then_inc(s("out_stored"), 16)
        sp.wait_ge(s("out_stored"), 64)

    block = ctx.enter_context(nc.Block())
    G = stages

    def pool_mlp(pool, n):
        for h in range(2):
            pool_stage(pool, G[f"{n}_up{h}"])
            pool_stage(pool, G[f"{n}_down{h}"])

    @block.sync
    def _(sp):
        sp_init(sp)
        for st in order:
            sp_stage(sp, st)
            if st.name == "l1_v":
                sp_b(sp)
            sp_extra(sp, st.name)
        sp_final(sp)

    @block.gpsimd
    def _(pool):
        pool_init(pool)
        for l in range(4):
            if l % 3 == 0:
                pool_a(pool, l)
            if l == 1:
                pool_stage(pool, G["l1_v"])
                pool_b(pool)
            pool_stage(pool, G[f"l{l}_out"])
            pool_mlp(pool, f"l{l}_mlp")
        pool_second(pool)

    @block.tensor
    def _(pe):
        pe_init(pe)
        for l in range(4):
            if l % 3 == 0:
                pe_stage(pe, G[f"l{l}_branch"])
                pe_a(pe, l)
                pe_stage(pe, G[f"l{l}_gate"])
            elif l == 1:
                pe_stage(pe, G["l1_v"])
                pe_stage(pe, G["l1_u"])
                pe_b(pe, G["l1_u"].norm)
            else:
                pe_stage(pe, G["l2_in"])
            pe_stage(pe, G[f"l{l}_out"])
            for h in range(2):
                pe_stage(pe, G[f"l{l}_mlp_up{h}"])
                pe_stage(pe, G[f"l{l}_mlp_down{h}"])
        pe_second(pe)
        pe_final(pe)

    @block.scalar
    def _(act):
        act_split(act, At(order[0], 0, 0, 0), 0)
        act_init(act)
        for l in range(4):
            if l % 3 == 0:
                act_stage(act, G[f"l{l}_branch"])
                act_a(act, l)
                act_stage(act, G[f"l{l}_gate"], custom=act_gate(l))
            elif l == 1:
                act_stage(act, G["l1_v"], vv, ACT.Gelu_apprx_tanh)
                act_stage(act, G["l1_u"], uu, ACT.Gelu_apprx_tanh)
                act_b(act, G["l1_u"].norm)
            else:
                act_stage(act, G["l2_in"], custom=act_conv3)
            act_stage(act, G[f"l{l}_out"])
            for h in range(2):
                act_stage(act, G[f"l{l}_mlp_up{h}"])
                act_stage(act, G[f"l{l}_mlp_down{h}"])
        act_second(act)
        act_final(act)

    @block.vector
    def _(dve):
        dve_split(dve, At(order[0], 0, 0, 0), 0)
        dve_init(dve)
        dve_softplus(dve)
        for l in range(4):
            if l % 3 == 0:
                dve_stage(dve, G[f"l{l}_branch"], custom=dve_conv4(l))
                dve_a(dve, l)
                dve_stage(dve, G[f"l{l}_gate"], custom=dve_gate(l))
            elif l == 1:
                dve_stage(dve, G["l1_v"])
                dve_stage(dve, G["l1_u"])
                dve_b(dve, G["l1_u"].norm)
            else:
                dve_stage(dve, G["l2_in"], custom=dve_conv3)
            dve_stage(dve, G[f"l{l}_out"])
            for h in range(2):
                dve_stage(dve, G[f"l{l}_mlp_up{h}"])
                dve_stage(dve, G[f"l{l}_mlp_down{h}"])
        dve_second(dve)
        dve_final(dve)

    ctx.close()


_INS = [
    "x", "norm_mix_g", "norm_mlp_g", "final_norm_g", "a_w_in", "a_conv_w", "a_conv_b", "gate_band", "a_gate_a_b",
    "a_gate_x_b", "a_lambda", "a_w_out", "b_w_in", "b_norm_g", "b_w_s", "b_s_bias", "b_w_out",
    "c_w_in", "c_conv_w", "c_w_out", "mlp_w1", "mlp_w2", "mem_2", "norm_mix_g_2", "w_in_2", "shift_mu_2", "w0_2",
    "w2_2", "a0_2", "a2_2", "g2_2", "k_k_2", "k_a_2", "r_k_2", "gn_w_2", "gn_b_2", "p_rwkv_2", "p_attn_2", "w_out_2",
    "norm_x_g_2", "norm_mem_g_2", "xa_wq_2", "xa_wkv_2", "xa_wo_2", "norm_ffn_g_2", "ffn_w1_2", "ffn_w2_2",
    "norm_final_g_2",
]


def pack_gates(inputs):
    import numpy as np

    w = np.stack([np.asarray(inputs["a_gate_a_w"]), np.asarray(inputs["a_gate_x_w"])])
    layers, n = w.shape[1], 5 * P
    full = np.zeros((2, layers, 2, n, n), w.dtype)
    for h in range(16):
        b = h % 8 * HDA
        full[:, :, h // 8, b:b + HDA, b:b + HDA] = w[:, :, h]
    packed = np.zeros((layers, 2, P, len(BAND), 2, P), w.dtype)
    for b, (i, o) in enumerate(BAND):
        packed[:, :, :, b] = full[:, :, :, i * P:i * P + P, o * P:o * P + P].transpose(1, 2, 3, 0, 4)
    return packed


def kernel(**inputs):
    import numpy as np
    import concourse.bacc as bacc
    from concourse.bass_utils import run_bass_kernel_spmd

    nc = bacc.Bacc("TRN2", target_bir_lowering=False, num_devices=1)
    arrays, aps = {}, {}
    for name in _INS:
        v = np.ascontiguousarray(pack_gates(inputs) if name == "gate_band" else inputs[name])
        arrays[f"in_{name}"] = v
        aps[name] = nc.dram_tensor(f"in_{name}", v.shape, mybir.dt.from_np(v.dtype), kind="ExternalInput").ap()
    out = nc.dram_tensor("out", (1, T, D), F32, kind="ExternalOutput").ap()
    build(nc, aps, out)
    r = run_bass_kernel_spmd(nc, [arrays], core_ids=[0])
    return r.results[0]["out"]
```
